# Optimizing a Trainium2 kernel written in Bass

```python
import math
import jax, jax.numpy as jnp
from jax import lax
import numpy as np

D_MODEL = 1024
BATCH = 1
SEQ = 512
DEPTH = 1

HEAD_DIM = 64
DIL_GROUPS = ((128, 1), (512, 4), (2048, 16))
DIL_HEADS_PER_GROUP = 4
N_DIL_HEADS = DIL_HEADS_PER_GROUP * len(DIL_GROUPS)
N_SB_HEADS = 8
DIL_WIDTH = N_DIL_HEADS * HEAD_DIM
DIL_OUT_WIDTH = DIL_HEADS_PER_GROUP * HEAD_DIM
SB_WIDTH = N_SB_HEADS * HEAD_DIM
D_FF = 4 * D_MODEL
BLOCK = 128
RMS_EPS = 1e-6
NEG_INF = -1e30
IN_COLS = 3 * DIL_WIDTH + 3 * SB_WIDTH + 2 * D_MODEL
SPLITS = (DIL_WIDTH, 2 * DIL_WIDTH, 3 * DIL_WIDTH,
          3 * DIL_WIDTH + SB_WIDTH, 3 * DIL_WIDTH + 2 * SB_WIDTH, 3 * DIL_WIDTH + 3 * SB_WIDTH,
          3 * DIL_WIDTH + 3 * SB_WIDTH + D_MODEL)


def rmsnorm(x, g):
    xf = x.astype(jnp.float32)
    y = xf * lax.rsqrt(jnp.mean(xf * xf, axis=-1, keepdims=True) + RMS_EPS)
    return (y * g.astype(jnp.float32)).astype(x.dtype)

def alibi_slopes(n):
    return jnp.exp2(-8.0 * jnp.arange(1, n + 1, dtype=jnp.float32) / n)

def dilated_window_group(q, k, v, slopes, window, dilation):
    b, s, h, dh = q.shape
    n_steps = window // dilation
    nb = -(-s // (dilation * BLOCK))
    sub_len = nb * BLOCK
    s_pad = sub_len * dilation

    def to_blocks(t):
        t = jnp.pad(t, ((0, 0), (0, s_pad - s), (0, 0), (0, 0)))
        t = t.reshape(b, sub_len, dilation, h, dh)
        t = t.transpose(0, 2, 3, 1, 4)
        return t.reshape(b, dilation, h, nb, BLOCK, dh)

    qb, kb, vb = to_blocks(q), to_blocks(k), to_blocks(v)

    def with_prev(t):
        prev = jnp.pad(t[:, :, :, :-1], ((0, 0), (0, 0), (0, 0), (1, 0), (0, 0), (0, 0)))
        return jnp.concatenate([prev, t], axis=4)

    kk, vv = with_prev(kb), with_prev(vb)
    scores = jnp.einsum('brhnqd,brhnkd->brhnqk', qb, kk).astype(jnp.float32) / math.sqrt(dh)
    qi = jnp.arange(BLOCK)[:, None]
    kj = jnp.arange(2 * BLOCK)[None, :]
    steps = qi + BLOCK - kj
    key_sub_idx = jnp.arange(nb)[:, None, None] * BLOCK + kj[None] - BLOCK
    valid = (steps >= 0) & (steps <= n_steps) & (key_sub_idx >= 0)
    bias = -slopes[:, None, None].astype(jnp.float32) * (steps * dilation).astype(jnp.float32)
    logits = scores + bias[None, None, :, None]
    logits = jnp.where(valid[None, None, None], logits, NEG_INF)
    lse = jax.nn.logsumexp(logits, axis=-1)
    p = jnp.exp(logits - lse[..., None])
    o = jnp.einsum('brhnqk,brhnkd->brhnqd', p.astype(v.dtype), vv)

    def from_blocks(t):
        extra = t.shape[5:]
        t = t.reshape((b, dilation, h, sub_len) + extra)
        t = jnp.moveaxis(t, 3, 1)
        t = t.reshape((b, s_pad, h) + extra)
        return t[:, :s]

    return from_blocks(o), from_blocks(lse)

def dilated_attention(q, k, v):
    b, s = q.shape[:2]
    slopes = alibi_slopes(N_DIL_HEADS)
    outs, lses = [], []
    for g, (window, dilation) in enumerate(DIL_GROUPS):
        sl = slice(g * DIL_HEADS_PER_GROUP, (g + 1) * DIL_HEADS_PER_GROUP)
        o, l = dilated_window_group(q[:, :, sl], k[:, :, sl], v[:, :, sl], slopes[sl], window, dilation)
        outs.append(o)
        lses.append(l)
    o_all = jnp.stack(outs, axis=0).astype(jnp.float32)
    w = jax.nn.softmax(jnp.stack(lses, axis=0), axis=0)
    out = jnp.sum(w[..., None] * o_all, axis=0).astype(q.dtype)
    return out.reshape(b, s, DIL_OUT_WIDTH)

def stick_breaking_attention(q, k, v):
    b, s, h, dh = q.shape
    nb = s // BLOCK
    scale = 1.0 / math.sqrt(dh)
    kt = k.transpose(0, 2, 1, 3)
    vt = v.transpose(0, 2, 1, 3)
    q_blocks = q.transpose(0, 2, 1, 3).reshape(b, h, nb, BLOCK, dh).transpose(2, 0, 1, 3, 4)
    key_pos = jnp.arange(s)

    def one_block(args):
        i, q_blk = args
        z = jnp.einsum('bhqd,bhkd->bhqk', q_blk, kt).astype(jnp.float32) * scale
        q_pos = i * BLOCK + jnp.arange(BLOCK)
        causal = key_pos[None, :] < q_pos[:, None]
        log_one_minus = jnp.where(causal, jax.nn.log_sigmoid(-z), 0.0)
        suffix = lax.cumsum(log_one_minus, axis=3, reverse=True) - log_one_minus
        log_a = jax.nn.log_sigmoid(z) + suffix
        a = jnp.where(causal, jnp.exp(log_a), 0.0)
        return jnp.einsum('bhqk,bhkd->bhqd', a.astype(vt.dtype), vt)

    o_blocks = lax.map(one_block, (jnp.arange(nb), q_blocks))
    return o_blocks.transpose(1, 0, 3, 2, 4).reshape(b, s, h * dh)

def first_inputs(seed: int = 0) -> dict:
    key = jax.random.key(seed)
    ks = jax.random.split(key, 12)
    f32 = jnp.float32
    x = jax.random.normal(ks[0], (BATCH, SEQ, D_MODEL), f32)
    norm_mix_g = 1.0 + 0.02 * jax.random.normal(ks[1], (DEPTH, D_MODEL), f32)
    w_in = jax.random.normal(ks[2], (DEPTH, D_MODEL, IN_COLS), f32) * D_MODEL ** -0.5
    b_gate = 0.02 * jax.random.normal(ks[3], (DEPTH, 2 * D_MODEL), f32)
    w_up_dil = jax.random.normal(ks[4], (DEPTH, DIL_OUT_WIDTH, D_MODEL), f32) * DIL_OUT_WIDTH ** -0.5
    w_up_sb = jax.random.normal(ks[5], (DEPTH, SB_WIDTH, D_MODEL), f32) * SB_WIDTH ** -0.5
    w_out = jax.random.normal(ks[6], (DEPTH, D_MODEL, D_MODEL), f32) * D_MODEL ** -0.5
    norm_mlp_g = 1.0 + 0.02 * jax.random.normal(ks[7], (DEPTH, D_MODEL), f32)
    w_mlp_in = jax.random.normal(ks[8], (DEPTH, D_MODEL, D_FF), f32) * D_MODEL ** -0.5
    w_mlp_out = jax.random.normal(ks[9], (DEPTH, D_FF, D_MODEL), f32) * D_FF ** -0.5
    norm_final_g = 1.0 + 0.02 * jax.random.normal(ks[10], (D_MODEL,), f32)
    return {"x": x, "norm_mix_g": norm_mix_g, "w_in": w_in, "b_gate": b_gate,
            "w_up_dil": w_up_dil, "w_up_sb": w_up_sb, "w_out": w_out,
            "norm_mlp_g": norm_mlp_g, "w_mlp_in": w_mlp_in, "w_mlp_out": w_mlp_out,
            "norm_final_g": norm_final_g}

def first_block(x, norm_mix_g, w_in, b_gate, w_up_dil, w_up_sb, w_out,
              norm_mlp_g, w_mlp_in, w_mlp_out, norm_final_g):
    b, s, _ = x.shape
    for layer in range(DEPTH):
        h = rmsnorm(x, norm_mix_g[layer])
        proj = h @ w_in[layer]
        q_a, k_a, v_a, q_b, k_b, v_b, gl_a, gl_b = jnp.split(proj, SPLITS, axis=-1)
        heads_a = lambda t: t.reshape(b, s, N_DIL_HEADS, HEAD_DIM)
        heads_b = lambda t: t.reshape(b, s, N_SB_HEADS, HEAD_DIM)
        o_a = dilated_attention(heads_a(q_a), heads_a(k_a), heads_a(v_a))
        o_b = stick_breaking_attention(heads_b(q_b), heads_b(k_b), heads_b(v_b))
        bg_a, bg_b = jnp.split(b_gate[layer], 2)
        g_a = jax.nn.sigmoid(gl_a + bg_a)
        g_b = jax.nn.sigmoid(gl_b + bg_b)
        merged = g_a * (o_a @ w_up_dil[layer]) + g_b * (o_b @ w_up_sb[layer])
        x = x + merged @ w_out[layer]
        h2 = rmsnorm(x, norm_mlp_g[layer])
        x = x + jnp.square(jax.nn.relu(h2 @ w_mlp_in[layer])) @ w_mlp_out[layer]
    return rmsnorm(x, norm_final_g)


CHUNK = 64
N_META = 16
EPS = 1e-6
POOL_WIDTH = 512
POOL_GROUPS = 4
POOL_GROUP_DIM = POOL_WIDTH // POOL_GROUPS
POOL_WINDOWS = (2, 4, 8, 16)
GLA_HEADS = 4
GLA_DK = 64
GLA_DV = 128
GLA_KEY = GLA_HEADS * GLA_DK
GLA_VAL = GLA_HEADS * GLA_DV
GLA_GATE_RANK = 16
GLA_TAU = 16.0
D_FF_2 = 4 * D_MODEL
IN_SIZES = (POOL_WIDTH, GLA_KEY, GLA_KEY, GLA_VAL, GLA_VAL, GLA_GATE_RANK, D_MODEL, D_MODEL)
N_IN = sum(IN_SIZES)
IN_SPLITS = [int(s) for s in np.cumsum(IN_SIZES)[:-1]]


def rmsnorm_2(x, g):
    xf = x.astype(jnp.float32)
    y = xf * lax.rsqrt(jnp.mean(xf * xf, axis=-1, keepdims=True) + EPS)
    return (y * g.astype(jnp.float32)).astype(x.dtype)

def multiscale_pool(a):
    B, L, _ = a.shape
    af = a.astype(jnp.float32)
    cs = jnp.concatenate([jnp.zeros((B, 1, POOL_WIDTH), jnp.float32), jnp.cumsum(af, axis=1)], axis=1)
    t = jnp.arange(L)
    outs = []
    for g, w in enumerate(POOL_WINDOWS):
        lo_c, hi_c = g * POOL_GROUP_DIM, (g + 1) * POOL_GROUP_DIM
        hi = cs[:, 1:, lo_c:hi_c]
        lo = jnp.concatenate([jnp.zeros((B, w - 1, POOL_GROUP_DIM), jnp.float32), cs[:, :L - w + 1, lo_c:hi_c]], axis=1)
        cnt = jnp.minimum(t + 1, w).astype(jnp.float32)[None, :, None]
        outs.append((hi - lo) / cnt)
    return (jnp.concatenate(outs, axis=-1) - af).astype(a.dtype)

def gla_chunk_step(S, inp):
    qc, kc, vc, ac = inp
    b = jnp.cumsum(ac, axis=2)
    decay = jnp.exp(-jnp.abs(b[:, :, :, None, :] - b[:, :, None, :, :]))
    scores = jnp.einsum('bhtk,bhsk,bhtsk->bhts', qc, kc, decay)
    o = jnp.einsum('bhts,bhsv->bhtv', scores, vc) + jnp.einsum('bhtk,bhkv->bhtv', qc * jnp.exp(b), S)
    b_end = b[:, :, -1:, :]
    S_new = jnp.exp(b_end[:, :, 0, :])[..., None] * S + jnp.einsum('bhsk,bhsv->bhkv', kc * jnp.exp(b_end - b), vc)
    return S_new, o

def gla_chunked(q, k, v, log_a):
    B = q.shape[0]
    pad = CHUNK - N_META

    def prep(t):
        t = jnp.pad(t.astype(jnp.float32), ((0, 0), (pad, 0), (0, 0), (0, 0)))
        n = t.shape[1] // CHUNK
        return t.reshape(B, n, CHUNK, GLA_HEADS, t.shape[-1]).transpose(1, 0, 3, 2, 4)

    qc, kc, vc, ac = prep(q), prep(k), prep(v), prep(log_a)
    S0 = jnp.zeros((B, GLA_HEADS, GLA_DK, GLA_DV), jnp.float32)
    _, o = lax.scan(gla_chunk_step, S0, (qc, kc, vc, ac))
    o = o.transpose(1, 0, 3, 2, 4).reshape(B, -1, GLA_HEADS, GLA_DV)[:, pad:]
    return o.astype(v.dtype)

def hybrid_mixer(u, w_in, w_pool_mix, pool_scale, w_pool_out, w_gate_up, b_gate, gla_norm, w_gla_out, w_out):
    B, L, _ = u.shape
    z = jnp.einsum('bld,dn->bln', u, w_in)
    a, q, k, v, r, lr, ga, gb = jnp.split(z, IN_SPLITS, axis=-1)
    p = multiscale_pool(a).reshape(B, L, POOL_GROUPS, POOL_GROUP_DIM)
    p = jnp.einsum('blgc,gce->blge', p, w_pool_mix).reshape(B, L, POOL_WIDTH) * pool_scale
    y_a = jnp.einsum('blc,cd->bld', p, w_pool_out)
    log_a = jax.nn.log_sigmoid((lr @ w_gate_up + b_gate).astype(jnp.float32)) / GLA_TAU
    q = q.reshape(B, L, GLA_HEADS, GLA_DK) * (GLA_DK ** -0.5)
    k = k.reshape(B, L, GLA_HEADS, GLA_DK)
    v = v.reshape(B, L, GLA_HEADS, GLA_DV)
    log_a = log_a.reshape(B, L, GLA_HEADS, GLA_DK)
    o = gla_chunked(q, k, v, log_a)
    o = rmsnorm_2(o, gla_norm.reshape(GLA_HEADS, GLA_DV)) * jax.nn.silu(r).reshape(B, L, GLA_HEADS, GLA_DV)
    y_b = jnp.einsum('blc,cd->bld', o.reshape(B, L, GLA_VAL), w_gla_out)
    m = jax.nn.sigmoid(ga) * y_a + jax.nn.sigmoid(gb) * y_b
    return jnp.einsum('bld,de->ble', m, w_out)

def squared_relu_mlp(u, w_ff1, w_ff2):
    hdn = jnp.square(jax.nn.relu(jnp.einsum('bld,df->blf', u, w_ff1)))
    return jnp.einsum('blf,fd->bld', hdn, w_ff2)

def second_inputs(seed: int = 0) -> dict:
    key = jax.random.key(seed)
    ks = jax.random.split(key, 20)
    f32 = jnp.float32
    nrm = lambda k, shape, s: jax.random.normal(k, shape, f32) * s
    return {
        "x": jax.random.normal(ks[0], (BATCH, SEQ, D_MODEL), f32),
        "meta_tokens": nrm(ks[1], (N_META, D_MODEL), 1.0),
        "norm_mix": 1.0 + nrm(ks[2], (DEPTH, D_MODEL), 0.05),
        "w_in": nrm(ks[3], (DEPTH, D_MODEL, N_IN), D_MODEL ** -0.5),
        "w_pool_mix": nrm(ks[4], (DEPTH, POOL_GROUPS, POOL_GROUP_DIM, POOL_GROUP_DIM), POOL_GROUP_DIM ** -0.5),
        "pool_scale": 1.0 + nrm(ks[5], (DEPTH, POOL_WIDTH), 0.1),
        "w_pool_out": nrm(ks[6], (DEPTH, POOL_WIDTH, D_MODEL), POOL_WIDTH ** -0.5),
        "w_gate_up": nrm(ks[7], (DEPTH, GLA_GATE_RANK, GLA_KEY), GLA_GATE_RANK ** -0.5),
        "b_gate": nrm(ks[8], (DEPTH, GLA_KEY), 0.1),
        "gla_norm": 1.0 + nrm(ks[9], (DEPTH, GLA_VAL), 0.05),
        "w_gla_out": nrm(ks[10], (DEPTH, GLA_VAL, D_MODEL), GLA_VAL ** -0.5),
        "w_out": nrm(ks[11], (DEPTH, D_MODEL, D_MODEL), D_MODEL ** -0.5),
        "norm_ffn": 1.0 + nrm(ks[12], (DEPTH, D_MODEL), 0.05),
        "w_ff1": nrm(ks[13], (DEPTH, D_MODEL, D_FF_2), D_MODEL ** -0.5),
        "w_ff2": nrm(ks[14], (DEPTH, D_FF_2, D_MODEL), D_FF_2 ** -0.5),
        "norm_final": 1.0 + nrm(ks[15], (D_MODEL,), 0.05),
    }

def second_block(x, meta_tokens, norm_mix, w_in, w_pool_mix, pool_scale, w_pool_out, w_gate_up, b_gate,
              gla_norm, w_gla_out, w_out, norm_ffn, w_ff1, w_ff2, norm_final):
    B = x.shape[0]
    meta = jnp.broadcast_to(meta_tokens[None].astype(x.dtype), (B, N_META, D_MODEL))
    h = jnp.concatenate([meta, x], axis=1)
    for l in range(DEPTH):
        h = h + hybrid_mixer(rmsnorm_2(h, norm_mix[l]), w_in[l], w_pool_mix[l], pool_scale[l], w_pool_out[l],
                             w_gate_up[l], b_gate[l], gla_norm[l], w_gla_out[l], w_out[l])
        h = h + squared_relu_mlp(rmsnorm_2(h, norm_ffn[l]), w_ff1[l], w_ff2[l])
    return rmsnorm_2(h, norm_final)[:, N_META:]


def setup_inputs(seed=0):
    out = dict(first_inputs(seed))
    for name, value in second_inputs(seed + 1).items():
        if name != "x":
            out[name + "_2"] = value
    return out


def reference(
    x, norm_mix_g, w_in, b_gate, w_up_dil, w_up_sb, w_out, norm_mlp_g, w_mlp_in, w_mlp_out,
    norm_final_g, meta_tokens_2, norm_mix_2, w_in_2, w_pool_mix_2, pool_scale_2, w_pool_out_2,
    w_gate_up_2, b_gate_2, gla_norm_2, w_gla_out_2, w_out_2, norm_ffn_2, w_ff1_2, w_ff2_2,
    norm_final_2,
):
    x = first_block(
        x, norm_mix_g, w_in, b_gate, w_up_dil, w_up_sb, w_out, norm_mlp_g, w_mlp_in, w_mlp_out,
        norm_final_g,
    )
    return second_block(
        x, meta_tokens_2, norm_mix_2, w_in_2, w_pool_mix_2, pool_scale_2, w_pool_out_2,
        w_gate_up_2, b_gate_2, gla_norm_2, w_gla_out_2, w_out_2, norm_ffn_2, w_ff1_2, w_ff2_2,
        norm_final_2,
    )


_drawn_inputs = setup_inputs


def setup_inputs(seed=0):
    import zlib

    import numpy as np

    out = dict(_drawn_inputs(seed))
    spreads = {}
    factors = {'norm_mix_g': 4.122,
     'b_gate': 8.0,
     'b_gate_2': 3.797,
     'gla_norm_2': 4.107,
     'norm_mlp_g': 4.287}
    for name, (base, spread) in spreads.items():
        noise = np.random.default_rng([zlib.crc32(name.encode()), seed]).standard_normal(out[name].shape)
        drawn = base * np.exp(spread * noise) if base else spread * noise
        out[name] = __import__('jax').numpy.asarray(drawn.astype(out[name].dtype))
    for name, factor in factors.items():
        out[name] = (out[name] * factor).astype(out[name].dtype)
    return out
```

```python
from contextlib import ExitStack

import concourse.bass as bass
from concourse import mybir

F32 = mybir.dt.float32
F32R = mybir.dt.float32r
I32 = mybir.dt.int32
U32 = mybir.dt.uint32
ALU = mybir.AluOpType
ACT = mybir.ActivationFunctionType
AX_X = mybir.AxisListType.X

P = 128
DM = 1024
KT = DM // P
S1 = 512
META = 16
S2 = META + S1
HALF2 = S2 // 2
DH = 64
DIL_W, SB_W = 768, 512
D_FF = 4 * DM
CHUNKS = D_FF // DM
NEG = -1.0e30
EPS = 1.0e-6
DILATIONS = (1, 4, 16)
SLOPES = [2.0 ** (-8.0 * (i + 1) / 12) for i in range(12)]
CH, NCH = 64, 9
PADL = NCH * CH
PAD = PADL - S2
TAU = 16.0
LEVELS = (64, 32, 16, 8, 4, 2)
WINDOWS = (2, 4, 8, 16)

G_MIX, G_MLP, G_FIN, G_MIX2, G_FFN2, G_FIN2, B_GATE, B_GATE2, POOL_SC, GLA_G, NVEC = (
    0, 8, 16, 24, 32, 40, 48, 64, 66, 70, 74)

T_QKV_A, T_GATE_A, T_QKV_B, T_GATE_B, T_UP_A, T_UP_B, T_OUT, T_MLP = 0, 18, 26, 38, 46, 54, 62, 70
T2 = T_MLP + 16 * CHUNKS
T2_K, T2_Q, T2_LR, T2_V, T2_A, T2_PM, T2_GY = T2, T2 + 2, T2 + 4, T2 + 5, T2 + 9, T2 + 13, T2 + 17
T2_R = T2_GY + 16
T2_M = T2_R + 4
T2_OUT = T2_M + 16
T2_MLP = T2_OUT + 8
T_END = T2_MLP + 16 * CHUNKS
N_MIX, N_MERGE, N_MLP, N_HID = 0, 8, 16, 24
N2_MIX = N_HID + 8 * CHUNKS
N2_POOL, N2_PM, N2_O, N2_M, N2_FFN = N2_MIX + 8, N2_MIX + 12, N2_MIX + 16, N2_MIX + 20, N2_MIX + 28
N2_HID = N2_FFN + 8


def make_loads():
    loads, t = [], 0

    def add(name, at, kt, slabs):
        nonlocal t
        loads.append((name, at, kt, slabs, t))
        t += slabs

    def wide(name, base, tiles, kt=KT):
        for i in range(0, tiles, 2):
            add(name, base + i * P, kt, 2)

    wide("w_in", 0, 18)
    wide("w_in", 3 * DIL_W + 3 * SB_W, 8)
    wide("w_in", 3 * DIL_W, 12)
    wide("w_in", 3 * DIL_W + 3 * SB_W + DM, 8)
    wide("w_up_dil", 0, 8, 2)
    wide("w_up_sb", 0, 8, 4)
    wide("w_out", 0, 8)
    assert t == T_MLP
    first_mlp = len(loads)
    for c in range(CHUNKS):
        wide("mlp_in", c * DM, 8)
        for i in range(4):
            add("mlp_out", (c, i), KT, 2)
    assert t == T2
    wide("w_in_2", 768, 2)
    wide("w_in_2", 512, 2)
    add("w_in_2", 2048, KT, 1)
    wide("w_in_2", 1024, 4)
    wide("w_in_2", 0, 4)
    add("pool_mix", 0, 1, 4)
    for i in range(0, 8, 2):
        add("w_in_2", 2064 + i * P, KT, 2)
        add("pool_out", i * P, 4, 2)
    wide("w_in_2", 1536, 4)
    for i in range(0, 8, 2):
        add("w_in_2", 2064 + DM + i * P, KT, 2)
        add("gla_out", i * P, 4, 2)
    wide("w_out_2", 0, 8)
    assert t == T2_MLP
    second_mlp = len(loads)
    for c in range(CHUNKS):
        wide("mlp_in_2", c * DM, 8)
        for i in range(4):
            add("mlp_out_2", (c, i), KT, 2)
    return loads, first_mlp, second_mlp


def make_between():
    between = {t: [] for t in range(T2, T2_MLP)}
    between[T2_LR + 1] += [("gate_up",)]
    between[T2_LR + 2] += [("decay",)]
    for i in range(4):
        between[T2_V + i + 1 + (i == 3)] += [("v_rows", i)]
    units = 2 * (len(LEVELS) + 3)
    t = T2_V + 3
    for y in range(units + 2):
        if y < units:
            between[t] += [("unit_d", y)]
        if 0 <= y - 1 < units:
            between[t] += [("unit_qk", y - 1)]
        if 0 <= y - 2 < units:
            between[t] += [("unit_mm", y - 2)]
        t += 1
    assert t <= T2_R, (t, T2_R)
    between[T2_R] += [("kv", 0)]
    between[T2_R + 1] += [("kv", 1)]
    for h in range(4):
        between[T2_R + 2 + h] += [("o_mm", h), ("o_norm", h)]
    return between


def build(nc, d):
    loads, first_mlp, second_mlp = make_loads()
    between = make_between()
    slab = {}
    for p, (_, _, kt, n, t) in enumerate(loads):
        for i in range(n):
            slab[t + i] = (p, i, kt, n)

    def weight_view(name, at, kt, cols):
        if name == "pool_mix":
            return d["w_pool_mix_2"][0].rearrange("g c e -> c g e")
        if name in ("mlp_out", "mlp_out_2"):
            c, i = at
            w = d["w_mlp_out" if name == "mlp_out" else "w_ff2_2"][0]
            return w[c * DM:(c + 1) * DM, i * 256:(i + 1) * 256].rearrange("(k p) n -> p k n", p=P)
        w = d[{"w_in": "w_in", "w_up_dil": "w_up_dil", "w_up_sb": "w_up_sb", "w_out": "w_out",
               "mlp_in": "w_mlp_in", "w_in_2": "w_in_2", "pool_out": "w_pool_out_2",
               "gla_out": "w_gla_out_2", "w_out_2": "w_out_2", "mlp_in_2": "w_ff1_2"}[name]][0]
        return w[:, at:at + cols].rearrange("(k p) n -> p k n", p=P)

    ctx = ExitStack()
    with ctx:
        def sb(name, shape, dt=F32):
            return ctx.enter_context(nc.sbuf_tensor(name, shape, dt))

        def sem(name):
            return ctx.enter_context(nc.semaphore(name))

        X = sb("X", [P, KT, S2])
        Ah, Al = sb("Ah", [P, KT, S2], F32R), sb("Al", [P, KT, S2], F32R)
        Bh, Bl = sb("Bh", [P, KT, S2], F32R), sb("Bl", [P, KT, S2], F32R)
        raw = sb("raw", [P, 2, 2 * DM])
        wh, wl = sb("wh", [P, 2, DM], F32R), sb("wl", [P, 2, DM], F32R)
        F = sb("F", [P, 2, S2])
        SQ = sb("SQ", [P, 2, META + S2])
        SS, RS = sb("SS", [P, S2]), sb("RS", [P, S2])
        ident, ones = sb("ident", [P, P]), sb("ones", [P, P])
        vecT = sb("vecT", [P, NVEC])
        negb = sb("negb", [P, 16])
        wgu = sb("wgu", [16, 256])
        stat = sb("stat", [P, 5, 16])
        ebe = sb("ebe", [P, 2, NCH])
        masks = sb("masks", [P, 6, CH])
        rcnt = sb("rcnt", [P, 16])
        AR = 19584
        arena = sb("arena", [P, AR])
        ps = ctx.enter_context(nc.psum_tensor("ps", [P, 8, 512], F32))

        def region(at, *shape):
            n = 1
            for s in shape:
                n *= s
            assert at + n <= AR, (at, shape)
            v = arena[:, at:at + n]
            if len(shape) == 2:
                v = v.rearrange("p (a b) -> p a b", a=shape[0])
            return v

        SBM = region(0, 512)
        D0, D1, D2 = region(512, 256), region(768, 512), region(1280, 512)
        qa, ka = region(1792, 6, 512), region(4864, 6, 512)
        Vna = region(7936, 4, 768)
        Lg = region(11008, 2, 1280)
        PT = region(13568, 10, 128)
        onat = [region(14848, 256), region(19200, 256)]
        vt = region(13568, 2, 512)
        GA = region(15104, 8, 512)
        qb, kb = region(1792, 4, 512), region(3840, 4, 512)
        Vnb = region(5888, 4, 512)
        GB = region(7936, 8, 512)
        Zs, Es, Cs = region(12032, 2, 512), region(13056, 2, 512), region(14080, 2, 512)
        PTb = region(512, 2, 512)
        onatb = SQ[:, 0, 0:512]
        vtb = region(512, 2, 512)
        xnat = region(1792, 4, 1024)
        mnat = region(5888, 1024)
        vrow = region(6912, 128)
        DI = arena[:, 11008:11520].bitcast(I32)
        DM4 = arena[:, 11520:12032].bitcast(I32)
        PEN = region(12032, 512)
        q2, k2 = region(0, 2, PADL), region(1152, 2, PADL)
        sr = region(0, 4, S2)
        bS = region(2304, 2, PADL)
        la = region(3456, 2, PADL)
        Kn = region(3456, 2, CH * 8)
        reset = region(4608, PADL)
        Ed = region(5184, 2, PADL)
        Qp, Kp = region(6336, 2, PADL), region(7488, 2, PADL)
        st = region(5184, 2, 8 * P)
        osb, osb2 = region(7232, S2), region(7760, S2)
        sc = region(8640, 2, PADL)
        Vn = region(9792, 2, NCH * P)
        Qs = region(12096, 2, PADL)
        G2 = region(13248, 2, S2)
        UU = region(13248, 2, S2)
        E2 = region(14304, S2)
        lr = region(14832, S2)
        v2 = region(15360, 4, PADL)
        apad = region(17664, 2, META + S2)
        wsum = SQ
        ma = region(15360, 8, S2)
        Y = region(0, 8, S1)
        ON = region(4096, 4, DM)

        params_in, x_in = sem("params_in"), sem("x_in")
        w_landed = [sem("w_landed0"), sem("w_landed1")]
        hi_ready, lo_ready = sem("hi_ready"), sem("lo_ready")
        slab_done, evac_done = sem("slab_done"), sem("evac_done")
        f_ready, hi_split, act_ready = sem("f_ready"), sem("hi_split"), sem("act_ready")
        sq_ready, ss_done = sem("sq_ready"), sem("ss_done")
        stat_done, ms_ready, sqrt_ready, rstd_ready = (
            sem("stat_done"), sem("ms_ready"), sem("sqrt_ready"), sem("rstd_ready"))
        consts_ready, pool_step = sem("consts_ready"), sem("pool_step")
        di_ready, dist_step, dist_raw = sem("di_ready"), sem("dist_step"), sem("dist_raw")
        bias_ready = sem("bias_ready")
        vec_psum, vec_ready, negb_ready = sem("vec_psum"), sem("vec_ready"), sem("negb_ready")
        xt_psum, xt_copied, meta_psum, meta_copied = (
            sem("xt_psum"), sem("xt_copied"), sem("meta_psum"), sem("meta_copied"))
        vtrans_done, vnat_copied = sem("vtrans_done"), sem("vnat_copied")
        gate_exp, gate_inc, gate_done = sem("gate_exp"), sem("gate_inc"), sem("gate_done")
        scores_done, logits_done, max_done, negmax_ready, probs_ready = (
            sem("scores_done"), sem("logits_done"), sem("max_done"), sem("negmax_ready"), sem("probs_ready"))
        pt_psum, pt_copied, pv_done, rden_done, o_norm = (
            sem("pt_psum"), sem("pt_copied"), sem("pv_done"), sem("rden_done"), sem("o_norm"))
        oT_psum, oa_hi, oa_ready = sem("oT_psum"), sem("oa_hi"), sem("oa_ready")
        sb_scores, z_done, sb_abs, sb_exp, sb_ln = (
            sem("sb_scores"), sem("z_done"), sem("sb_abs"), sem("sb_exp"), sem("sb_ln"))
        sb_sp, sb_scan, sb_la, sb_probs = sem("sb_sp"), sem("sb_scan"), sem("sb_la"), sem("sb_probs")
        sb_pt_psum, sb_pt_copied, sb_pv = sem("sb_pt_psum"), sem("sb_pt_copied"), sem("sb_pv")
        ob_nat, obT_psum, ob_hi, ob_ready = sem("ob_nat"), sem("obT_psum"), sem("ob_hi"), sem("ob_ready")
        x_normed = sem("x_normed")
        zeros2_ready = sem("zeros2_ready")
        gu_psum, u_ready, u_abs, u_exp, u_ln, la_ready, bs_ready, ebe_ready = (
            sem("gu_psum"), sem("u_ready"), sem("u_abs"), sem("u_exp"), sem("u_ln"), sem("la_ready"),
            sem("bs_ready"), sem("ebe_ready"))
        vr_psum, vr_copied = sem("vr_psum"), sem("vr_copied")
        d_ready, d_abs, d_exp, qk_ready, mm_done, sc_done = (
            sem("d_ready"), sem("d_abs"), sem("d_exp"), sem("qk_ready"), sem("mm_done"), sem("sc_done"))
        kn_psum, kn_copied, kv_psum, st_done = sem("kn_psum"), sem("kn_copied"), sem("kv_psum"), sem("st_done")
        o_psum, o_copied, o_sq, o_stat, o_ms, o_sqrt, o_rstd, o_scaled = (
            sem("o_psum"), sem("o_copied"), sem("o_sq"), sem("o_stat"), sem("o_ms"), sem("o_sqrt"),
            sem("o_rstd"), sem("o_scaled"))
        win_done, edge_done = sem("win_done"), sem("edge_done")
        silu_exp, silu_inc, silu_rec, silu_done = (
            sem("silu_exp"), sem("silu_inc"), sem("silu_rec"), sem("silu_done"))
        prod_done = sem("prod_done")
        y_ready, y_psum, y_copied, out_done = sem("y_ready"), sem("y_psum"), sem("y_copied"), sem("out_done")

        def dense_psum(t, block):
            if block == 1:
                return ps[:, t % 2, :]
            return ps[:, 2 * (t % 2):2 * (t % 2) + 2, 0:HALF2]

        def tokens(ap, block):
            return ap if block == 1 else ap.rearrange("p (a b) -> p a b", a=2)

        def flat(bank):
            return ps[:, bank:bank + 2, :].rearrange("p a b -> p (a b)")

        def width(block):
            return S1 if block == 1 else S2

        def raw_half(p_slot, half, kt, n):
            return raw[:, p_slot, 0:kt * n * P].rearrange("p (k n) -> p k n", k=kt)[
                :, :, half * P:(half + 1) * P]

        def raw_slab(t):
            p, half, kt, n = slab[t]
            if loads[p][0] == "pool_mix":
                return raw[:, p % 2, 0:512].rearrange("p (k n) -> p k n", k=4)[:, half:half + 1, :]
            return raw_half(p % 2, half, kt, n)

        def w_slab(w, slot, kt):
            return w[:, slot, 0:kt * P].rearrange("p (k n) -> p k n", k=kt)

        def dil_groups(n):
            nb0 = 1 if n == 0 else 2
            return [(P * (n + 1 - nb0), nb0, 0), (0, n + 1, nb0 * P), (0, n + 1, (nb0 + n + 1) * P)]

        def level_ref(y):
            l, j = y // 2, y % 2
            b = LEVELS[l] if l < len(LEVELS) else CH
            at = b // 2 - 1 if l < len(LEVELS) else CH - 1
            v = bS[:, j, :].rearrange("p (a b) -> p a b", b=b)
            return v, v[:, :, at:at + 1].to_broadcast([P, PADL // b, b]), b

        U_DIAG, U_END, U_START = 2 * len(LEVELS), 2 * len(LEVELS) + 2, 2 * len(LEVELS) + 4
        def exp_no(y):
            return y if y < U_DIAG else y - 2
        MLPS = {1: (T_MLP, N_HID, first_mlp), 2: (T2_MLP, N2_HID, second_mlp)}

        block = ctx.enter_context(nc.Block())

        @block.sync
        def _(sp):
            sp.dma_start(xnat, d["x"][0].rearrange("(a p) d -> p a d", p=P)).then_inc(x_in, 16)
            row = 0
            for name, n in (("norm_mix_g", 8), ("norm_mlp_g", 8), ("norm_final_g", 8), ("norm_mix_2", 8),
                            ("norm_ffn_2", 8), ("norm_final_2", 8), ("b_gate", 16), ("b_gate_2", 2),
                            ("pool_scale_2", 4), ("gla_norm_2", 4)):
                v = d[name] if len(d[name].shape) == 1 else d[name][0]
                sp.dma_start(vrow[row:row + n, :], v.rearrange("(a b) -> a b", b=P)).then_inc(params_in, 16)
                row += n
            sp.dma_start(mnat[0:META, :], d["meta_tokens_2"]).then_inc(params_in, 16)
            sp.dma_start(wgu[:, :], d["w_gate_up_2"][0]).then_inc(params_in, 16)

            def load(p):
                name, at, kt, n, t = loads[p]
                if p >= 2:
                    sp.wait_ge(lo_ready, loads[p - 2][4] + loads[p - 2][3])
                view = weight_view(name, at, kt, n * P)
                k = 4 if name == "pool_mix" else kt
                sp.dma_start(raw[:, p % 2, 0:kt * n * P].rearrange("p (k n) -> p k n", k=k), view)\
                  .then_inc(w_landed[p % 2], 16)

            def mlp_loads(which, w1, w2):
                t0, _, p0 = MLPS[which]
                with sp.Fori(0, CHUNKS - 1) as c:
                    for i in range(8):
                        sp.wait_ge(lo_ready, t0 + 16 * c + 2 * i - 2)
                        if i < 4:
                            src = w1[:, bass.ds(c * DM + i * 256, 256)]
                        else:
                            src = w2[bass.ds(c * DM, DM), (i - 4) * 256:(i - 3) * 256]
                        sp.dma_start(raw[:, (p0 + i) % 2, :].rearrange("p (k n) -> p k n", k=KT),
                                     src.rearrange("(k p) n -> p k n", p=P))\
                          .then_inc(w_landed[(p0 + i) % 2], 16)

            for p in range(first_mlp):
                load(p)
            mlp_loads(1, d["w_mlp_in"][0], d["w_mlp_out"][0])
            for p in range(first_mlp + 8 * (CHUNKS - 1), second_mlp):
                load(p)
            mlp_loads(2, d["w_ff1_2"][0], d["w_ff2_2"][0])
            for p in range(second_mlp + 8 * (CHUNKS - 1), len(loads)):
                load(p)
            for a in range(4):
                sp.wait_ge(y_copied, 2 * a + 2)
                sp.dma_start(d["out"][0, a * P:(a + 1) * P, :], ON[:, a, :]).then_inc(out_done, 16)
            sp.wait_ge(out_done, 64)

        @block.gpsimd
        def _(pool):
            step = 0

            def after(ins):
                nonlocal step
                step += 1
                ins.then_inc(pool_step, 1)
                pool.wait_ge(pool_step, step)

            after(pool.memset(ident[:, :], 0.0))
            pool.memset(ones[:, :], 1.0).then_inc(consts_ready, 1)
            pool.affine_select(out=ident[:, :], in_=ident[:, :], compare_op=ALU.not_equal, fill=1.0, base=0,
                               pattern=[[-1, P]], channel_multiplier=1).then_inc(consts_ready, 1)
            pool.iota(DI, pattern=[[-1, 512]], base=384, channel_multiplier=1).then_inc(di_ready, 1)
            after(pool.memset(SBM, 0.0))
            pool.affine_select(out=SBM, in_=SBM, compare_op=ALU.is_gt, fill=NEG, base=384,
                               pattern=[[-1, 512]], channel_multiplier=1).then_inc(bias_ready, 1)
            pool.wait_ge(dist_raw, 3)
            for dist, base, n in ((D1, 384, 512), (D2, 384, 512)):
                pool.affine_select(out=dist, in_=dist, compare_op=ALU.is_ge, fill=NEG, base=base,
                                   pattern=[[-1, n]], channel_multiplier=1).then_inc(bias_ready, 1)
            after(pool.affine_select(out=D0, in_=D0, compare_op=ALU.is_ge, fill=NEG, base=128,
                                     pattern=[[-1, 256]], channel_multiplier=1))
            pool.affine_select(out=D0, in_=D0, compare_op=ALU.is_ge, fill=NEG, base=0,
                               pattern=[[1, 256]], channel_multiplier=-1).then_inc(bias_ready, 1)
            after(pool.memset(masks[:, :, :], 1.0))
            for i, b in enumerate((32, 16, 8, 4, 2, 1)):
                for h in range(2):
                    v = masks[64 * h:64 * h + 64, i, :].rearrange("p (a b) -> p a b", b=b)
                    after(pool.affine_select(out=v, in_=v, compare_op=ALU.is_ge, fill=0.0, base=0,
                                             pattern=[[-b, CH // b], [0, b]], channel_multiplier=1))
                    after(pool.affine_select(out=v, in_=v, compare_op=ALU.is_ge, fill=0.0, base=b - 1,
                                             pattern=[[b, CH // b], [0, b]], channel_multiplier=-1))
            after(pool.iota(rcnt[:, :], pattern=[[1, 16]], base=1, channel_multiplier=0,
                            allow_small_or_imprecise_dtypes=True))
            pool.wait_ge(act_ready, N_MERGE + 8)
            pool.memset(q2[:, :, 0:PAD], 0.0)
            pool.memset(k2[:, :, 0:PAD], 0.0)
            pool.memset(la[:, :, 0:PAD], 0.0)
            pool.memset(v2[:, :, 0:PAD], 0.0)
            pool.memset(apad[:, :, 0:META], 0.0)
            after(pool.memset(reset, 1.0))
            pool.memset(reset.rearrange("p (a b) -> p a b", b=CH)[:, :, 0:1], 0.0).then_inc(zeros2_ready, 1)

        @block.scalar
        def _(act):
            def convert(t):
                if t >= T_END:
                    return
                p, half, kt, n = slab[t]
                if half == 0:
                    act.wait_ge(w_landed[p % 2], 16 * (p // 2 + 1))
                if t >= 2:
                    act.wait_ge(slab_done, t - 1)
                act.activation(w_slab(wh, t % 2, kt), raw_slab(t), ACT.Copy).then_inc(hi_ready, 1)

            def split(n, dst, src):
                act.wait_ge(f_ready, n + 1)
                act.activation(dst, src, ACT.Copy).then_inc(hi_split, 1)

            def square(norm, m, block):
                f = 8 * norm + m
                if f >= 2:
                    act.wait_ge(ss_done, f - 1)
                src = X[:, m, S2 - width(block):S2]
                act.activation(SQ[:, f % 2, 0:width(block)], src, ACT.Square).then_inc(sq_ready, 1)

            def feed(norm, n, m, block, dst=None):
                split(n, (Ah if dst is None else dst)[:, m, 0:width(block)], F[:, n % 2, 0:width(block)])
                square(norm, m, block)

            def stats(norm, block):
                act.wait_ge(ms_ready, norm + 1)
                act.activation(RS[:, 0:width(block)], RS[:, 0:width(block)], ACT.Sqrt).then_inc(sqrt_ready, 1)

            def gate(t, g, col, no, block):
                act.wait_ge(evac_done, t + 1)
                act.activation(g, g, ACT.Exp, bias=negb[:, col:col + 1] if col is not None else 0.0,
                               scale=-1.0).then_inc(gate_exp, 1)

            def mlp_chunk(which, c, last):
                t0, n0, p0 = MLPS[which]
                w = width(which)
                for j in range(16):
                    t = t0 + j
                    if not (last and j == 15 and which == 2):
                        i = (j + 1) // 2
                        if j % 2:
                            act.wait_ge(w_landed[(p0 + i) % 2], (p0 + i) // 2 * 16 + 16 + 64 * c)
                        act.wait_ge(slab_done, t + 16 * c)
                        if last and j == 15:
                            p, half, kt, n = slab[T2]
                            src = raw_half(p % 2, half, kt, n)
                        else:
                            src = raw_half((p0 + i) % 2, (j + 1) % 2, KT, 2)
                        act.activation(w_slab(wh, (t + 1) % 2, KT), src, ACT.Copy).then_inc(hi_ready, 1)
                    if j < 8:
                        act.wait_ge(f_ready, n0 + 8 * c + (j + 1))
                        act.activation(Ah[:, j, 0:w], F[:, (n0 + j) % 2, 0:w], ACT.Copy).then_inc(hi_split, 1)
                    elif last:
                        act.wait_ge(evac_done, t + 16 * c + 1)
                        square(2 if which == 1 else 5, j - 8, which)

            def mlp(which):
                with act.Fori(0, CHUNKS - 1) as c:
                    mlp_chunk(which, c, False)
                mlp_chunk(which, CHUNKS - 1, True)

            act.wait_ge(vec_ready, 1)
            act.activation(negb[:, :], vecT[:, B_GATE:B_GATE + 16], ACT.Copy, scale=-1.0).then_inc(negb_ready, 1)
            convert(0)
            for m in range(KT):
                feed(0, N_MIX + m, m, 1)
            act.wait_ge(negb_ready, 1)

            def v_copy(i, dst):
                act.wait_ge(vtrans_done, i + 1)
                act.activation(dst, ps[:, 6 + i % 2, :].rearrange("p (a b) -> p a b", a=4), ACT.Copy)\
                   .then_inc(vnat_copied, 1)

            for t in range(T_QKV_A, T_GATE_A):
                convert(t + 1)
                if t == 0:
                    stats(0, 1)
                if t >= T_QKV_A + 14:
                    v_copy(t - 14, Vna[:, :, (t - 14) * P:(t - 13) * P])
            for i in (4, 5):
                v_copy(i, Vna[:, :, i * P:(i + 1) * P])

            def dil_exp(u):
                ncol = sum(g[1] for g in dil_groups(u // 4)) * P
                act.wait_ge(negmax_ready, u + 1)
                act.activation(Lg[:, u % 2, 0:ncol], Lg[:, u % 2, 0:ncol], ACT.Exp, bias=stat[:, 1, u:u + 1],
                               scale=0.125, accum_out=stat[:, 2, u:u + 1]).then_inc(probs_ready, 1)

            def dil_copy(u):
                if u >= 1:
                    act.wait_ge(pv_done, u)
                for g, (_, nb, col) in enumerate(dil_groups(u // 4)):
                    act.wait_ge(pt_psum, 3 * u + g + 1)
                    act.activation(PT[:, col // P:col // P + nb, :],
                                   ps[:, 5 + (3 * u + g) % 2, 0:nb * P].rearrange("p (a b) -> p a b", a=nb), ACT.Copy)\
                       .then_inc(pt_copied, 1)

            def oa_hi_copy(n):
                act.wait_ge(oT_psum, n + 1)
                act.activation(Bh[:, 0:2, n * P:(n + 1) * P],
                               ps[:, 7, 256:512].rearrange("p (a b) -> p a b", a=2), ACT.Copy).then_inc(oa_hi, 1)

            for u in range(16 + 3):
                if u % 2 == 0 and u < 16:
                    s = u // 2
                    convert(T_GATE_A + s + 1)
                if 0 <= u - 2 < 16:
                    dil_copy(u - 2)
                if u >= 7 and u % 4 == 3:
                    oa_hi_copy(u // 4 - 1)
                if 0 <= u - 1 < 16:
                    dil_exp(u - 1)
                if u % 2 == 0 and 2 <= u < 16:
                    s = u // 2
                    gate(T_GATE_A + s - 1, GA[:, s - 1, :], s - 1, s - 1, 1)
            gate(T_GATE_A + 7, GA[:, 7, :], 7, 7, 1)
            oa_hi_copy(3)

            for t in range(T_QKV_B, T_GATE_B):
                convert(t + 1)
                i = t - T_QKV_B - 8 - 2
                if i >= 0:
                    v_copy(6 + i, Vnb[:, :, i * P:(i + 1) * P])
            for i in (2, 3):
                v_copy(6 + i, Vnb[:, :, i * P:(i + 1) * P])

            def sb_ln_chain(w):
                e = Es[:, w % 2, 0:P * (w // 8 + 1)]
                act.wait_ge(z_done, w + 1)
                if w >= 2:
                    act.wait_ge(sb_scan, w - 1)
                act.activation(e, Zs[:, w % 2, 0:P * (w // 8 + 1)], ACT.Abs).then_inc(sb_abs, 1)
                act.wait_ge(sb_abs, w + 1)
                act.activation(e, e, ACT.Exp, scale=-1.0).then_inc(sb_exp, 1)
                act.wait_ge(sb_exp, w + 1)
                act.activation(e, e, ACT.Ln, bias=1.0).then_inc(sb_ln, 1)

            def sb_prob(w):
                act.wait_ge(sb_la, w + 1)
                c = Cs[:, w % 2, 0:P * (w // 8 + 1)]
                act.activation(c, c, ACT.Exp).then_inc(sb_probs, 1)

            def sb_copy(w):
                act.wait_ge(sb_pt_psum, w + 1)
                if w >= 2:
                    act.wait_ge(sb_pv, w - 1)
                nk = P * (w // 8 + 1)
                act.activation(PTb[:, w % 2, 0:nk], ps[:, 4 + w % 2, 0:nk], ACT.Copy).then_inc(sb_pt_copied, 1)

            def sb_out(n):
                act.wait_ge(sb_pv, 8 * n + 8)
                if n >= 1:
                    act.wait_ge(obT_psum, n)
                act.activation(onatb, ps[:, 6, :], ACT.Copy).then_inc(ob_nat, 1)

            def ob_hi_copy(n):
                act.wait_ge(obT_psum, n + 1)
                act.activation(Bh[:, 2:6, n * P:(n + 1) * P],
                               ps[:, 7, :].rearrange("p (a b) -> p a b", a=4), ACT.Copy).then_inc(ob_hi, 1)

            for i in range(32 + 6):
                if i % 4 == 0 and i < 32:
                    convert(T_GATE_B + i // 4 + 1)
                if 0 <= i - 4 < 32:
                    sb_copy(i - 4)
                if 0 <= i - 1 < 32:
                    sb_ln_chain(i - 1)
                if 0 <= i - 2 < 32:
                    sb_prob(i - 2)
                if i % 4 == 0 and 4 <= i <= 32:
                    s = i // 4 - 1
                    gate(T_GATE_B + s, GB[:, s, :], 8 + s, 8 + s, 1)
                if i >= 12 and (i - 12) % 8 == 0:
                    sb_out((i - 12) // 8)
                if i >= 13 and (i - 13) % 8 == 0:
                    ob_hi_copy((i - 13) // 8)

            for t in range(T_UP_A, T_UP_B):
                convert(t + 1)
            for m in range(KT):
                convert(T_UP_B + m + 1)
                split(N_MERGE + m, Ah[:, m, 0:S1], F[:, (N_MERGE + m) % 2, 0:S1])
            for m in range(KT):
                convert(T_OUT + m + 1)
                feed(1, N_MLP + m, m, 1, Bh)
            stats(1, 1)
            mlp(1)

            stats(2, 1)
            for m in range(KT):
                feed(3, N2_MIX + m, m, 2)

            def decay_exp():
                for j in range(2):
                    u, e = UU[:, j, :], E2
                    act.wait_ge(u_ready, j + 1)
                    if j == 1:
                        act.wait_ge(la_ready, 1)
                    act.activation(e, u, ACT.Abs).then_inc(u_abs, 1)
                    act.wait_ge(u_abs, j + 1)
                    act.activation(e, e, ACT.Exp, scale=-1.0).then_inc(u_exp, 1)
                    act.wait_ge(u_exp, j + 1)
                    act.activation(e, e, ACT.Ln, bias=1.0).then_inc(u_ln, 1)
                for j in range(2):
                    act.wait_ge(bs_ready, j + 1)
                    act.activation(ebe[:, j, :], bS[:, j, CH - 1:PADL:CH], ACT.Exp, scale=1.0 / TAU)\
                       .then_inc(ebe_ready, 1)

            def v_rows(i):
                for g in range(3) if i == 3 else ():
                    pass

            def job(what):
                kind = what[0]
                if kind == "decay":
                    decay_exp()
                elif kind == "v_rows":
                    h = what[1]
                    for g, (c0, nc_) in enumerate(((0, 4), (4, 4), (8, 1))):
                        act.wait_ge(vr_psum, 3 * h + g + 1)
                        beta = 64 * (h % 2)
                        act.activation(Vn[beta:beta + 64, h // 2, c0 * P:(c0 + nc_) * P],
                                       ps[beta:beta + 64, 4 + (3 * h + g) % 4, 0:nc_ * P], ACT.Copy)\
                           .then_inc(vr_copied, 1)
                elif kind == "unit_d":
                    y = what[1]
                    l, j = y // 2, y % 2
                    if l == U_DIAG // 2:
                        return
                    x = exp_no(y)
                    e = Ed[:, x % 2, :]
                    if y < U_START:
                        act.wait_ge(d_ready, x + 1)
                        act.activation(e, e, ACT.Abs).then_inc(d_abs, 1)
                        act.wait_ge(d_abs, x + 1)
                        act.activation(e, e, ACT.Exp, scale=-1.0 / TAU).then_inc(d_exp, 1)
                    else:
                        act.wait_ge(qk_ready, y - 2 + 1)
                        act.activation(e, bS[:, j, :], ACT.Exp, scale=1.0 / TAU).then_inc(d_exp, 1)
                elif kind == "unit_mm":
                    y = what[1]
                    if U_END <= y < U_START:
                        j = y - U_END
                        act.wait_ge(kn_psum, j + 1)
                        act.activation(Kn[:, j, :], ps[:, 4 + 2 * j, :], ACT.Copy).then_inc(kn_copied, 1)
                elif kind == "o_mm":
                    h = what[1]
                    act.wait_ge(o_copied, h + 1)
                    if h >= 1:
                        act.wait_ge(o_stat, h)
                    act.activation(osb2, osb, ACT.Square).then_inc(o_sq, 1)
                elif kind == "o_norm":
                    h = what[1]
                    act.wait_ge(o_ms, h + 1)
                    act.activation(SS[:, :], SS[:, :], ACT.Sqrt).then_inc(o_sqrt, 1)
                    n = N2_O + h
                    split(n, Bh[:, h, :], F[:, n % 2, :])

            def evac(t):
                if T2_A <= t < T2_PM:
                    n = N2_POOL + t - T2_A
                    split(n, Bh[:, t - T2_A, :], F[:, n % 2, :])
                elif T2_PM <= t < T2_GY:
                    n = N2_PM + t - T2_PM
                    split(n, Bh[:, 4 + t - T2_PM, :], F[:, n % 2, :])
                elif T2_GY <= t < T2_R and (t - T2_GY) % 4 < 2:
                    gate(t, G2[:, (t - T2_GY) % 2, :], None, 16 + (t - T2_GY) // 4 * 2 + (t - T2_GY) % 4, 2)
                elif T2_R <= t < T2_M:
                    i = t - T2_R
                    act.wait_ge(evac_done, t + 1)
                    act.activation(G2[:, i % 2, :], sr[:, i, :], ACT.Exp, scale=-1.0).then_inc(silu_exp, 1)
                elif T2_M <= t < T2_OUT and (t - T2_M) % 4 < 2:
                    gate(t, G2[:, (t - T2_M) % 2, :], None, 24, 2)

            for t in range(T2, T2_OUT):
                convert(t + 1)
                if t == T2:
                    stats(3, 2)
                if t > T2:
                    evac(t - 1)
                for what in between[t]:
                    job(what)
            for m in range(KT):
                n = N2_M + m
                split(n, Ah[:, m, :], ma[:, m, :])
            for m in range(KT):
                convert(T2_OUT + m + 1)
                feed(4, N2_FFN + m, m, 2, Bh)
            stats(4, 2)
            mlp(2)
            stats(5, 2)
            for a in range(4):
                act.wait_ge(y_psum, 2 * a + 1)
                act.activation(ON[:, a, 0:512], ps[:, 4, :], ACT.Copy).then_inc(y_copied, 1)
                act.wait_ge(y_psum, 2 * a + 2)
                act.activation(ON[:, a, 512:1024], ps[:, 5, :], ACT.Copy).then_inc(y_copied, 1)

        @block.vector
        def _(dve):
            def convert(t):
                if t >= T_END:
                    return
                kt = slab[t][2]
                dve.wait_ge(hi_ready, t + 1)
                dve.tensor_tensor(w_slab(wl, t % 2, kt), raw_slab(t), w_slab(wh, t % 2, kt), ALU.subtract)\
                   .then_inc(lo_ready, 1)

            def split(n, lo, src, hi):
                dve.wait_ge(hi_split, n + 1)
                dve.tensor_tensor(lo, src, hi, ALU.subtract).then_inc(act_ready, 1)

            def add_square(norm, m, block):
                w = width(block)
                f = 8 * norm + m
                dve.wait_ge(sq_ready, f + 1)
                if m == 0:
                    dve.tensor_copy(SS[:, 0:w], SQ[:, f % 2, 0:w]).then_inc(ss_done, 1)
                else:
                    dve.wait_ge(ss_done, f)
                    dve.tensor_tensor(SS[:, 0:w], SS[:, 0:w], SQ[:, f % 2, 0:w], ALU.add).then_inc(ss_done, 1)

            def scale_feed(n, m, col, block):
                w = width(block)
                dve.tensor_scalar(F[:, n % 2, 0:w], X[:, m, S2 - w:S2], vecT[:, col + m:col + m + 1], None, ALU.mult)\
                   .then_inc(f_ready, 1)

            def rest_feed(norm, n, m, block, hi=None, lo=None):
                w = width(block)
                hi, lo = (Ah, Al) if hi is None else (hi, lo)
                split(n, lo[:, m, 0:w], F[:, n % 2, 0:w], hi[:, m, 0:w])
                add_square(norm, m, block)

            def stats(norm, block):
                w = width(block)
                dve.wait_ge(stat_done, norm + 1)
                src = ps[:, 7, :] if block == 1 else ps[:, 6:8, 0:HALF2]
                dve.tensor_scalar(tokens(RS[:, 0:w], block), src, 1.0 / DM, EPS, ALU.mult, ALU.add)\
                   .then_inc(ms_ready, 1)
                dve.wait_ge(sqrt_ready, norm + 1)
                dve.reciprocal(RS[:, 0:w], RS[:, 0:w]).then_inc(rstd_ready, 1)
                dve.wait_ge(rstd_ready, norm + 1)

            def scaled(t, dst, block, rows=P):
                dve.wait_ge(slab_done, t + 1)
                dve.tensor_tensor(tokens(dst, block), dense_psum(t, block)[0:rows],
                                  tokens(RS[0:rows, 0:width(block)], block), ALU.mult).then_inc(evac_done, 1)

            def finish_gate(no, g):
                dve.wait_ge(gate_exp, no + 1)
                dve.tensor_scalar(g, g, 1.0, None, ALU.add).then_inc(gate_inc, 1)
                dve.wait_ge(gate_inc, no + 1)
                dve.reciprocal(g, g).then_inc(gate_done, 1)

            def add_residual(t, ps_t, m, block):
                w = width(block)
                dve.wait_ge(slab_done, t + 1)
                dve.tensor_tensor(tokens(X[:, m, S2 - w:S2], block), tokens(X[:, m, S2 - w:S2], block),
                                  dense_psum(ps_t, block), ALU.add).then_inc(evac_done, 1)

            def mlp_chunk(which, c, last):
                t0, n0, p0 = MLPS[which]
                w = width(which)
                for j in range(16):
                    t = t0 + j
                    if not (last and j == 15 and which == 2):
                        if last and j == 15:
                            p, half, kt, n = slab[T2]
                            src = raw_half(p % 2, half, kt, n)
                        else:
                            src = raw_half((p0 + (j + 1) // 2) % 2, (j + 1) % 2, KT, 2)
                        dve.wait_ge(hi_ready, t + 16 * c + 2)
                        dve.tensor_tensor(w_slab(wl, (t + 1) % 2, KT), src, w_slab(wh, (t + 1) % 2, KT),
                                          ALU.subtract).then_inc(lo_ready, 1)
                    if j < 8:
                        f = F[:, (n0 + j) % 2, 0:w]
                        dve.wait_ge(slab_done, t + 16 * c + 1)
                        dve.tensor_tensor(tokens(f, which), dense_psum(t, which), tokens(RS[:, 0:w], which),
                                          ALU.mult).then_inc(evac_done, 1)
                        dve.wait_ge(evac_done, t + 16 * c + 1)
                        dve.scalar_tensor_tensor(out=f, in0=f, scalar=0.0, in1=f, op0=ALU.max, op1=ALU.mult)\
                           .then_inc(f_ready, 1)
                        dve.wait_ge(hi_split, n0 + 8 * c + (j + 1))
                        dve.tensor_tensor(Al[:, j, 0:w], f, Ah[:, j, 0:w], ALU.subtract).then_inc(act_ready, 1)
                    else:
                        add_residual(t + 16 * c, t, j - 8, which)
                        if last:
                            add_square(2 if which == 1 else 5, j - 8, which)

            def mlp(which):
                with dve.Fori(0, CHUNKS - 1) as c:
                    mlp_chunk(which, c, False)
                mlp_chunk(which, CHUNKS - 1, True)

            dve.wait_ge(di_ready, 1)
            for i, (dist, dil) in enumerate(((D1, 4), (D2, 16))):
                dve.tensor_scalar(DM4, DI, dil - 1, None, ALU.bitwise_and).then_inc(dist_step, 1)
                dve.wait_ge(dist_step, 2 * i + 1)
                dve.tensor_scalar(PEN, DM4, 0.0, NEG, ALU.is_gt, ALU.mult).then_inc(dist_step, 1)
                dve.wait_ge(dist_step, 2 * i + 2)
                dve.scalar_tensor_tensor(out=dist, in0=DI, scalar=-1.0, in1=PEN, op0=ALU.mult, op1=ALU.add)\
                   .then_inc(dist_raw, 1)
                dve.wait_ge(dist_raw, i + 1)
            dve.tensor_scalar(D0, DI[:, 256:512], -1.0, None, ALU.mult).then_inc(dist_raw, 1)
            dve.wait_ge(vec_psum, 1)
            dve.tensor_copy(vecT[:, :], ps[:, 5, 0:NVEC]).then_inc(vec_ready, 1)
            dve.wait_ge(meta_psum, 1)
            dve.tensor_copy(X[:, :, 0:META], ps[:, 4, 0:KT * META].rearrange("p (a b) -> p a b", a=KT))\
               .then_inc(meta_copied, 1)
            dve.wait_ge(vec_ready, 1)
            for m in range(KT):
                dve.wait_ge(xt_psum, m + 1)
                dve.tensor_copy(X[:, m, META:S2], ps[:, 2 + m % 2, :]).then_inc(xt_copied, 1)
                dve.wait_ge(xt_copied, m + 1)
                scale_feed(N_MIX + m, m, G_MIX, 1)
                if m == 0:
                    convert(0)
                rest_feed(0, N_MIX + m, m, 1)

            for t in range(T_QKV_A, T_GATE_A + 1):
                if t == T_QKV_A + 1:
                    stats(0, 1)
                if t > T_QKV_A:
                    i = t - 1
                    if i >= 14:
                        dve.wait_ge(vtrans_done, i - 13)
                    scaled(i, qa[:, i, :] if i < 6 else ka[:, i - 6, :] if i < 12 else vt[:, i % 2, :], 1)
                if t < T_GATE_A:
                    convert(t + 1)

            def dil_softmax(u):
                n, j = u // 4, u % 4
                groups = dil_groups(n)
                dve.wait_ge(scores_done, u + 1)
                if u >= 2:
                    dve.wait_ge(pt_psum, 3 * (u - 1))
                for g, (k0, nb, col) in enumerate(groups):
                    dist = (D0, D1, D2)[g]
                    w = nb * P
                    dve.scalar_tensor_tensor(out=Lg[:, u % 2, col:col + w], in0=dist[:, dist.shape[1] - w:],
                                             scalar=8.0 * SLOPES[4 * g + j], in1=ps[:, 2 + g, 0:w],
                                             op0=ALU.mult, op1=ALU.add).then_inc(logits_done, 1)
                dve.wait_ge(logits_done, 3 * u + 3)
                ncol = sum(g[1] for g in groups) * P
                dve.tensor_reduce(stat[:, 0, u:u + 1], Lg[:, u % 2, 0:ncol], AX_X, ALU.max).then_inc(max_done, 1)
                dve.wait_ge(max_done, u + 1)
                dve.tensor_scalar(stat[:, 1, u:u + 1], stat[:, 0, u:u + 1], -0.125, None, ALU.mult)\
                   .then_inc(negmax_ready, 1)

            def dil_norm(u):
                n, j = u // 4, u % 4
                dve.wait_ge(probs_ready, u + 1)
                dve.reciprocal(stat[:, 3, u:u + 1], stat[:, 2, u:u + 1]).then_inc(rden_done, 1)
                dve.wait_ge(rden_done, u + 1)
                dve.wait_ge(pv_done, u + 1)
                if j == 0 and n >= 2:
                    dve.wait_ge(oT_psum, n - 1)
                dve.tensor_scalar(onat[n % 2][:, j * DH:(j + 1) * DH], ps[:, 7, j * DH:(j + 1) * DH],
                                  stat[:, 3, u:u + 1], None, ALU.mult).then_inc(o_norm, 1)

            def oa_lo(n):
                dve.wait_ge(oa_hi, n + 1)
                dve.tensor_tensor(Bl[:, 0:2, n * P:(n + 1) * P],
                                  ps[:, 7, 256:512].rearrange("p (a b) -> p a b", a=2),
                                  Bh[:, 0:2, n * P:(n + 1) * P], ALU.subtract).then_inc(oa_ready, 1)

            dve.wait_ge(bias_ready, 4)
            for u in range(16 + 3):
                if 0 <= u - 3 < 16:
                    dil_norm(u - 3)
                if u >= 7 and u % 4 == 3:
                    oa_lo((u - 7) // 4)
                if u % 2 == 0 and u < 16:
                    s = u // 2
                    if s >= 1:
                        scaled(T_GATE_A + s - 1, GA[:, s - 1, :], 1)
                    convert(T_GATE_A + s + 1)
                if u % 2 == 1 and 3 <= u < 16:
                    finish_gate(u // 2 - 1, GA[:, u // 2 - 1, :])
                if 0 <= u - 1 < 16:
                    dil_softmax(u - 1)
                if u == 16:
                    scaled(T_GATE_A + 7, GA[:, 7, :], 1)
            finish_gate(7, GA[:, 7, :])
            oa_lo(3)

            for t in range(T_QKV_B, T_GATE_B + 1):
                if t > T_QKV_B:
                    i = t - 1 - T_QKV_B
                    if i >= 10:
                        dve.wait_ge(vtrans_done, 6 + i - 9)
                    scaled(t - 1, qb[:, i, :] if i < 4 else kb[:, i - 4, :] if i < 8 else vtb[:, i % 2, :], 1)
                if t < T_GATE_B:
                    convert(t + 1)

            def sb_z(w):
                n = w // 8
                nk = P * (n + 1)
                dve.wait_ge(sb_scores, w + 1)
                if w >= 2:
                    dve.wait_ge(sb_la, w - 1)
                dve.scalar_tensor_tensor(out=Zs[:, w % 2, 0:nk], in0=ps[:, 2 + w % 2, 0:nk], scalar=0.125,
                                         in1=SBM[:, 512 - nk:512], op0=ALU.mult, op1=ALU.add).then_inc(z_done, 1)

            def sb_log_a(w):
                nk = P * (w // 8 + 1)
                z, e, c = Zs[:, w % 2, 0:nk], Es[:, w % 2, 0:nk], Cs[:, w % 2, 0:nk]
                dve.wait_ge(sb_ln, w + 1)
                dve.scalar_tensor_tensor(out=e, in0=z, scalar=0.0, in1=e, op0=ALU.max, op1=ALU.add)\
                   .then_inc(sb_sp, 1)
                dve.wait_ge(sb_sp, w + 1)
                if w >= 2:
                    dve.wait_ge(sb_pt_psum, w - 1)
                dve.tensor_tensor_scan(c[:, ::-1], ones[:, 0:1].to_broadcast([P, nk]), e[:, ::-1], 0.0,
                                       ALU.mult, ALU.add).then_inc(sb_scan, 1)
                dve.wait_ge(sb_scan, w + 1)
                dve.tensor_tensor(c, z, c, ALU.subtract).then_inc(sb_la, 1)

            def ob_lo(n):
                dve.wait_ge(ob_hi, n + 1)
                dve.tensor_tensor(Bl[:, 2:6, n * P:(n + 1) * P], ps[:, 7, :].rearrange("p (a b) -> p a b", a=4),
                                  Bh[:, 2:6, n * P:(n + 1) * P], ALU.subtract).then_inc(ob_ready, 1)

            for i in range(32 + 6):
                if i % 4 == 0 and i <= 32:
                    s = i // 4
                    if s >= 1:
                        scaled(T_GATE_B + s - 1, GB[:, s - 1, :], 1)
                    if s < 8:
                        convert(T_GATE_B + s + 1)
                if 0 <= i - 1 < 32:
                    sb_z(i - 1)
                if 0 <= i - 2 < 32:
                    sb_log_a(i - 2)
                if i % 4 == 2 and 4 <= i <= 35:
                    finish_gate(8 + i // 4 - 1, GB[:, i // 4 - 1, :])
                if i >= 13 and (i - 13) % 8 == 0:
                    ob_lo((i - 13) // 8)

            for m in range(KT):
                convert(T_UP_A + m + 1)
                t = T_UP_A + m
                dve.wait_ge(slab_done, t + 1)
                dve.wait_ge(gate_done, m + 1)
                dve.tensor_tensor(GA[:, m, :], dense_psum(t, 1), GA[:, m, :], ALU.mult).then_inc(evac_done, 1)
            for m in range(KT):
                convert(T_UP_B + m + 1)
                t = T_UP_B + m
                n = N_MERGE + m
                f = F[:, n % 2, 0:S1]
                dve.wait_ge(slab_done, t + 1)
                dve.wait_ge(gate_done, 8 + m + 1)
                dve.tensor_tensor(f, dense_psum(t, 1), GB[:, m, :], ALU.mult).then_inc(evac_done, 1)
                dve.wait_ge(evac_done, t + 1)
                dve.tensor_tensor(f, f, GA[:, m, :], ALU.add).then_inc(f_ready, 1)
                split(n, Al[:, m, 0:S1], f, Ah[:, m, 0:S1])
            for m in range(KT):
                convert(T_OUT + m + 1)
                t = T_OUT + m
                add_residual(t, t, m, 1)
                dve.wait_ge(evac_done, t + 1)
                scale_feed(N_MLP + m, m, G_MLP, 1)
                rest_feed(1, N_MLP + m, m, 1, Bh, Bl)
            stats(1, 1)
            mlp(1)

            stats(2, 1)
            for m in range(KT):
                x = X[:, m, META:S2]
                dve.scalar_tensor_tensor(out=x, in0=x, scalar=vecT[:, G_FIN + m:G_FIN + m + 1], in1=RS[:, 0:S1],
                                         op0=ALU.mult, op1=ALU.mult).then_inc(x_normed, 1)
                dve.wait_ge(x_normed, m + 1)
                if m == 0:
                    dve.wait_ge(meta_copied, 1)
                scale_feed(N2_MIX + m, m, G_MIX2, 2)
                rest_feed(3, N2_MIX + m, m, 2)

            steps = {"win": 0, "edge": 0, "prod": 0}

            def pool_window(g):
                a = apad[:, g % 2, :]
                cur = a
                for k in range(g + 1):
                    s = 2 ** k
                    nxt = wsum[:, k % 2, :]
                    lo = 2 * s if k < g else META
                    dve.tensor_tensor(nxt[:, lo:], cur[:, lo:], cur[:, lo - s:META + S2 - s], ALU.add)\
                       .then_inc(win_done, 1)
                    steps["win"] += 1
                    dve.wait_ge(win_done, steps["win"])
                    cur = nxt
                w = WINDOWS[g]
                head = cur[:, META:META + w - 1]
                dve.tensor_tensor(head, head, rcnt[:, 0:w - 1], ALU.mult).then_inc(edge_done, 1)
                steps["edge"] += 1
                dve.wait_ge(edge_done, steps["edge"])
                n = N2_POOL + g
                f = F[:, n % 2, :]
                dve.tensor_tensor(f[:, 0:w - 1], head, a[:, META:META + w - 1], ALU.subtract)
                dve.scalar_tensor_tensor(out=f[:, w - 1:], in0=cur[:, META + w - 1:], scalar=1.0 / w,
                                         in1=a[:, META + w - 1:], op0=ALU.mult, op1=ALU.subtract)\
                   .then_inc(f_ready, 1)
                split(n, Bl[:, g, :], f, Bh[:, g, :])

            gate_no = [16]

            def evac(t):
                if t < T2_LR:
                    i = t - T2
                    dst = (k2 if i < 2 else q2)[:, i % 2, PAD:PADL]
                    dve.wait_ge(slab_done, t + 1)
                    if i < 2:
                        scaled(t, dst, 2)
                    else:
                        dve.scalar_tensor_tensor(out=tokens(dst, 2), in0=dense_psum(t, 2), scalar=0.125,
                                                 in1=tokens(RS[:, :], 2), op0=ALU.mult, op1=ALU.mult)\
                           .then_inc(evac_done, 1)
                elif t == T2_LR:
                    scaled(t, lr[0:16, :], 2, 16)
                elif t < T2_A:
                    scaled(t, v2[:, t - T2_V, PAD:PADL], 2)
                elif t < T2_PM:
                    g = t - T2_A
                    scaled(t, apad[:, g % 2, META:], 2)
                    dve.wait_ge(evac_done, t + 1)
                    pool_window(g)
                elif t < T2_GY:
                    g = t - T2_PM
                    n = N2_PM + g
                    f = F[:, n % 2, :]
                    dve.wait_ge(slab_done, t + 1)
                    dve.tensor_scalar(tokens(f, 2), dense_psum(t, 2), vecT[:, POOL_SC + g:POOL_SC + g + 1], None,
                                      ALU.mult).then_inc(evac_done, 1)
                    dve.wait_ge(evac_done, t + 1)
                    dve.sem_inc(f_ready, 1)
                    split(n, Bl[:, 4 + g, :], f, Bh[:, 4 + g, :])
                elif t < T2_R:
                    i = t - T2_GY
                    if i % 4 < 2:
                        scaled(t, G2[:, i % 2, :], 2)
                    else:
                        m = i // 4 * 2 + i % 2
                        finish_gate(gate_no[0], G2[:, i % 2, :])
                        gate_no[0] += 1
                        dve.wait_ge(gate_done, gate_no[0])
                        dve.wait_ge(slab_done, t + 1)
                        if m == 0:
                            dve.wait_ge(vr_psum, 12)
                        dve.tensor_tensor(tokens(ma[:, m, :], 2), dense_psum(t, 2), tokens(G2[:, i % 2, :], 2),
                                          ALU.mult).then_inc(evac_done, 1)
                elif t < T2_M:
                    i = t - T2_R
                    scaled(t, sr[:, i, :], 2)
                    dve.wait_ge(silu_exp, i + 1)
                    g = G2[:, i % 2, :]
                    dve.tensor_scalar(g, g, 1.0, None, ALU.add).then_inc(silu_inc, 1)
                    dve.wait_ge(silu_inc, i + 1)
                    dve.reciprocal(g, g).then_inc(silu_rec, 1)
                    dve.wait_ge(silu_rec, i + 1)
                    dve.tensor_tensor(sr[:, i, :], sr[:, i, :], g, ALU.mult).then_inc(silu_done, 1)
                elif t < T2_OUT:
                    i = t - T2_M
                    if i % 4 < 2:
                        scaled(t, G2[:, i % 2, :], 2)
                    else:
                        m = i // 4 * 2 + i % 2
                        g = G2[:, i % 2, :]
                        finish_gate(gate_no[0], g)
                        gate_no[0] += 1
                        dve.wait_ge(gate_done, gate_no[0])
                        dve.wait_ge(slab_done, t + 1)
                        dve.tensor_tensor(tokens(g, 2), dense_psum(t, 2), tokens(g, 2), ALU.mult)\
                           .then_inc(evac_done, 1)
                        dve.wait_ge(evac_done, t + 1)
                        dve.tensor_tensor(ma[:, m, :], ma[:, m, :], g, ALU.add).then_inc(f_ready, 1)

            def job(what):
                kind = what[0]
                if kind == "gate_up":
                    for j in range(2):
                        dve.wait_ge(gu_psum, j + 1)
                        dve.tensor_scalar(tokens(UU[:, j, :], 2), ps[:, 4 + 2 * j:6 + 2 * j, 0:HALF2],
                                          vecT[:, B_GATE2 + j:B_GATE2 + j + 1], None, ALU.add).then_inc(u_ready, 1)
                elif kind == "decay":
                    for j in range(2):
                        dve.wait_ge(u_ln, j + 1)
                        dve.scalar_tensor_tensor(out=la[:, j, PAD:PADL], in0=UU[:, j, :], scalar=0.0, in1=E2,
                                                 op0=ALU.min, op1=ALU.subtract).then_inc(la_ready, 1)
                        dve.wait_ge(la_ready, j + 1)
                        dve.tensor_tensor_scan(bS[:, j, :], reset, la[:, j, :], 0.0, ALU.mult, ALU.add)\
                           .then_inc(bs_ready, 1)
                    dve.wait_ge(bs_ready, 2)
                elif kind == "unit_d":
                    y = what[1]
                    if y // 2 == U_DIAG // 2 or y >= U_START:
                        return
                    x = exp_no(y)
                    v, ref, b = level_ref(y)
                    if x >= 2:
                        dve.wait_ge(qk_ready, (y - 2 if y < U_DIAG else y - 4) + 1)
                    dve.tensor_tensor(Ed[:, x % 2, :].rearrange("p (a b) -> p a b", b=b), v, ref, ALU.subtract)\
                       .then_inc(d_ready, 1)
                elif kind == "unit_qk":
                    y = what[1]
                    l, j = y // 2, y % 2
                    if l == U_DIAG // 2:
                        dve.sem_inc(qk_ready, 1)
                        return
                    x = exp_no(y)
                    e = Ed[:, x % 2, :]
                    dve.wait_ge(d_exp, x + 1)
                    if y < U_DIAG:
                        if y >= 2:
                            dve.wait_ge(mm_done, y - 1)
                        dve.tensor_tensor(Qp[:, j, :], q2[:, j, :], e, ALU.mult)
                        dve.tensor_tensor(Kp[:, j, :], k2[:, j, :], e, ALU.mult).then_inc(qk_ready, 1)
                    elif y < U_START:
                        dve.wait_ge(mm_done, U_DIAG - 2 + j + 1)
                        dve.tensor_tensor(Kp[:, j, :], k2[:, j, :], e, ALU.mult).then_inc(qk_ready, 1)
                    else:
                        dve.tensor_tensor(Qs[:, j, :], q2[:, j, :], e, ALU.mult).then_inc(qk_ready, 1)
                    dve.wait_ge(qk_ready, y + 1)
                elif kind == "unit_mm":
                    y = what[1]
                    l, j = y // 2, y % 2
                    if y >= U_END:
                        return
                    dve.wait_ge(mm_done, y + 1)
                    src = flat(4 + 2 * j)[:, 0:PADL]
                    if l == 0:
                        dve.tensor_copy(sc[:, j, :], src).then_inc(sc_done, 1)
                    else:
                        dve.wait_ge(sc_done, y - 1)
                        dve.copy_predicated(
                            sc[:, j, :].rearrange("p (a b) -> p a b", b=CH),
                            masks[:, l - 1, :].bitcast(U32).unsqueeze(1).to_broadcast([P, NCH, CH]),
                            src.rearrange("p (a b) -> p a b", b=CH)).then_inc(sc_done, 1)
                elif kind == "kv":
                    j = what[1]
                    dve.wait_ge(kv_psum, j + 1)
                    dve.wait_ge(ebe_ready, 2)
                    if j == 0:
                        dve.wait_ge(kn_psum, 2)
                    for c in range(8):
                        kv = flat(4 + 2 * j)[:, c * P:(c + 1) * P]
                        dst = st[:, j, c * P:(c + 1) * P]
                        if c == 0:
                            ins = dve.tensor_copy(dst, kv)
                        else:
                            ins = dve.scalar_tensor_tensor(out=dst, in0=st[:, j, (c - 1) * P:c * P],
                                                           scalar=ebe[:, j, c:c + 1], in1=kv,
                                                           op0=ALU.mult, op1=ALU.add)
                        ins.then_inc(st_done, 1)
                        dve.wait_ge(st_done, 8 * j + c + 1)
                elif kind == "o_mm":
                    h = what[1]
                    dve.wait_ge(o_psum, h + 1)
                    dve.tensor_copy(osb, flat(4)[:, PAD:PADL]).then_inc(o_copied, 1)
                elif kind == "o_norm":
                    h = what[1]
                    dve.wait_ge(o_stat, h + 1)
                    dve.tensor_scalar(tokens(SS[:, :], 2), ps[:, 6:8, 0:HALF2], 1.0 / P, EPS, ALU.mult, ALU.add)\
                       .then_inc(o_ms, 1)
                    dve.wait_ge(o_sqrt, h + 1)
                    dve.reciprocal(SS[:, :], SS[:, :]).then_inc(o_rstd, 1)
                    dve.wait_ge(o_rstd, h + 1)
                    dve.tensor_tensor(osb, osb, SS[:, :], ALU.mult).then_inc(o_scaled, 1)
                    dve.wait_ge(o_scaled, h + 1)
                    dve.wait_ge(silu_done, h + 1)
                    n = N2_O + h
                    f = F[:, n % 2, :]
                    dve.scalar_tensor_tensor(out=f, in0=osb, scalar=vecT[:, GLA_G + h:GLA_G + h + 1],
                                             in1=sr[:, h, :], op0=ALU.mult, op1=ALU.mult).then_inc(f_ready, 1)
                    split(n, Bl[:, h, :], f, Bh[:, h, :])

            dve.wait_ge(zeros2_ready, 1)
            dve.reciprocal(rcnt[:, :], rcnt[:, :]).then_inc(prod_done, 1)
            dve.wait_ge(prod_done, 1)
            for t in range(T2, T2_OUT + 1):
                if t == T2 + 1:
                    stats(3, 2)
                if t > T2:
                    evac(t - 1)
                if t < T2_OUT:
                    convert(t + 1)
                    for what in between[t]:
                        job(what)
            for m in range(KT):
                split(N2_M + m, Al[:, m, :], ma[:, m, :], Ah[:, m, :])
            for m in range(KT):
                convert(T2_OUT + m + 1)
                t = T2_OUT + m
                add_residual(t, t, m, 2)
                dve.wait_ge(evac_done, t + 1)
                scale_feed(N2_FFN + m, m, G_FFN2, 2)
                rest_feed(4, N2_FFN + m, m, 2, Bh, Bl)
            stats(4, 2)
            mlp(2)
            stats(5, 2)
            for m in range(KT):
                dve.scalar_tensor_tensor(out=Y[:, m, :], in0=X[:, m, META:S2],
                                         scalar=vecT[:, G_FIN2 + m:G_FIN2 + m + 1], in1=RS[:, META:S2],
                                         op0=ALU.mult, op1=ALU.mult).then_inc(y_ready, 1)

        @block.tensor
        def _(pe):
            def products(t_ps, slot, kt, Oh, Ol, o0, block, k_from, k_to, ready=None):
                h, l = w_slab(wh, slot, kt), w_slab(wl, slot, kt)
                last = None
                for k in range(k_from, k_to):
                    if ready is not None:
                        ready(k)
                    for i, (a, b) in enumerate(((h, Oh), (h, Ol), (l, Oh))):
                        for half in range(block):
                            w = S1 if block == 1 else HALF2
                            dst = (ps[:, t_ps % 2, :] if block == 1
                                   else ps[:, 2 * (t_ps % 2) + half, 0:HALF2])
                            last = pe.matmul(dst, a[:, k, :], b[:, o0 + k, half * w:(half + 1) * w],
                                             start=(k == 0 and i == 0), stop=(k == kt - 1 and i == 2))
                return last

            def slab_start(t):
                pe.wait_ge(lo_ready, t + 1)
                if t >= 2:
                    pe.wait_ge(evac_done, t - 1)

            def full_slab(t, Oh, Ol, o0, block, ready=None):
                kt = slab[t][2]
                slab_start(t)
                products(t, t % 2, kt, Oh, Ol, o0, block, 0, kt, ready).then_inc(slab_done, 1)

            def split_ready(n0):
                return lambda k: pe.wait_ge(act_ready, n0 + k + 1)

            def stats(norm, block):
                pe.wait_ge(ss_done, 8 * norm + 8)
                if block == 1:
                    pe.matmul(ps[:, 7, :], ones[:, :], SS[:, 0:S1], start=True, stop=True).then_inc(stat_done, 1)
                else:
                    for half in range(2):
                        mm = pe.matmul(ps[:, 6 + half, 0:HALF2], ones[:, :],
                                       SS[:, half * HALF2:(half + 1) * HALF2], start=True, stop=True)
                    mm.then_inc(stat_done, 1)

            def mlp_chunk(which, c, last):
                t0, n0, _ = MLPS[which]
                feed_n = N_MLP if which == 1 else N2_FFN
                for j in range(16):
                    t = t0 + j
                    pe.wait_ge(lo_ready, t + 16 * c + 1)
                    pe.wait_ge(evac_done, t + 16 * c - 1)
                    if j < 8:
                        ready = None
                        if not last and j == 0:
                            ready = split_ready(feed_n)
                        mm = products(t, t % 2, KT, Bh, Bl, 0, which, 0, KT, ready)
                    else:
                        ready = None
                        if j == 8:
                            def ready(k):
                                pe.wait_ge(act_ready, n0 + 8 * c + (k + 1))
                        mm = products(t, t % 2, KT, Ah, Al, 0, which, 0, KT, ready)
                    mm.then_inc(slab_done, 1)

            def mlp(which):
                with pe.Fori(0, CHUNKS - 1) as c:
                    mlp_chunk(which, c, False)
                mlp_chunk(which, CHUNKS - 1, True)

            pe.wait_ge(consts_ready, 2)
            pe.wait_ge(params_in, 16 * 12)
            pe.transpose(ps[:, 5, 0:NVEC], vrow[0:NVEC, :], ident[0:NVEC, 0:NVEC]).then_inc(vec_psum, 1)
            for m in range(KT):
                mm = pe.transpose(ps[:, 4, m * META:(m + 1) * META], mnat[0:META, m * P:(m + 1) * P],
                                  ident[0:META, 0:META])
            mm.then_inc(meta_psum, 1)
            pe.wait_ge(x_in, 16)
            for m in range(KT):
                if m >= 2:
                    pe.wait_ge(xt_copied, m - 1)
                for a in range(4):
                    mm = pe.transpose(ps[:, 2 + m % 2, a * P:(a + 1) * P], xnat[:, a, m * P:(m + 1) * P], ident[:, :])
                mm.then_inc(xt_psum, 1)

            def v_turn(i, src):
                if i >= 2:
                    pe.wait_ge(vnat_copied, i - 1)
                for a in range(4):
                    mm = pe.transpose(ps[:, 6 + i % 2, a * P:(a + 1) * P], src[:, a * P:(a + 1) * P], ident[:, :])
                mm.then_inc(vtrans_done, 1)

            full_slab(0, Ah, Al, 0, 1, split_ready(N_MIX))
            stats(0, 1)
            for t in range(1, T_GATE_A):
                full_slab(t, Ah, Al, 0, 1)
                if t >= 13:
                    pe.wait_ge(evac_done, t)
                    if t == 13:
                        pe.wait_ge(ms_ready, 1)
                    v_turn(t - 13, vt[:, (t - 1) % 2, :])
            pe.wait_ge(evac_done, T_GATE_A)
            v_turn(5, vt[:, 1, :])

            def dil_scores(u):
                n, j = u // 4, u % 4
                if u >= 1:
                    pe.wait_ge(logits_done, 3 * u)
                for g, (k0, nb, _) in enumerate(dil_groups(n)):
                    head = 4 * g + j
                    b = DH * (head % 2)
                    mm = pe.matmul(ps[:, 2 + g, 0:nb * P], qa[b:b + DH, head // 2, n * P:(n + 1) * P],
                                   ka[b:b + DH, head // 2, k0:k0 + nb * P], start=True, stop=True)
                mm.then_inc(scores_done, 1)

            def dil_turn(u):
                pe.wait_ge(probs_ready, u + 1)
                for g, (_, nb, col) in enumerate(dil_groups(u // 4)):
                    if 3 * u + g >= 2:
                        pe.wait_ge(pt_copied, 3 * u + g - 1)
                    for i in range(nb):
                        mm = pe.transpose(ps[:, 5 + (3 * u + g) % 2, i * P:(i + 1) * P],
                                          Lg[:, u % 2, col + i * P:col + (i + 1) * P], ident[:, :])
                    mm.then_inc(pt_psum, 1)

            def dil_pv(u):
                n, j = u // 4, u % 4
                pe.wait_ge(pt_copied, 3 * u + 3)
                if u >= 1:
                    pe.wait_ge(o_norm, u)
                if u >= 5 and u % 4 == 1:
                    pe.wait_ge(oa_ready, u // 4)
                groups = dil_groups(n)
                total = sum(g[1] for g in groups)
                done = 0
                for g, (k0, nb, col) in enumerate(groups):
                    head = 4 * g + j
                    for i in range(nb):
                        mm = pe.matmul(ps[:, 7, j * DH:(j + 1) * DH], PT[:, col // P + i, :],
                                       Vna[:, k0 // P + i, head * DH:(head + 1) * DH],
                                       start=(done == 0), stop=(done == total - 1))
                        done += 1
                mm.then_inc(pv_done, 1)

            def oa_turn(n):
                pe.wait_ge(o_norm, min(4 * n + 5, 16))
                for i in range(2):
                    mm = pe.transpose(ps[:, 7, 256 + i * P:256 + (i + 1) * P], onat[n % 2][:, i * P:(i + 1) * P], ident[:, :])
                mm.then_inc(oT_psum, 1)

            pe.wait_ge(vnat_copied, 6)
            for u in range(16 + 3):
                if u >= 7 and u % 4 == 3:
                    oa_turn(u // 4 - 1)
                if u < 16:
                    t = T_GATE_A + u // 2
                    if u % 2 == 0:
                        slab_start(t)
                    mm = products(t, t % 2, KT, Ah, Al, 0, 1, 4 * (u % 2), 4 * (u % 2) + 4)
                    if u % 2:
                        mm.then_inc(slab_done, 1)
                if 0 <= u - 2 < 16:
                    dil_pv(u - 2)
                if 0 <= u - 1 < 16:
                    dil_turn(u - 1)
                if u < 16:
                    dil_scores(u)
            oa_turn(3)

            for t in range(T_QKV_B, T_GATE_B):
                full_slab(t, Ah, Al, 0, 1)
                i = t - T_QKV_B - 9
                if i >= 0:
                    pe.wait_ge(evac_done, t)
                    v_turn(6 + i, vtb[:, i % 2, :])
            pe.wait_ge(evac_done, T_GATE_B)
            v_turn(9, vtb[:, 1, :])

            def sb_scores_mm(w):
                n, h = w // 8, w % 8
                b = DH * (h % 2)
                if w >= 2:
                    pe.wait_ge(z_done, w - 1)
                pe.matmul(ps[:, 2 + w % 2, 0:(n + 1) * P], qb[b:b + DH, h // 2, n * P:(n + 1) * P],
                          kb[b:b + DH, h // 2, 0:(n + 1) * P], start=True, stop=True).then_inc(sb_scores, 1)

            def sb_turn(w):
                pe.wait_ge(sb_probs, w + 1)
                if w >= 2:
                    pe.wait_ge(sb_pt_copied, w - 1)
                for i in range(w // 8 + 1):
                    mm = pe.transpose(ps[:, 4 + w % 2, i * P:(i + 1) * P], Cs[:, w % 2, i * P:(i + 1) * P], ident[:, :])
                mm.then_inc(sb_pt_psum, 1)

            def sb_pv_mm(w):
                n, h = w // 8, w % 8
                pe.wait_ge(sb_pt_copied, w + 1)
                if h == 0 and n >= 1:
                    pe.wait_ge(ob_nat, n)
                for i in range(n + 1):
                    mm = pe.matmul(ps[:, 6, h * DH:(h + 1) * DH], PTb[:, w % 2, i * P:(i + 1) * P],
                                   Vnb[:, i, h * DH:(h + 1) * DH], start=(i == 0), stop=(i == n))
                mm.then_inc(sb_pv, 1)

            def ob_turn(n):
                pe.wait_ge(ob_nat, n + 1)
                if n >= 1:
                    pe.wait_ge(ob_ready, n)
                for i in range(4):
                    mm = pe.transpose(ps[:, 7, i * P:(i + 1) * P], onatb[:, i * P:(i + 1) * P], ident[:, :])
                mm.then_inc(obT_psum, 1)

            pe.wait_ge(vnat_copied, 10)
            for i in range(32 + 6):
                if i < 32:
                    t = T_GATE_B + i // 4
                    if i % 4 == 0:
                        slab_start(t)
                    mm = products(t, t % 2, KT, Ah, Al, 0, 1, 2 * (i % 4), 2 * (i % 4) + 2)
                    if i % 4 == 3:
                        mm.then_inc(slab_done, 1)
                if 0 <= i - 4 < 32:
                    sb_pv_mm(i - 4)
                if 0 <= i - 3 < 32:
                    sb_turn(i - 3)
                if i < 32:
                    sb_scores_mm(i)
                if i >= 12 and (i - 12) % 8 == 0:
                    ob_turn((i - 12) // 8)

            pe.wait_ge(oa_ready, 4)
            for t in range(T_UP_A, T_UP_B):
                full_slab(t, Bh, Bl, 0, 1)
            pe.wait_ge(ob_ready, 4)
            for t in range(T_UP_B, T_OUT):
                full_slab(t, Bh, Bl, 2, 1)
            for t in range(T_OUT, T_MLP):
                full_slab(t, Ah, Al, 0, 1, split_ready(N_MERGE) if t == T_OUT else None)
            pe.wait_ge(ob_ready, 4)
            stats(1, 1)
            mlp(1)

            stats(2, 1)

            full_slab(T2, Ah, Al, 0, 2, split_ready(N2_MIX))
            stats(3, 2)

            def job(what):
                kind = what[0]
                if kind == "gate_up":
                    pe.wait_ge(evac_done, T2_LR + 1)
                    pe.wait_ge(ms_ready, 4)
                    for j in range(2):
                        for half in range(2):
                            mm = pe.matmul(ps[:, 4 + 2 * j + half, 0:HALF2], wgu[:, j * P:(j + 1) * P],
                                           lr[0:16, half * HALF2:(half + 1) * HALF2], start=True, stop=True)
                        mm.then_inc(gu_psum, 1)
                elif kind == "v_rows":
                    h = what[1]
                    beta = 64 * (h % 2)
                    pe.wait_ge(evac_done, T2_V + h + 1)
                    for g, (c0, nc_) in enumerate(((0, 4), (4, 4), (8, 1))):
                        x = 3 * h + g
                        if x >= 4:
                            pe.wait_ge(vr_copied, x - 3)
                        else:
                            pe.wait_ge(u_ready, 2)
                        for i in range(nc_):
                            c = c0 + i
                            mm = pe.matmul(ps[beta:beta + 64, 4 + x % 4, i * P:(i + 1) * P],
                                           v2[:, h, c * CH:(c + 1) * CH], ident[:, :], start=True, stop=True)
                        mm.then_inc(vr_psum, 1)
                elif kind == "unit_mm":
                    y = what[1]
                    l, j = y // 2, y % 2
                    if y >= U_START:
                        return
                    pe.wait_ge(qk_ready, y + 1)
                    if y < 2:
                        pe.wait_ge(vr_copied, 12)
                    else:
                        pe.wait_ge(sc_done, min(y - 1, U_END))
                    if y < U_END:
                        Q, K = (Qp, Kp) if l < U_DIAG // 2 else (q2, k2)
                        for c in range(NCH):
                            for hh in range(2):
                                b = 64 * hh
                                mm = pe.matmul(ps[b:b + 64, 4 + 2 * j + c // 8, (c % 8) * CH:(c % 8 + 1) * CH],
                                               K[b:b + 64, j, c * CH:(c + 1) * CH],
                                               Q[b:b + 64, j, c * CH:(c + 1) * CH], start=True, stop=True)
                        mm.then_inc(mm_done, 1)
                    else:
                        pe.wait_ge(sc_done, U_END)
                        for c in range(8):
                            for hh in range(2):
                                b = 64 * hh
                                mm = pe.matmul(ps[b:b + 64, 4 + 2 * j, c * CH:(c + 1) * CH],
                                               Kp[b:b + 64, j, c * CH:(c + 1) * CH], ident[b:b + 64, b:b + 64],
                                               start=True, stop=True)
                        mm.then_inc(kn_psum, 1)
                elif kind == "kv":
                    j = what[1]
                    pe.wait_ge(kn_copied, 2)
                    for c in range(8):
                        for hh in range(2):
                            b = 64 * hh
                            mm = pe.matmul(ps[b:b + 64, 4 + 2 * j + c // 4, (c % 4) * P:(c % 4 + 1) * P],
                                           Kn[b:b + 64, j, c * CH:(c + 1) * CH],
                                           Vn[b:b + 64, j, c * P:(c + 1) * P], start=True, stop=True)
                    mm.then_inc(kv_psum, 1)
                elif kind == "o_mm":
                    h = what[1]
                    j, b = h // 2, 64 * (h % 2)
                    if h == 0:
                        pe.wait_ge(st_done, 16)
                        pe.wait_ge(qk_ready, U_START + 2)
                    else:
                        pe.wait_ge(o_copied, h)
                    for c in range(NCH):
                        dst = ps[:, 4 + c // 8, (c % 8) * CH:(c % 8 + 1) * CH]
                        mm = pe.matmul(dst, Vn[b:b + 64, j, c * P:(c + 1) * P], sc[b:b + 64, j, c * CH:(c + 1) * CH],
                                       start=True, stop=(c == 0))
                        if c >= 1:
                            mm = pe.matmul(dst, st[b:b + 64, j, (c - 1) * P:c * P],
                                           Qs[b:b + 64, j, c * CH:(c + 1) * CH], start=False, stop=True)
                    mm.then_inc(o_psum, 1)
                elif kind == "o_norm":
                    h = what[1]
                    pe.wait_ge(o_sq, h + 1)
                    if h >= 1:
                        pe.wait_ge(o_ms, h)
                    for half in range(2):
                        mm = pe.matmul(ps[:, 6 + half, 0:HALF2], ones[:, :],
                                       osb2[:, half * HALF2:(half + 1) * HALF2], start=True, stop=True)
                    mm.then_inc(o_stat, 1)

            for t in range(T2, T2_OUT):
                if t > T2:
                    if T2_PM <= t < T2_GY:
                        g = t - T2_PM
                        full_slab(t, Bh, Bl, g, 2, lambda k: pe.wait_ge(act_ready, N2_POOL + g + 1))
                    elif T2_GY <= t < T2_R and (t - T2_GY) % 4 >= 2:
                        full_slab(t, Bh, Bl, 4, 2, split_ready(N2_PM))
                    elif T2_M <= t and (t - T2_M) % 4 >= 2:
                        full_slab(t, Bh, Bl, 0, 2, split_ready(N2_O))
                    else:
                        full_slab(t, Ah, Al, 0, 2)
                for what in between[t]:
                    job(what)
            for t in range(T2_OUT, T2_MLP):
                full_slab(t, Ah, Al, 0, 2, split_ready(N2_M) if t == T2_OUT else None)
            stats(4, 2)
            mlp(2)
            stats(5, 2)
            pe.wait_ge(y_ready, KT)
            for a in range(4):
                for half in range(2):
                    if a >= 1:
                        pe.wait_ge(y_copied, 2 * a - 1 + half)
                    for i in range(4):
                        mm = pe.transpose(ps[:, 4 + half, i * P:(i + 1) * P],
                                          Y[:, 4 * half + i, a * P:(a + 1) * P], ident[:, :])
                    mm.then_inc(y_psum, 1)


_INS = ["x", "norm_mix_g", "w_in", "b_gate", "w_up_dil", "w_up_sb", "w_out", "norm_mlp_g", "w_mlp_in",
        "w_mlp_out", "norm_final_g", "meta_tokens_2", "norm_mix_2", "w_in_2", "w_pool_mix_2", "pool_scale_2",
        "w_pool_out_2", "w_gate_up_2", "b_gate_2", "gla_norm_2", "w_gla_out_2", "w_out_2", "norm_ffn_2",
        "w_ff1_2", "w_ff2_2", "norm_final_2"]


def kernel(**inputs):
    import numpy as _np
    import concourse.bacc as _bacc
    from concourse.bass_utils import run_bass_kernel_spmd as _run

    nc = _bacc.Bacc("TRN2", target_bir_lowering=False, num_devices=1)
    arrays, aps = {}, {}
    for name in _INS:
        a = _np.ascontiguousarray(inputs[name])
        arrays[f"in_{name}"] = a
        aps[name] = nc.dram_tensor(f"in_{name}", a.shape, mybir.dt.from_np(a.dtype), kind="ExternalInput").ap()
    aps["out"] = nc.dram_tensor("out_0", (1, S1, DM), F32, kind="ExternalOutput").ap()
    build(nc, aps)
    r = _run(nc, [arrays], core_ids=[0])
    return r.results[0]["out_0"]
```

```python
from contextlib import ExitStack

import concourse.bass as bass
from concourse import mybir

F32 = mybir.dt.float32
F32R = mybir.dt.float32r
I32 = mybir.dt.int32
U32 = mybir.dt.uint32
ALU = mybir.AluOpType
ACT = mybir.ActivationFunctionType
AX_X = mybir.AxisListType.X

P = 128
DM = 1024
KT = DM // P
S1 = 512
META = 16
S2 = META + S1
ONE, ALL, REAL = 1, 2, 3
HALF2 = S2 // 2
DH = 64
DIL_W, SB_W = 768, 512
D_FF = 4 * DM
CHUNKS = D_FF // DM
NEG = -1.0e30
EPS = 1.0e-6
DILATIONS = (1, 4, 16)
SLOPES = [2.0 ** (-8.0 * (i + 1) / 12) for i in range(12)]
CH, NCH = 64, 9
PADL = NCH * CH
PAD = PADL - S2
TAU = 16.0
EXP_LN_SET = "natural_log_exp_and_others"
LEVELS = (64, 32, 16, 8, 4, 2)
WINDOWS = (2, 4, 8, 16)

G_MIX, G_MLP, G_FIN, G_MIX2, G_FFN2, G_FIN2, B_GATE, B_GATE2, POOL_SC, GLA_G, NVEC = (
    0, 8, 16, 24, 32, 40, 48, 64, 66, 70, 74)

T_QKV_A, T_GATE_A, T_QKV_B, T_GATE_B, T_UP_A, T_UP_B, T_OUT, T_MLP = 0, 18, 26, 38, 46, 54, 62, 70
T2 = T_MLP + 16 * CHUNKS
T2_K, T2_LR, T2_Q, T2_A, T2_V, T2_PM, T2_R, T2_GY = (
    T2, T2 + 2, T2 + 3, T2 + 5, T2 + 9, T2 + 13, T2 + 17, T2 + 21)
T2_GB = T2_GY + 16
T2_GO = T2_GB + 8
T2_OUT = T2_GO + 8
T2_MLP = T2_OUT + 8
T_END = T2_MLP + 16 * CHUNKS
N_MIX, N_MERGE, N_MLP, N_HID = 0, 8, 16, 24
N2_MIX = N_HID + 8 * CHUNKS
N2_POOL, N2_PM, N2_O, N2_M, N2_FFN = N2_MIX + 8, N2_MIX + 12, N2_MIX + 16, N2_MIX + 20, N2_MIX + 28
N2_HID = N2_FFN + 8


def staged(n):
    return n + 1 - sum(KT for n0 in (N_MIX, N_MLP, N2_MIX, N2_FFN) if n0 < n)


def make_loads():
    loads, t = [], 0

    def add(name, at, kt, slabs):
        nonlocal t
        loads.append((name, at, kt, slabs, t))
        t += slabs

    def wide(name, base, tiles, kt=KT):
        for i in range(0, tiles, 2):
            add(name, base + i * P, kt, 2)

    wide("w_in", 0, 18)
    wide("w_in", 3 * DIL_W + 3 * SB_W, 8)
    wide("w_in", 3 * DIL_W, 12)
    wide("w_in", 3 * DIL_W + 3 * SB_W + DM, 8)
    wide("w_up_dil", 0, 8, 2)
    wide("w_up_sb", 0, 8, 4)
    wide("w_out", 0, 8)
    assert t == T_MLP
    first_mlp = len(loads)
    for c in range(CHUNKS):
        wide("mlp_in", c * DM, 8)
        for i in range(4):
            add("mlp_out", (c, i), KT, 2)
    assert t == T2
    wide("w_in_2", 768, 2)
    add("w_in_2", 2048, KT, 1)
    wide("w_in_2", 512, 2)
    wide("w_in_2", 0, 4)
    wide("w_in_2", 1024, 4)
    add("pool_mix", 0, 1, 4)
    wide("w_in_2", 1536, 4)
    for i in range(0, 8, 2):
        add("w_in_2", 2064 + i * P, KT, 2)
        add("pool_out", i * P, 4, 2)
    wide("w_in_2", 2064 + DM, 8)
    wide("gla_out", 0, 8, 4)
    wide("w_out_2", 0, 8)
    assert t == T2_MLP
    second_mlp = len(loads)
    for c in range(CHUNKS):
        wide("mlp_in_2", c * DM, 8)
        for i in range(4):
            add("mlp_out_2", (c, i), KT, 2)
    return loads, first_mlp, second_mlp


def make_between():
    between = {t: [] for t in range(T2, T2_MLP)}
    between[T2_LR + 1] += [("gate_up",)]
    between[T2_LR + 2] += [("decay",)]
    for g in range(4):
        between[T2_A + g + 2] += [("pool_split", g)]
        between[T2_V + g + 1 + (g == 3)] += [("v_rows", g)]
    units = 2 * (len(LEVELS) + 3)
    t = T2_A
    for y in range(units + 2):
        if y < units:
            between[t] += [("unit_d", y)]
        if 0 <= y - 1 < units:
            between[t] += [("unit_qk", y - 1)]
        if 0 <= y - 2 < units:
            between[t] += [("unit_mm", y - 2)]
        t += 1
        while T2_PM <= t < T2_R:
            t += 1
    between[t] += [("kv", 0)]
    between[t + 1] += [("kv", 1)]
    t = T2_GY + 12
    assert t > T2_GY + 9
    for h in range(4):
        between[t + 2 * h] += [("o_mm", h)]
        between[t + 2 * h + 1] += [("o_stat", h)]
        between[t + 2 * h + 2] += [("o_norm", h)]
    assert t + 8 < T2_GO
    return between


def build(nc, d):
    loads, first_mlp, second_mlp = make_loads()
    between = make_between()
    slab = {}
    for p, (_, _, kt, n, t) in enumerate(loads):
        for i in range(n):
            slab[t + i] = (p, i, kt, n)

    def weight_view(name, at, kt, cols):
        if name == "pool_mix":
            return d["w_pool_mix_2"][0].rearrange("g c e -> c g e")
        if name in ("mlp_out", "mlp_out_2"):
            c, i = at
            w = d["w_mlp_out" if name == "mlp_out" else "w_ff2_2"][0]
            return w[c * DM:(c + 1) * DM, i * 256:(i + 1) * 256].rearrange("(k p) n -> p k n", p=P)
        w = d[{"w_in": "w_in", "w_up_dil": "w_up_dil", "w_up_sb": "w_up_sb", "w_out": "w_out",
               "mlp_in": "w_mlp_in", "w_in_2": "w_in_2", "pool_out": "w_pool_out_2",
               "gla_out": "w_gla_out_2", "w_out_2": "w_out_2", "mlp_in_2": "w_ff1_2"}[name]][0]
        return w[:, at:at + cols].rearrange("(k p) n -> p k n", p=P)

    ctx = ExitStack()
    with ctx:
        def sb(name, shape, dt=F32):
            return ctx.enter_context(nc.sbuf_tensor(name, shape, dt))

        def sem(name):
            return ctx.enter_context(nc.semaphore(name))

        X = sb("X", [P, KT, S2])
        Ah, Al = sb("Ah", [P, KT, S2], F32R), sb("Al", [P, KT, S2], F32R)
        Bh, Bl = sb("Bh", [P, KT, S2], F32R), sb("Bl", [P, KT, S2], F32R)
        raw = sb("raw", [P, 2, 2 * DM])
        wh, wl = sb("wh", [P, 2, DM], F32R), sb("wl", [P, 2, DM], F32R)
        F = sb("F", [P, 2, S2])
        SQ = sb("SQ", [P, 2, META + S2])
        SS, RS = sb("SS", [P, S2]), sb("RS", [P, S2])
        ident, ones = sb("ident", [P, P]), sb("ones", [P, P])
        vecT = sb("vecT", [P, NVEC])
        halfb = sb("halfb", [P, 16])
        wgu = sb("wgu", [16, 256])
        stat = sb("stat", [P, 5, 16])
        ebe = sb("ebe", [P, 2, NCH])
        masks = sb("masks", [P, 6, CH])
        AR = 19584
        arena = sb("arena", [P, AR])
        ps = ctx.enter_context(nc.psum_tensor("ps", [P, 8, 512], F32))

        def region(at, *shape):
            n = 1
            for s in shape:
                n *= s
            assert at + n <= AR, (at, shape)
            v = arena[:, at:at + n]
            if len(shape) == 2:
                v = v.rearrange("p (a b) -> p a b", a=shape[0])
            return v

        SBM = region(0, 512)
        D0, D1, D2 = region(512, 256), region(768, 512), region(1280, 512)
        qa, ka = region(1792, 6, 512), region(4864, 6, 512)
        Vna = region(7936, 4, 768)
        Lg = region(11008, 2, 1280)
        PT = region(13568, 10, 128)
        onat = [region(14848, 256), region(19200, 256)]
        vt = region(13568, 2, 512)
        GA = region(15104, 8, 512)
        qb, kb = region(1792, 4, 512), region(3840, 4, 512)
        Vnb = region(5888, 4, 512)
        GB = region(7936, 8, 512)
        Zs, Es, Cs = region(12032, 2, 512), region(13056, 2, 512), region(14080, 2, 512)
        PTb = region(512, 2, 512)
        onatb = SQ[:, 0, 0:512]
        vtb = region(512, 2, 512)
        xnat = region(1792, 4, 1024)
        mnat = region(5888, 1024)
        vrow = region(6912, 128)
        DI = arena[:, 11008:11520].bitcast(I32)
        DM4 = arena[:, 11520:12032].bitcast(I32)
        PEN = region(12032, 512)
        k2, q2 = region(0, 2, PADL), region(1152, 2, S1)
        bS = region(2176, 2, PADL)
        la = region(3328, 2, PADL)
        Kn = region(3328, 2, CH * 8)
        GB2 = region(0, 8, S1)
        Ed = region(4480, 2, S1)
        Qp, Kp = region(5504, 2, S1), region(6528, 2, S1)
        st = region(4480, 2, 8 * P)
        osb = region(6528, 2, S1)
        osb2 = region(19072, S1)
        sc = region(7552, 2, S1)
        Vn = region(8576, 2, NCH * P)
        Qs = region(10880, 2, S1)
        sr = region(11904, 4, S1)
        apad = region(11904, 2, S2)
        G2 = region(13952, 2, S1)
        reset = region(13952, PADL)
        UU = region(14976, 2, S2)
        E2 = region(16032, S2)
        lr = region(16560, S2)
        v2 = region(17088, 4, PADL)
        ma = region(14976, 8, S1)
        wsum = SQ
        Y = region(0, 8, S1)
        ON = region(4096, 4, DM)

        params_in, x_in = sem("params_in"), sem("x_in")
        w_landed = [sem("w_landed0"), sem("w_landed1")]
        hi_ready, lo_ready = sem("hi_ready"), sem("lo_ready")
        slab_done, evac_done = sem("slab_done"), sem("evac_done")
        f_ready, hi_split, act_ready = sem("f_ready"), sem("hi_split"), sem("act_ready")
        sq_ready, ss_done = sem("sq_ready"), sem("ss_done")
        stat_done, ms_ready, sqrt_ready, rstd_ready = (
            sem("stat_done"), sem("ms_ready"), sem("sqrt_ready"), sem("rstd_ready"))
        consts_ready, pool_step = sem("consts_ready"), sem("pool_step")
        di_ready, dist_step, dist_raw = sem("di_ready"), sem("dist_step"), sem("dist_raw")
        bias_ready = sem("bias_ready")
        vec_psum, vec_ready, halfb_ready = sem("vec_psum"), sem("vec_ready"), sem("halfb_ready")
        xt_psum, xt_copied, meta_psum, meta_copied = (
            sem("xt_psum"), sem("xt_copied"), sem("meta_psum"), sem("meta_copied"))
        vtrans_done, vnat_copied = sem("vtrans_done"), sem("vnat_copied")
        gate_done = sem("gate_done")
        scores_done, logits_done, max_done, negmax_ready, probs_ready = (
            sem("scores_done"), sem("logits_done"), sem("max_done"), sem("negmax_ready"), sem("probs_ready"))
        pt_psum, pt_copied, pv_done, rden_done, o_norm = (
            sem("pt_psum"), sem("pt_copied"), sem("pv_done"), sem("rden_done"), sem("o_norm"))
        oT_psum, oa_hi, oa_ready = sem("oT_psum"), sem("oa_hi"), sem("oa_ready")
        sb_scores, z_done, sb_abs, sb_exp, sb_ln = (
            sem("sb_scores"), sem("z_done"), sem("sb_abs"), sem("sb_exp"), sem("sb_ln"))
        sb_sp, sb_scan, sb_la, sb_probs = sem("sb_sp"), sem("sb_scan"), sem("sb_la"), sem("sb_probs")
        sb_pt_psum, sb_pt_copied, sb_pv = sem("sb_pt_psum"), sem("sb_pt_copied"), sem("sb_pv")
        ob_nat, obT_psum, ob_hi, ob_ready = sem("ob_nat"), sem("obT_psum"), sem("ob_hi"), sem("ob_ready")
        x_normed = sem("x_normed")
        zeros2_ready = sem("zeros2_ready")
        gu_psum, u_ready, u_abs, u_exp, u_ln, la_ready, bs_ready, ebe_ready = (
            sem("gu_psum"), sem("u_ready"), sem("u_abs"), sem("u_exp"), sem("u_ln"), sem("la_ready"),
            sem("bs_ready"), sem("ebe_ready"))
        vr_psum, vr_copied = sem("vr_psum"), sem("vr_copied")
        d_ready, d_abs, d_exp, qk_ready, mm_done, sc_done = (
            sem("d_ready"), sem("d_abs"), sem("d_exp"), sem("qk_ready"), sem("mm_done"), sem("sc_done"))
        kn_psum, kn_copied, kv_psum, st_done = sem("kn_psum"), sem("kn_copied"), sem("kv_psum"), sem("st_done")
        o_psum, o_copied, o_sq, o_stat, o_ms, o_sqrt, o_rstd, o_scaled = (
            sem("o_psum"), sem("o_copied"), sem("o_sq"), sem("o_stat"), sem("o_ms"), sem("o_sqrt"),
            sem("o_rstd"), sem("o_scaled"))
        win_done = sem("win_done")
        silu_tanh, silu_done = sem("silu_tanh"), sem("silu_done")
        y_ready, y_psum, y_copied, out_done = sem("y_ready"), sem("y_psum"), sem("y_copied"), sem("out_done")

        def dense_psum(t, kind):
            if kind == ONE:
                return ps[:, t % 2, :]
            if kind == REAL:
                return ps[:, 2 * (t % 2), :]
            return ps[:, 2 * (t % 2):2 * (t % 2) + 2, 0:HALF2]

        def tokens(ap, kind):
            return ap.rearrange("p (a b) -> p a b", a=2) if kind == ALL else ap

        def flat(bank):
            return ps[:, bank:bank + 2, :].rearrange("p a b -> p (a b)")

        def width(kind):
            return S2 if kind == ALL else S1

        def raw_half(p_slot, half, kt, n):
            return raw[:, p_slot, 0:kt * n * P].rearrange("p (k n) -> p k n", k=kt)[
                :, :, half * P:(half + 1) * P]

        def raw_slab(t):
            p, half, kt, n = slab[t]
            if loads[p][0] == "pool_mix":
                return raw[:, p % 2, 0:512].rearrange("p (k n) -> p k n", k=4)[:, half:half + 1, :]
            return raw_half(p % 2, half, kt, n)

        def w_slab(w, slot, kt):
            return w[:, slot, 0:kt * P].rearrange("p (k n) -> p k n", k=kt)

        def dil_groups(n):
            nb0 = 1 if n == 0 else 2
            return [(P * (n + 1 - nb0), nb0, 0), (0, n + 1, nb0 * P), (0, n + 1, (nb0 + n + 1) * P)]

        def level_ref(y):
            l, j = y // 2, y % 2
            c0 = 1 if l < len(LEVELS) else 0
            b = LEVELS[l] if l < len(LEVELS) else CH
            at = b // 2 - 1 if l < len(LEVELS) else CH - 1
            v = bS[:, j, c0 * CH:(c0 + 8) * CH].rearrange("p (a b) -> p a b", b=b)
            return v, v[:, :, at:at + 1].to_broadcast([P, S1 // b, b]), b

        U_DIAG, U_END, U_START = 2 * len(LEVELS), 2 * len(LEVELS) + 2, 2 * len(LEVELS) + 4
        def exp_no(y):
            return y if y < U_DIAG else y - 2
        MLPS = {ONE: (T_MLP, N_HID, first_mlp), REAL: (T2_MLP, N2_HID, second_mlp)}

        block = ctx.enter_context(nc.Block())

        @block.sync
        def _(sp):
            sp.dma_start(xnat, d["x"][0].rearrange("(a p) d -> p a d", p=P)).then_inc(x_in, 16)
            row = 0
            for name, n in (("norm_mix_g", 8), ("norm_mlp_g", 8), ("norm_final_g", 8), ("norm_mix_2", 8),
                            ("norm_ffn_2", 8), ("norm_final_2", 8), ("b_gate", 16), ("b_gate_2", 2),
                            ("pool_scale_2", 4), ("gla_norm_2", 4)):
                v = d[name] if len(d[name].shape) == 1 else d[name][0]
                sp.dma_start(vrow[row:row + n, :], v.rearrange("(a b) -> a b", b=P)).then_inc(params_in, 16)
                row += n
            sp.dma_start(mnat[0:META, :], d["meta_tokens_2"]).then_inc(params_in, 16)
            sp.dma_start(wgu[:, :], d["w_gate_up_2"][0]).then_inc(params_in, 16)

            def load(p):
                name, at, kt, n, t = loads[p]
                if p >= 2:
                    sp.wait_ge(lo_ready, loads[p - 2][4] + loads[p - 2][3])
                view = weight_view(name, at, kt, n * P)
                k = 4 if name == "pool_mix" else kt
                sp.dma_start(raw[:, p % 2, 0:kt * n * P].rearrange("p (k n) -> p k n", k=k), view)\
                  .then_inc(w_landed[p % 2], 16)

            def mlp_loads(which, w1, w2):
                t0, _, p0 = MLPS[which]
                with sp.Fori(0, CHUNKS - 1) as c:
                    for i in range(8):
                        sp.wait_ge(lo_ready, t0 + 16 * c + 2 * i - 2)
                        if i < 4:
                            src = w1[:, bass.ds(c * DM + i * 256, 256)]
                        else:
                            src = w2[bass.ds(c * DM, DM), (i - 4) * 256:(i - 3) * 256]
                        sp.dma_start(raw[:, (p0 + i) % 2, :].rearrange("p (k n) -> p k n", k=KT),
                                     src.rearrange("(k p) n -> p k n", p=P))\
                          .then_inc(w_landed[(p0 + i) % 2], 16)

            for p in range(first_mlp):
                load(p)
            mlp_loads(ONE, d["w_mlp_in"][0], d["w_mlp_out"][0])
            for p in range(first_mlp + 8 * (CHUNKS - 1), second_mlp):
                load(p)
            mlp_loads(REAL, d["w_ff1_2"][0], d["w_ff2_2"][0])
            for p in range(second_mlp + 8 * (CHUNKS - 1), len(loads)):
                load(p)
            for a in range(4):
                sp.wait_ge(y_copied, 2 * a + 2)
                sp.dma_start(d["out"][0, a * P:(a + 1) * P, :], ON[:, a, :]).then_inc(out_done, 16)
            sp.wait_ge(out_done, 64)

        @block.gpsimd
        def _(pool):
            step = 0

            def after(ins):
                nonlocal step
                step += 1
                ins.then_inc(pool_step, 1)
                pool.wait_ge(pool_step, step)

            after(pool.memset(ident[:, :], 0.0))
            pool.memset(ones[:, :], 1.0).then_inc(consts_ready, 1)
            pool.affine_select(out=ident[:, :], in_=ident[:, :], compare_op=ALU.not_equal, fill=1.0, base=0,
                               pattern=[[-1, P]], channel_multiplier=1).then_inc(consts_ready, 1)
            pool.iota(DI, pattern=[[-1, 512]], base=384, channel_multiplier=1).then_inc(di_ready, 1)
            after(pool.memset(SBM, 0.0))
            pool.affine_select(out=SBM, in_=SBM, compare_op=ALU.is_gt, fill=NEG, base=384,
                               pattern=[[-1, 512]], channel_multiplier=1).then_inc(bias_ready, 1)
            pool.wait_ge(dist_raw, 3)
            for dist, base, n in ((D1, 384, 512), (D2, 384, 512)):
                pool.affine_select(out=dist, in_=dist, compare_op=ALU.is_ge, fill=NEG, base=base,
                                   pattern=[[-1, n]], channel_multiplier=1).then_inc(bias_ready, 1)
            after(pool.affine_select(out=D0, in_=D0, compare_op=ALU.is_ge, fill=NEG, base=128,
                                     pattern=[[-1, 256]], channel_multiplier=1))
            pool.affine_select(out=D0, in_=D0, compare_op=ALU.is_ge, fill=NEG, base=0,
                               pattern=[[1, 256]], channel_multiplier=-1).then_inc(bias_ready, 1)
            after(pool.memset(masks[:, :, :], 1.0))
            for i, b in enumerate((32, 16, 8, 4, 2, 1)):
                for h in range(2):
                    v = masks[64 * h:64 * h + 64, i, :].rearrange("p (a b) -> p a b", b=b)
                    after(pool.affine_select(out=v, in_=v, compare_op=ALU.is_ge, fill=0.0, base=0,
                                             pattern=[[-b, CH // b], [0, b]], channel_multiplier=1))
                    after(pool.affine_select(out=v, in_=v, compare_op=ALU.is_ge, fill=0.0, base=b - 1,
                                             pattern=[[b, CH // b], [0, b]], channel_multiplier=-1))

            def add_squares(norm, kind):
                w = width(kind)
                if norm >= 1:
                    pool.wait_ge(stat_done, norm)
                for m in range(KT - 1):
                    f = 8 * norm + m
                    pool.wait_ge(sq_ready, f + 1)
                    if m == 0:
                        pool.tensor_copy(SS[:, 0:w], SQ[:, f % 2, 0:w]).then_inc(ss_done, 1)
                    else:
                        pool.wait_ge(ss_done, f)
                        pool.tensor_tensor(SS[:, 0:w], SS[:, 0:w], SQ[:, f % 2, 0:w], ALU.add).then_inc(ss_done, 1)

            add_squares(0, ONE)
            add_squares(1, ONE)
            pool.wait_ge(act_ready, N_MERGE + 8)
            pool.memset(k2[:, :, 0:PAD], 0.0)
            pool.memset(la[:, :, 0:PAD], 0.0)
            pool.memset(v2[:, :, 0:PAD], 0.0)
            after(pool.memset(reset, 1.0))
            pool.memset(reset.rearrange("p (a b) -> p a b", b=CH)[:, :, 0:1], 0.0).then_inc(zeros2_ready, 1)
            add_squares(2, ONE)
            add_squares(3, ALL)
            done = 0
            for g in range(4):
                pool.wait_ge(evac_done, T2_A + g + 1)
                if g >= 1:
                    pool.wait_ge(f_ready, staged(N2_POOL + g - 1))
                else:
                    pool.wait_ge(ss_done, 32)
                cur = apad[:, g % 2, :]
                for k in range(g + 1):
                    s = 2 ** k
                    nxt = wsum[:, k % 2, 0:S2]
                    lo = 2 * s - 1 if k < g else META
                    pool.tensor_tensor(nxt[:, lo:], cur[:, lo:], cur[:, lo - s:S2 - s], ALU.add)\
                        .then_inc(win_done, 1)
                    done += 1
                    pool.wait_ge(win_done, done)
                    cur = nxt
            add_squares(4, REAL)
            add_squares(5, REAL)

        @block.scalar
        def _(act):
            def convert(t):
                if t >= T_END:
                    return
                p, half, kt, n = slab[t]
                if half == 0:
                    act.wait_ge(w_landed[p % 2], 16 * (p // 2 + 1))
                if t >= 2:
                    act.wait_ge(slab_done, t - 1)
                act.activation(w_slab(wh, t % 2, kt), raw_slab(t), ACT.Copy).then_inc(hi_ready, 1)

            def split(n, dst, src):
                act.wait_ge(f_ready, staged(n))
                act.activation(dst, src, ACT.Copy).then_inc(hi_split, 1)

            def square(norm, m, kind):
                f = 8 * norm + m
                if f >= 2:
                    act.wait_ge(ss_done, f - 1)
                src = X[:, m, S2 - width(kind):S2]
                act.activation(SQ[:, f % 2, 0:width(kind)], src, ACT.Square).then_inc(sq_ready, 1)

            def feed(norm, n, m, col, kind, dst=None, ready=None):
                if ready is not None:
                    ready()
                act.activation((Ah if dst is None else dst)[:, m, 0:width(kind)], X[:, m, S2 - width(kind):S2],
                               ACT.Copy, scale=vecT[:, col + m:col + m + 1]).then_inc(hi_split, 1)
                square(norm, m, kind)

            def stats(norm, kind):
                act.wait_ge(ms_ready, norm + 1)
                act.activation(RS[:, 0:width(kind)], RS[:, 0:width(kind)], ACT.Sqrt).then_inc(sqrt_ready, 1)

            def gate(t, g, col=None):
                act.wait_ge(evac_done, t + 1)
                act.activation(g, g, ACT.Tanh, bias=halfb[:, col:col + 1] if col is not None else 0.0,
                               scale=0.5).then_inc(gate_done, 1)

            def mlp_chunk(which, c, last):
                t0, n0, p0 = MLPS[which]
                w = width(which)
                for j in range(16):
                    t = t0 + j
                    if not (last and j == 15 and which == REAL):
                        i = (j + 1) // 2
                        if j % 2:
                            act.wait_ge(w_landed[(p0 + i) % 2], (p0 + i) // 2 * 16 + 16 + 64 * c)
                        act.wait_ge(slab_done, t + 16 * c)
                        if last and j == 15:
                            p, half, kt, n = slab[T2]
                            src = raw_half(p % 2, half, kt, n)
                        else:
                            src = raw_half((p0 + i) % 2, (j + 1) % 2, KT, 2)
                        act.activation(w_slab(wh, (t + 1) % 2, KT), src, ACT.Copy).then_inc(hi_ready, 1)
                    if j < 8:
                        act.wait_ge(f_ready, staged(n0) + 8 * c + j)
                        act.activation(Ah[:, j, 0:w], F[:, (n0 + j) % 2, 0:w], ACT.Copy).then_inc(hi_split, 1)
                    elif last:
                        act.wait_ge(evac_done, t + 16 * c + 1)
                        square(2 if which == ONE else 5, j - 8, which)

            def mlp(which):
                with act.Fori(0, CHUNKS - 1) as c:
                    mlp_chunk(which, c, False)
                mlp_chunk(which, CHUNKS - 1, True)

            act.wait_ge(vec_ready, 1)
            act.activation(halfb[:, :], vecT[:, B_GATE:B_GATE + 16], ACT.Copy, scale=0.5).then_inc(halfb_ready, 1)
            convert(0)
            for m in range(KT):
                feed(0, N_MIX + m, m, G_MIX, ONE, ready=lambda: act.wait_ge(xt_copied, m + 1))
            act.wait_ge(halfb_ready, 1)

            def v_copy(i, dst):
                act.wait_ge(vtrans_done, i + 1)
                act.activation(dst, ps[:, 6 + i % 2, :].rearrange("p (a b) -> p a b", a=4), ACT.Copy)\
                   .then_inc(vnat_copied, 1)

            for t in range(T_QKV_A, T_GATE_A):
                convert(t + 1)
                if t == 0:
                    stats(0, ONE)
                if t >= T_QKV_A + 14:
                    v_copy(t - 14, Vna[:, :, (t - 14) * P:(t - 13) * P])
            for i in (4, 5):
                v_copy(i, Vna[:, :, i * P:(i + 1) * P])

            def dil_exp(u):
                ncol = sum(g[1] for g in dil_groups(u // 4)) * P
                act.wait_ge(negmax_ready, u + 1)
                act.activation(Lg[:, u % 2, 0:ncol], Lg[:, u % 2, 0:ncol], ACT.Exp, bias=stat[:, 1, u:u + 1],
                               scale=0.125, accum_out=stat[:, 2, u:u + 1]).then_inc(probs_ready, 1)

            def dil_copy(u):
                if u >= 1:
                    act.wait_ge(pv_done, u)
                for g, (_, nb, col) in enumerate(dil_groups(u // 4)):
                    act.wait_ge(pt_psum, 3 * u + g + 1)
                    act.activation(PT[:, col // P:col // P + nb, :],
                                   ps[:, 5 + (3 * u + g) % 2, 0:nb * P].rearrange("p (a b) -> p a b", a=nb), ACT.Copy)\
                       .then_inc(pt_copied, 1)

            def oa_hi_copy(n):
                act.wait_ge(oT_psum, n + 1)
                act.activation(Bh[:, 0:2, n * P:(n + 1) * P],
                               ps[:, 7, 256:512].rearrange("p (a b) -> p a b", a=2), ACT.Copy).then_inc(oa_hi, 1)

            for u in range(16 + 3):
                if u % 2 == 0 and u < 16:
                    s = u // 2
                    convert(T_GATE_A + s + 1)
                if 0 <= u - 2 < 16:
                    dil_copy(u - 2)
                if u >= 7 and u % 4 == 3:
                    oa_hi_copy(u // 4 - 1)
                if 0 <= u - 1 < 16:
                    dil_exp(u - 1)
                if u % 2 == 0 and 2 <= u < 16:
                    s = u // 2
                    gate(T_GATE_A + s - 1, GA[:, s - 1, :], s - 1)
            gate(T_GATE_A + 7, GA[:, 7, :], 7)
            oa_hi_copy(3)

            for t in range(T_QKV_B, T_GATE_B):
                convert(t + 1)
                i = t - T_QKV_B - 8 - 2
                if i >= 0:
                    v_copy(6 + i, Vnb[:, :, i * P:(i + 1) * P])
            for i in (2, 3):
                v_copy(6 + i, Vnb[:, :, i * P:(i + 1) * P])

            def sb_ln_chain(w):
                e = Es[:, w % 2, 0:P * (w // 8 + 1)]
                act.wait_ge(z_done, w + 1)
                if w >= 2:
                    act.wait_ge(sb_scan, w - 1)
                act.activation(e, Zs[:, w % 2, 0:P * (w // 8 + 1)], ACT.Abs).then_inc(sb_abs, 1)
                act.wait_ge(sb_abs, w + 1)
                act.activation(e, e, ACT.Exp, scale=-1.0).then_inc(sb_exp, 1)
                act.wait_ge(sb_exp, w + 1)
                act.activation(e, e, ACT.Ln, bias=1.0).then_inc(sb_ln, 1)

            def sb_prob(w):
                act.wait_ge(sb_la, w + 1)
                c = Cs[:, w % 2, 0:P * (w // 8 + 1)]
                act.activation(c, c, ACT.Exp).then_inc(sb_probs, 1)

            def sb_copy(w):
                act.wait_ge(sb_pt_psum, w + 1)
                if w >= 2:
                    act.wait_ge(sb_pv, w - 1)
                nk = P * (w // 8 + 1)
                act.activation(PTb[:, w % 2, 0:nk], ps[:, 4 + w % 2, 0:nk], ACT.Copy).then_inc(sb_pt_copied, 1)

            def sb_out(n):
                act.wait_ge(sb_pv, 8 * n + 8)
                if n >= 1:
                    act.wait_ge(obT_psum, n)
                act.activation(onatb, ps[:, 6, :], ACT.Copy).then_inc(ob_nat, 1)

            def ob_hi_copy(n):
                act.wait_ge(obT_psum, n + 1)
                act.activation(Bh[:, 2:6, n * P:(n + 1) * P],
                               ps[:, 7, :].rearrange("p (a b) -> p a b", a=4), ACT.Copy).then_inc(ob_hi, 1)

            act.preload_act_table_set(EXP_LN_SET)
            for i in range(32 + 6):
                if i % 4 == 0 and i < 32:
                    convert(T_GATE_B + i // 4 + 1)
                if 0 <= i - 4 < 32:
                    sb_copy(i - 4)
                if 0 <= i - 1 < 32:
                    sb_ln_chain(i - 1)
                if 0 <= i - 2 < 32:
                    sb_prob(i - 2)
                if i >= 12 and (i - 12) % 8 == 0:
                    sb_out((i - 12) // 8)
                if i >= 13 and (i - 13) % 8 == 0:
                    ob_hi_copy((i - 13) // 8)

            for m in range(KT):
                convert(T_UP_A + m + 1)
                gate(T_GATE_B + m, GB[:, m, :], 8 + m)
            for m in range(KT):
                convert(T_UP_B + m + 1)
                split(N_MERGE + m, Ah[:, m, 0:S1], F[:, (N_MERGE + m) % 2, 0:S1])
            for m in range(KT):
                convert(T_OUT + m + 1)
                feed(1, N_MLP + m, m, G_MLP, ONE, Bh, lambda: act.wait_ge(evac_done, T_OUT + m + 1))
            stats(1, ONE)
            mlp(ONE)

            stats(2, ONE)
            for m in range(KT):
                feed(3, N2_MIX + m, m, G_MIX2, ALL, ready=lambda: act.wait_ge(x_normed, m + 1))

            def decay_exp():
                act.preload_act_table_set(EXP_LN_SET)
                for j in range(2):
                    u, e = UU[:, j, :], E2
                    act.wait_ge(u_ready, j + 1)
                    if j == 1:
                        act.wait_ge(la_ready, 1)
                    act.activation(e, u, ACT.Abs).then_inc(u_abs, 1)
                    act.wait_ge(u_abs, j + 1)
                    act.activation(e, e, ACT.Exp, scale=-1.0).then_inc(u_exp, 1)
                    act.wait_ge(u_exp, j + 1)
                    act.activation(e, e, ACT.Ln, bias=1.0).then_inc(u_ln, 1)
                for j in range(2):
                    act.wait_ge(bs_ready, j + 1)
                    act.activation(ebe[:, j, :], bS[:, j, CH - 1:PADL:CH], ACT.Exp, scale=1.0 / TAU)\
                       .then_inc(ebe_ready, 1)

            def job(what):
                kind = what[0]
                if kind == "decay":
                    decay_exp()
                elif kind == "v_rows":
                    h = what[1]
                    for g, (c0, nc_) in enumerate(((0, 4), (4, 4), (8, 1))):
                        act.wait_ge(vr_psum, 3 * h + g + 1)
                        beta = 64 * (h % 2)
                        act.activation(Vn[beta:beta + 64, h // 2, c0 * P:(c0 + nc_) * P],
                                       ps[beta:beta + 64, 5 + 2 * ((3 * h + g) % 2), 0:nc_ * P], ACT.Copy)\
                           .then_inc(vr_copied, 1)
                elif kind == "unit_d":
                    y = what[1]
                    l, j = y // 2, y % 2
                    if l == U_DIAG // 2:
                        return
                    x = exp_no(y)
                    e = Ed[:, x % 2, :]
                    if y < U_START:
                        act.wait_ge(d_ready, x + 1)
                        act.activation(e, e, ACT.Abs).then_inc(d_abs, 1)
                        act.wait_ge(d_abs, x + 1)
                        act.activation(e, e, ACT.Exp, scale=-1.0 / TAU).then_inc(d_exp, 1)
                    else:
                        act.wait_ge(qk_ready, y - 2 + 1)
                        act.activation(e, bS[:, j, CH:], ACT.Exp, scale=1.0 / TAU).then_inc(d_exp, 1)
                elif kind == "unit_mm":
                    y = what[1]
                    if U_END <= y < U_START:
                        j = y - U_END
                        act.wait_ge(kn_psum, j + 1)
                        act.activation(Kn[:, j, :], ps[:, 4 + 2 * j, :], ACT.Copy).then_inc(kn_copied, 1)
                elif kind == "o_mm":
                    h = what[1]
                    act.wait_ge(o_copied, h + 1)
                    if h >= 1:
                        act.wait_ge(o_stat, h)
                    act.activation(osb2, osb[:, h % 2, :], ACT.Square).then_inc(o_sq, 1)
                elif kind == "o_stat":
                    h = what[1]
                    act.wait_ge(o_ms, h + 1)
                    act.activation(SQ[:, h % 2, 0:S1], SQ[:, h % 2, 0:S1], ACT.Sqrt).then_inc(o_sqrt, 1)
                elif kind == "o_norm":
                    h = what[1]
                    n = N2_O + h
                    split(n, Bh[:, h, 0:S1], F[:, n % 2, 0:S1])
                elif kind == "pool_split":
                    g = what[1]
                    n = N2_POOL + g
                    split(n, Bh[:, g, 0:S1], F[:, n % 2, 0:S1])

            def evac(t):
                if T2_PM <= t < T2_R:
                    n = N2_PM + t - T2_PM
                    split(n, Bh[:, 4 + t - T2_PM, 0:S1], F[:, n % 2, 0:S1])
                elif T2_R <= t < T2_GY:
                    i = t - T2_R
                    act.wait_ge(evac_done, t + 1)
                    if i >= 2:
                        act.wait_ge(silu_done, i - 1)
                    act.activation(G2[:, i % 2, :], sr[:, i, :], ACT.Tanh, scale=0.5).then_inc(silu_tanh, 1)
                elif T2_GY <= t < T2_GB and (t - T2_GY) % 4 < 2:
                    gate(t, G2[:, (t - T2_GY) % 2, :])
                elif T2_GB <= t < T2_GO:
                    gate(t, GB2[:, t - T2_GB, :])
                elif T2_GO <= t < T2_OUT:
                    n = N2_M + t - T2_GO
                    if t == T2_GO:
                        act.wait_ge(slab_done, T2_GO)
                    split(n, Ah[:, t - T2_GO, 0:S1], F[:, n % 2, 0:S1])

            for t in range(T2, T2_OUT):
                convert(t + 1)
                if t == T2:
                    stats(3, ALL)
                if t > T2:
                    evac(t - 1)
                for what in between[t]:
                    job(what)
            evac(T2_OUT - 1)
            for m in range(KT):
                convert(T2_OUT + m + 1)
                feed(4, N2_FFN + m, m, G_FFN2, REAL, Bh, lambda: act.wait_ge(evac_done, T2_OUT + m + 1))
            stats(4, REAL)
            mlp(REAL)
            stats(5, REAL)
            for a in range(4):
                act.wait_ge(y_psum, 2 * a + 1)
                act.activation(ON[:, a, 0:512], ps[:, 4, :], ACT.Copy).then_inc(y_copied, 1)
                act.wait_ge(y_psum, 2 * a + 2)
                act.activation(ON[:, a, 512:1024], ps[:, 5, :], ACT.Copy).then_inc(y_copied, 1)

        @block.vector
        def _(dve):
            def convert(t):
                if t >= T_END:
                    return
                kt = slab[t][2]
                dve.wait_ge(hi_ready, t + 1)
                dve.tensor_tensor(w_slab(wl, t % 2, kt), raw_slab(t), w_slab(wh, t % 2, kt), ALU.subtract)\
                   .then_inc(lo_ready, 1)

            def split(n, lo, src, hi):
                dve.wait_ge(hi_split, n + 1)
                dve.tensor_tensor(lo, src, hi, ALU.subtract).then_inc(act_ready, 1)

            def add_square(norm, m, kind):
                w = width(kind)
                f = 8 * norm + m
                dve.wait_ge(sq_ready, f + 1)
                dve.wait_ge(ss_done, f)
                dve.tensor_tensor(SS[:, 0:w], SS[:, 0:w], SQ[:, f % 2, 0:w], ALU.add).then_inc(ss_done, 1)

            def feed(norm, n, m, col, kind, hi=None, lo=None):
                w = width(kind)
                hi, lo = (Ah, Al) if hi is None else (hi, lo)
                dve.wait_ge(hi_split, n + 1)
                dve.scalar_tensor_tensor(out=lo[:, m, 0:w], in0=X[:, m, S2 - w:S2], scalar=vecT[:, col + m:col + m + 1],
                                         in1=hi[:, m, 0:w], op0=ALU.mult, op1=ALU.subtract).then_inc(act_ready, 1)
                if m == KT - 1:
                    add_square(norm, m, kind)

            def stats(norm, kind):
                w = width(kind)
                dve.wait_ge(stat_done, norm + 1)
                src = ps[:, 6:8, 0:HALF2] if kind == ALL else ps[:, 7, :]
                dve.tensor_scalar(tokens(RS[:, 0:w], kind), src, 1.0 / DM, EPS, ALU.mult, ALU.add)\
                   .then_inc(ms_ready, 1)
                dve.wait_ge(sqrt_ready, norm + 1)
                dve.reciprocal(RS[:, 0:w], RS[:, 0:w]).then_inc(rstd_ready, 1)
                dve.wait_ge(rstd_ready, norm + 1)

            def scaled(t, dst, kind, rows=P):
                scale = RS[0:rows, META:S2] if kind == REAL else RS[0:rows, 0:width(kind)]
                dve.wait_ge(slab_done, t + 1)
                dve.tensor_tensor(tokens(dst, kind), dense_psum(t, kind)[0:rows], tokens(scale, kind), ALU.mult)\
                   .then_inc(evac_done, 1)

            def gated(t, no, g, dst, kind):
                dve.wait_ge(slab_done, t + 1)
                dve.wait_ge(gate_done, no + 1)
                dve.scalar_tensor_tensor(out=dst, in0=g, scalar=1.0, in1=dense_psum(t, kind),
                                         op0=ALU.add, op1=ALU.mult).then_inc(evac_done, 1)

            def add_half(t, m, kind):
                dve.wait_ge(slab_done, t + 1)
                x = X[:, m, META:S2]
                dve.scalar_tensor_tensor(out=x, in0=dense_psum(t, kind), scalar=0.5, in1=x,
                                         op0=ALU.mult, op1=ALU.add).then_inc(evac_done, 1)

            def add_residual(t, ps_t, m, kind):
                dve.wait_ge(slab_done, t + 1)
                dve.tensor_tensor(X[:, m, META:S2], X[:, m, META:S2], dense_psum(ps_t, kind), ALU.add)\
                   .then_inc(evac_done, 1)

            def mlp_chunk(which, c, last):
                t0, n0, p0 = MLPS[which]
                w = width(which)
                for j in range(16):
                    t = t0 + j
                    if not (last and j == 15 and which == REAL):
                        if last and j == 15:
                            p, half, kt, n = slab[T2]
                            src = raw_half(p % 2, half, kt, n)
                        else:
                            src = raw_half((p0 + (j + 1) // 2) % 2, (j + 1) % 2, KT, 2)
                        dve.wait_ge(hi_ready, t + 16 * c + 2)
                        dve.tensor_tensor(w_slab(wl, (t + 1) % 2, KT), src, w_slab(wh, (t + 1) % 2, KT),
                                          ALU.subtract).then_inc(lo_ready, 1)
                    if j < 8:
                        f = F[:, (n0 + j) % 2, 0:w]
                        dve.wait_ge(slab_done, t + 16 * c + 1)
                        dve.tensor_tensor(f, dense_psum(t, which), RS[:, 0:w], ALU.mult).then_inc(evac_done, 1)
                        dve.wait_ge(evac_done, t + 16 * c + 1)
                        dve.scalar_tensor_tensor(out=f, in0=f, scalar=0.0, in1=f, op0=ALU.max, op1=ALU.mult)\
                           .then_inc(f_ready, 1)
                        dve.wait_ge(hi_split, n0 + 8 * c + (j + 1))
                        dve.tensor_tensor(Al[:, j, 0:w], f, Ah[:, j, 0:w], ALU.subtract).then_inc(act_ready, 1)
                    else:
                        add_residual(t + 16 * c, t, j - 8, which)
                        if last and j == 15:
                            add_square(2 if which == ONE else 5, KT - 1, which)

            def mlp(which):
                with dve.Fori(0, CHUNKS - 1) as c:
                    mlp_chunk(which, c, False)
                mlp_chunk(which, CHUNKS - 1, True)

            dve.wait_ge(di_ready, 1)
            for i, (dist, dil) in enumerate(((D1, 4), (D2, 16))):
                dve.tensor_scalar(DM4, DI, dil - 1, None, ALU.bitwise_and).then_inc(dist_step, 1)
                dve.wait_ge(dist_step, 2 * i + 1)
                dve.tensor_scalar(PEN, DM4, 0.0, NEG, ALU.is_gt, ALU.mult).then_inc(dist_step, 1)
                dve.wait_ge(dist_step, 2 * i + 2)
                dve.scalar_tensor_tensor(out=dist, in0=DI, scalar=-1.0, in1=PEN, op0=ALU.mult, op1=ALU.add)\
                   .then_inc(dist_raw, 1)
                dve.wait_ge(dist_raw, i + 1)
            dve.tensor_scalar(D0, DI[:, 256:512], -1.0, None, ALU.mult).then_inc(dist_raw, 1)
            dve.wait_ge(vec_psum, 1)
            dve.tensor_copy(vecT[:, :], ps[:, 5, 0:NVEC]).then_inc(vec_ready, 1)
            dve.wait_ge(meta_psum, 1)
            dve.tensor_copy(X[:, :, 0:META], ps[:, 4, 0:KT * META].rearrange("p (a b) -> p a b", a=KT))\
               .then_inc(meta_copied, 1)
            dve.wait_ge(vec_ready, 1)
            for m in range(KT):
                dve.wait_ge(xt_psum, m + 1)
                dve.tensor_copy(X[:, m, META:S2], ps[:, 2 + m % 2, :]).then_inc(xt_copied, 1)
                dve.wait_ge(xt_copied, m + 1)
                if m == 0:
                    convert(0)
                feed(0, N_MIX + m, m, G_MIX, ONE)

            for t in range(T_QKV_A, T_GATE_A + 1):
                if t == T_QKV_A + 1:
                    stats(0, ONE)
                if t > T_QKV_A:
                    i = t - 1
                    if i >= 14:
                        dve.wait_ge(vtrans_done, i - 13)
                    scaled(i, qa[:, i, :] if i < 6 else ka[:, i - 6, :] if i < 12 else vt[:, i % 2, :], 1)
                if t < T_GATE_A:
                    convert(t + 1)

            def dil_softmax(u):
                n, j = u // 4, u % 4
                groups = dil_groups(n)
                dve.wait_ge(scores_done, u + 1)
                if u >= 2:
                    dve.wait_ge(pt_psum, 3 * (u - 1))
                for g, (k0, nb, col) in enumerate(groups):
                    dist = (D0, D1, D2)[g]
                    w = nb * P
                    dve.scalar_tensor_tensor(out=Lg[:, u % 2, col:col + w], in0=dist[:, dist.shape[1] - w:],
                                             scalar=8.0 * SLOPES[4 * g + j], in1=ps[:, 2 + g, 0:w],
                                             op0=ALU.mult, op1=ALU.add).then_inc(logits_done, 1)
                dve.wait_ge(logits_done, 3 * u + 3)
                ncol = sum(g[1] for g in groups) * P
                dve.tensor_reduce(stat[:, 0, u:u + 1], Lg[:, u % 2, 0:ncol], AX_X, ALU.max).then_inc(max_done, 1)
                dve.wait_ge(max_done, u + 1)
                dve.tensor_scalar(stat[:, 1, u:u + 1], stat[:, 0, u:u + 1], -0.125, None, ALU.mult)\
                   .then_inc(negmax_ready, 1)

            def dil_norm(u):
                n, j = u // 4, u % 4
                dve.wait_ge(probs_ready, u + 1)
                dve.reciprocal(stat[:, 3, u:u + 1], stat[:, 2, u:u + 1]).then_inc(rden_done, 1)
                dve.wait_ge(rden_done, u + 1)
                dve.wait_ge(pv_done, u + 1)
                if j == 0 and n >= 2:
                    dve.wait_ge(oT_psum, n - 1)
                dve.tensor_scalar(onat[n % 2][:, j * DH:(j + 1) * DH], ps[:, 7, j * DH:(j + 1) * DH],
                                  stat[:, 3, u:u + 1], None, ALU.mult).then_inc(o_norm, 1)

            def oa_lo(n):
                dve.wait_ge(oa_hi, n + 1)
                dve.tensor_tensor(Bl[:, 0:2, n * P:(n + 1) * P],
                                  ps[:, 7, 256:512].rearrange("p (a b) -> p a b", a=2),
                                  Bh[:, 0:2, n * P:(n + 1) * P], ALU.subtract).then_inc(oa_ready, 1)

            dve.wait_ge(bias_ready, 4)
            for u in range(16 + 3):
                if 0 <= u - 3 < 16:
                    dil_norm(u - 3)
                if u >= 7 and u % 4 == 3:
                    oa_lo((u - 7) // 4)
                if u % 2 == 0 and u < 16:
                    s = u // 2
                    if s >= 1:
                        scaled(T_GATE_A + s - 1, GA[:, s - 1, :], 1)
                    convert(T_GATE_A + s + 1)
                if 0 <= u - 1 < 16:
                    dil_softmax(u - 1)
                if u == 16:
                    scaled(T_GATE_A + 7, GA[:, 7, :], 1)
            oa_lo(3)

            for t in range(T_QKV_B, T_GATE_B + 1):
                if t > T_QKV_B:
                    i = t - 1 - T_QKV_B
                    if i >= 10:
                        dve.wait_ge(vtrans_done, 6 + i - 9)
                    scaled(t - 1, qb[:, i, :] if i < 4 else kb[:, i - 4, :] if i < 8 else vtb[:, i % 2, :], 1)
                if t < T_GATE_B:
                    convert(t + 1)

            def sb_z(w):
                n = w // 8
                nk = P * (n + 1)
                dve.wait_ge(sb_scores, w + 1)
                if w >= 2:
                    dve.wait_ge(sb_la, w - 1)
                dve.scalar_tensor_tensor(out=Zs[:, w % 2, 0:nk], in0=ps[:, 2 + w % 2, 0:nk], scalar=0.125,
                                         in1=SBM[:, 512 - nk:512], op0=ALU.mult, op1=ALU.add).then_inc(z_done, 1)

            def sb_log_a(w):
                nk = P * (w // 8 + 1)
                z, e, c = Zs[:, w % 2, 0:nk], Es[:, w % 2, 0:nk], Cs[:, w % 2, 0:nk]
                dve.wait_ge(sb_ln, w + 1)
                dve.scalar_tensor_tensor(out=e, in0=z, scalar=0.0, in1=e, op0=ALU.max, op1=ALU.add)\
                   .then_inc(sb_sp, 1)
                dve.wait_ge(sb_sp, w + 1)
                if w >= 2:
                    dve.wait_ge(sb_pt_psum, w - 1)
                dve.tensor_tensor_scan(c[:, ::-1], ones[:, 0:1].to_broadcast([P, nk]), e[:, ::-1], 0.0,
                                       ALU.mult, ALU.add).then_inc(sb_scan, 1)
                dve.wait_ge(sb_scan, w + 1)
                dve.tensor_tensor(c, z, c, ALU.subtract).then_inc(sb_la, 1)

            def ob_lo(n):
                dve.wait_ge(ob_hi, n + 1)
                dve.tensor_tensor(Bl[:, 2:6, n * P:(n + 1) * P], ps[:, 7, :].rearrange("p (a b) -> p a b", a=4),
                                  Bh[:, 2:6, n * P:(n + 1) * P], ALU.subtract).then_inc(ob_ready, 1)

            for i in range(32 + 6):
                if i % 4 == 0 and i <= 32:
                    s = i // 4
                    if s >= 1:
                        scaled(T_GATE_B + s - 1, GB[:, s - 1, :], 1)
                    if s < 8:
                        convert(T_GATE_B + s + 1)
                if 0 <= i - 1 < 32:
                    sb_z(i - 1)
                if 0 <= i - 2 < 32:
                    sb_log_a(i - 2)
                if i >= 13 and (i - 13) % 8 == 0:
                    ob_lo((i - 13) // 8)

            for m in range(KT):
                convert(T_UP_A + m + 1)
                gated(T_UP_A + m, m, GA[:, m, :], GA[:, m, :], ONE)
            for m in range(KT):
                convert(T_UP_B + m + 1)
                t = T_UP_B + m
                n = N_MERGE + m
                f = F[:, n % 2, 0:S1]
                gated(t, 8 + m, GB[:, m, :], f, ONE)
                dve.wait_ge(evac_done, t + 1)
                dve.tensor_tensor(f, f, GA[:, m, :], ALU.add).then_inc(f_ready, 1)
                split(n, Al[:, m, 0:S1], f, Ah[:, m, 0:S1])
            for m in range(KT):
                convert(T_OUT + m + 1)
                add_half(T_OUT + m, m, ONE)
                feed(1, N_MLP + m, m, G_MLP, ONE, Bh, Bl)
            stats(1, ONE)
            mlp(ONE)

            stats(2, ONE)
            for m in range(KT):
                x = X[:, m, META:S2]
                dve.scalar_tensor_tensor(out=x, in0=x, scalar=vecT[:, G_FIN + m:G_FIN + m + 1], in1=RS[:, 0:S1],
                                         op0=ALU.mult, op1=ALU.mult).then_inc(x_normed, 1)
                dve.wait_ge(x_normed, m + 1)
                if m == 0:
                    dve.wait_ge(meta_copied, 1)
                feed(3, N2_MIX + m, m, G_MIX2, ALL)

            def silu(i):
                dve.wait_ge(silu_tanh, i + 1)
                dve.scalar_tensor_tensor(out=sr[:, i, :], in0=G2[:, i % 2, :], scalar=1.0, in1=sr[:, i, :],
                                         op0=ALU.add, op1=ALU.mult).then_inc(silu_done, 1)

            def evac(t):
                if t < T2_LR:
                    scaled(t, k2[:, t - T2_K, PAD:PADL], ALL)
                elif t == T2_LR:
                    scaled(t, lr[0:16, :], ALL, 16)
                elif t < T2_A:
                    dve.wait_ge(slab_done, t + 1)
                    dve.scalar_tensor_tensor(out=q2[:, t - T2_Q, :], in0=dense_psum(t, REAL), scalar=0.125,
                                             in1=RS[:, META:S2], op0=ALU.mult, op1=ALU.mult).then_inc(evac_done, 1)
                elif t < T2_V:
                    scaled(t, apad[:, (t - T2_A) % 2, :], ALL)
                elif t < T2_PM:
                    scaled(t, v2[:, t - T2_V, PAD:PADL], ALL)
                elif t < T2_R:
                    g = t - T2_PM
                    n = N2_PM + g
                    f = F[:, n % 2, 0:S1]
                    dve.wait_ge(slab_done, t + 1)
                    dve.tensor_scalar(f, dense_psum(t, REAL), vecT[:, POOL_SC + g:POOL_SC + g + 1], None,
                                      ALU.mult).then_inc(evac_done, 1)
                    dve.wait_ge(evac_done, t + 1)
                    dve.sem_inc(f_ready, 1)
                    split(n, Bl[:, 4 + g, 0:S1], f, Bh[:, 4 + g, 0:S1])
                elif t < T2_GY:
                    i = t - T2_R
                    scaled(t, sr[:, i, :], REAL)
                    if i >= 1:
                        silu(i - 1)
                elif t < T2_GB:
                    i = t - T2_GY
                    if i == 0:
                        silu(3)
                        dve.wait_ge(silu_done, 4)
                    if i % 4 < 2:
                        scaled(t, G2[:, i % 2, :], REAL)
                    else:
                        m = i // 4 * 2 + i % 2
                        if m == 0:
                            dve.wait_ge(vr_psum, 12)
                        gated(t, 16 + m, G2[:, i % 2, :], ma[:, m, :], REAL)
                elif t < T2_GO:
                    scaled(t, GB2[:, t - T2_GB, :], REAL)
                elif t < T2_OUT:
                    m = t - T2_GO
                    n = N2_M + m
                    f, g = F[:, n % 2, 0:S1], G2[:, m % 2, :]
                    gated(t, 24 + m, GB2[:, m, :], g, REAL)
                    dve.wait_ge(evac_done, t + 1)
                    dve.tensor_tensor(f, ma[:, m, :], g, ALU.add).then_inc(f_ready, 1)
                    split(n, Al[:, m, 0:S1], f, Ah[:, m, 0:S1])

            def job(what):
                kind = what[0]
                if kind == "gate_up":
                    for j in range(2):
                        dve.wait_ge(gu_psum, j + 1)
                        dve.tensor_scalar(tokens(UU[:, j, :], 2), ps[:, 4 + 2 * j:6 + 2 * j, 0:HALF2],
                                          vecT[:, B_GATE2 + j:B_GATE2 + j + 1], None, ALU.add).then_inc(u_ready, 1)
                elif kind == "decay":
                    for j in range(2):
                        dve.wait_ge(u_ln, j + 1)
                        dve.scalar_tensor_tensor(out=la[:, j, PAD:PADL], in0=UU[:, j, :], scalar=0.0, in1=E2,
                                                 op0=ALU.min, op1=ALU.subtract).then_inc(la_ready, 1)
                        dve.wait_ge(la_ready, j + 1)
                        dve.tensor_tensor_scan(bS[:, j, :], reset, la[:, j, :], 0.0, ALU.mult, ALU.add)\
                           .then_inc(bs_ready, 1)
                    dve.wait_ge(bs_ready, 2)
                elif kind == "unit_d":
                    y = what[1]
                    if y // 2 == U_DIAG // 2 or y >= U_START:
                        return
                    x = exp_no(y)
                    v, ref, b = level_ref(y)
                    if x >= 2:
                        dve.wait_ge(qk_ready, (y - 2 if y < U_DIAG else y - 4) + 1)
                    dve.tensor_tensor(Ed[:, x % 2, :].rearrange("p (a b) -> p a b", b=b), v, ref, ALU.subtract)\
                       .then_inc(d_ready, 1)
                elif kind == "unit_qk":
                    y = what[1]
                    l, j = y // 2, y % 2
                    if l == U_DIAG // 2:
                        dve.sem_inc(qk_ready, 1)
                        return
                    x = exp_no(y)
                    e = Ed[:, x % 2, :]
                    dve.wait_ge(d_exp, x + 1)
                    if y < U_DIAG:
                        if y >= 2:
                            dve.wait_ge(mm_done, y - 1)
                        dve.tensor_tensor(Qp[:, j, :], q2[:, j, :], e, ALU.mult)
                        dve.tensor_tensor(Kp[:, j, :], k2[:, j, CH:], e, ALU.mult).then_inc(qk_ready, 1)
                    elif y < U_START:
                        dve.wait_ge(mm_done, U_DIAG - 2 + j + 1)
                        dve.tensor_tensor(Kp[:, j, :], k2[:, j, 0:8 * CH], e, ALU.mult).then_inc(qk_ready, 1)
                    else:
                        dve.tensor_tensor(Qs[:, j, :], q2[:, j, :], e, ALU.mult).then_inc(qk_ready, 1)
                    dve.wait_ge(qk_ready, y + 1)
                elif kind == "unit_mm":
                    y = what[1]
                    l, j = y // 2, y % 2
                    if y >= U_END:
                        return
                    dve.wait_ge(mm_done, y + 1)
                    src = ps[:, 4 + 2 * j, :]
                    if l == 0:
                        dve.tensor_copy(sc[:, j, :], src).then_inc(sc_done, 1)
                    else:
                        dve.wait_ge(sc_done, y - 1)
                        dve.copy_predicated(
                            sc[:, j, :].rearrange("p (a b) -> p a b", b=CH),
                            masks[:, l - 1, :].bitcast(U32).unsqueeze(1).to_broadcast([P, NCH - 1, CH]),
                            src.rearrange("p (a b) -> p a b", b=CH)).then_inc(sc_done, 1)
                elif kind == "kv":
                    j = what[1]
                    dve.wait_ge(kv_psum, j + 1)
                    dve.wait_ge(ebe_ready, 2)
                    if j == 0:
                        dve.wait_ge(kn_psum, 2)
                    for c in range(8):
                        kv = flat(4 + 2 * j)[:, c * P:(c + 1) * P]
                        dst = st[:, j, c * P:(c + 1) * P]
                        if c == 0:
                            ins = dve.tensor_copy(dst, kv)
                        else:
                            ins = dve.scalar_tensor_tensor(out=dst, in0=st[:, j, (c - 1) * P:c * P],
                                                           scalar=ebe[:, j, c:c + 1], in1=kv,
                                                           op0=ALU.mult, op1=ALU.add)
                        ins.then_inc(st_done, 1)
                        dve.wait_ge(st_done, 8 * j + c + 1)
                elif kind == "o_mm":
                    h = what[1]
                    dve.wait_ge(o_psum, h + 1)
                    if h >= 2:
                        dve.wait_ge(f_ready, staged(N2_O + h - 2))
                    dve.tensor_copy(osb[:, h % 2, :], ps[:, 4 + h % 2, :]).then_inc(o_copied, 1)
                elif kind == "o_stat":
                    h = what[1]
                    dve.wait_ge(o_stat, h + 1)
                    dve.tensor_scalar(SQ[:, h % 2, 0:S1], ps[:, 6 + h % 2, :], 4.0 / P, 4.0 * EPS, ALU.mult, ALU.add)\
                       .then_inc(o_ms, 1)
                elif kind == "o_norm":
                    h = what[1]
                    o, r = osb[:, h % 2, :], SQ[:, h % 2, 0:S1]
                    dve.wait_ge(o_sqrt, h + 1)
                    dve.reciprocal(r, r).then_inc(o_rstd, 1)
                    dve.wait_ge(o_rstd, h + 1)
                    dve.tensor_tensor(o, o, r, ALU.mult).then_inc(o_scaled, 1)
                    dve.wait_ge(o_scaled, h + 1)
                    n = N2_O + h
                    f = F[:, n % 2, 0:S1]
                    dve.scalar_tensor_tensor(out=f, in0=o, scalar=vecT[:, GLA_G + h:GLA_G + h + 1],
                                             in1=sr[:, h, :], op0=ALU.mult, op1=ALU.mult).then_inc(f_ready, 1)
                    split(n, Bl[:, h, 0:S1], f, Bh[:, h, 0:S1])
                elif kind == "pool_split":
                    g = what[1]
                    w = WINDOWS[g]
                    n = N2_POOL + g
                    f = F[:, n % 2, 0:S1]
                    dve.wait_ge(win_done, (g + 1) * (g + 2) // 2)
                    dve.scalar_tensor_tensor(out=f, in0=wsum[:, g % 2, META:S2], scalar=1.0 / w,
                                             in1=apad[:, g % 2, META:], op0=ALU.mult, op1=ALU.subtract)\
                       .then_inc(f_ready, 1)
                    split(n, Bl[:, g, 0:S1], f, Bh[:, g, 0:S1])

            dve.wait_ge(zeros2_ready, 1)
            for t in range(T2, T2_OUT + 1):
                if t == T2 + 1:
                    stats(3, ALL)
                if t > T2:
                    evac(t - 1)
                if t < T2_OUT:
                    convert(t + 1)
                    for what in between[t]:
                        job(what)
            for m in range(KT):
                convert(T2_OUT + m + 1)
                add_half(T2_OUT + m, m, REAL)
                feed(4, N2_FFN + m, m, G_FFN2, REAL, Bh, Bl)
            stats(4, REAL)
            mlp(REAL)
            stats(5, REAL)
            for m in range(KT):
                dve.scalar_tensor_tensor(out=Y[:, m, :], in0=X[:, m, META:S2],
                                         scalar=vecT[:, G_FIN2 + m:G_FIN2 + m + 1], in1=RS[:, 0:S1],
                                         op0=ALU.mult, op1=ALU.mult).then_inc(y_ready, 1)

        @block.tensor
        def _(pe):
            def products(t_ps, slot, kt, Oh, Ol, o0, kind, k_from, k_to, ready=None, col0=0):
                h, l = w_slab(wh, slot, kt), w_slab(wl, slot, kt)
                last = None
                for k in range(k_from, k_to):
                    if ready is not None:
                        ready(k)
                    for i, (a, b) in enumerate(((h, Oh), (h, Ol), (l, Oh))):
                        start, stop = k == 0 and i == 0, k == kt - 1 and i == 2
                        if kind == ALL:
                            for half in range(2):
                                last = pe.matmul(ps[:, 2 * (t_ps % 2) + half, 0:HALF2], a[:, k, :],
                                                 b[:, o0 + k, half * HALF2:(half + 1) * HALF2],
                                                 start=start, stop=stop)
                        else:
                            last = pe.matmul(dense_psum(t_ps, kind), a[:, k, :], b[:, o0 + k, col0:col0 + S1],
                                             start=start, stop=stop)
                return last

            def slab_start(t):
                pe.wait_ge(lo_ready, t + 1)
                if t >= 2:
                    pe.wait_ge(evac_done, t - 1)

            def full_slab(t, Oh, Ol, o0, kind, ready=None, col0=0):
                kt = slab[t][2]
                slab_start(t)
                products(t, t % 2, kt, Oh, Ol, o0, kind, 0, kt, ready, col0).then_inc(slab_done, 1)

            def split_ready(n0):
                return lambda k: pe.wait_ge(act_ready, n0 + k + 1)

            def stats(norm, kind):
                pe.wait_ge(ss_done, 8 * norm + 8)
                if kind != ALL:
                    pe.matmul(ps[:, 7, :], ones[:, :], SS[:, 0:S1], start=True, stop=True).then_inc(stat_done, 1)
                else:
                    for half in range(2):
                        mm = pe.matmul(ps[:, 6 + half, 0:HALF2], ones[:, :],
                                       SS[:, half * HALF2:(half + 1) * HALF2], start=True, stop=True)
                    mm.then_inc(stat_done, 1)

            def mlp_chunk(which, c, last):
                t0, n0, _ = MLPS[which]
                feed_n = N_MLP if which == ONE else N2_FFN
                for j in range(16):
                    t = t0 + j
                    pe.wait_ge(lo_ready, t + 16 * c + 1)
                    pe.wait_ge(evac_done, t + 16 * c - 1)
                    if j < 8:
                        ready = None
                        if not last and j == 0:
                            ready = split_ready(feed_n)
                        mm = products(t, t % 2, KT, Bh, Bl, 0, which, 0, KT, ready)
                    else:
                        ready = None
                        if j == 8:
                            def ready(k):
                                pe.wait_ge(act_ready, n0 + 8 * c + (k + 1))
                        mm = products(t, t % 2, KT, Ah, Al, 0, which, 0, KT, ready)
                    mm.then_inc(slab_done, 1)

            def mlp(which):
                with pe.Fori(0, CHUNKS - 1) as c:
                    mlp_chunk(which, c, False)
                mlp_chunk(which, CHUNKS - 1, True)

            pe.wait_ge(consts_ready, 2)
            pe.wait_ge(params_in, 16 * 12)
            pe.transpose(ps[:, 5, 0:NVEC], vrow[0:NVEC, :], ident[0:NVEC, 0:NVEC]).then_inc(vec_psum, 1)
            for m in range(KT):
                mm = pe.transpose(ps[:, 4, m * META:(m + 1) * META], mnat[0:META, m * P:(m + 1) * P],
                                  ident[0:META, 0:META])
            mm.then_inc(meta_psum, 1)
            pe.wait_ge(x_in, 16)
            for m in range(KT):
                if m >= 2:
                    pe.wait_ge(xt_copied, m - 1)
                for a in range(4):
                    mm = pe.transpose(ps[:, 2 + m % 2, a * P:(a + 1) * P], xnat[:, a, m * P:(m + 1) * P], ident[:, :])
                mm.then_inc(xt_psum, 1)

            def v_turn(i, src):
                if i >= 2:
                    pe.wait_ge(vnat_copied, i - 1)
                for a in range(4):
                    mm = pe.transpose(ps[:, 6 + i % 2, a * P:(a + 1) * P], src[:, a * P:(a + 1) * P], ident[:, :])
                mm.then_inc(vtrans_done, 1)

            full_slab(0, Ah, Al, 0, 1, split_ready(N_MIX))
            stats(0, ONE)
            for t in range(1, T_GATE_A):
                full_slab(t, Ah, Al, 0, 1)
                if t >= 13:
                    pe.wait_ge(evac_done, t)
                    if t == 13:
                        pe.wait_ge(ms_ready, 1)
                    v_turn(t - 13, vt[:, (t - 1) % 2, :])
            pe.wait_ge(evac_done, T_GATE_A)
            v_turn(5, vt[:, 1, :])

            def dil_scores(u):
                n, j = u // 4, u % 4
                if u >= 1:
                    pe.wait_ge(logits_done, 3 * u)
                for g, (k0, nb, _) in enumerate(dil_groups(n)):
                    head = 4 * g + j
                    b = DH * (head % 2)
                    mm = pe.matmul(ps[:, 2 + g, 0:nb * P], qa[b:b + DH, head // 2, n * P:(n + 1) * P],
                                   ka[b:b + DH, head // 2, k0:k0 + nb * P], start=True, stop=True)
                mm.then_inc(scores_done, 1)

            def dil_turn(u):
                pe.wait_ge(probs_ready, u + 1)
                for g, (_, nb, col) in enumerate(dil_groups(u // 4)):
                    if 3 * u + g >= 2:
                        pe.wait_ge(pt_copied, 3 * u + g - 1)
                    for i in range(nb):
                        mm = pe.transpose(ps[:, 5 + (3 * u + g) % 2, i * P:(i + 1) * P],
                                          Lg[:, u % 2, col + i * P:col + (i + 1) * P], ident[:, :])
                    mm.then_inc(pt_psum, 1)

            def dil_pv(u):
                n, j = u // 4, u % 4
                pe.wait_ge(pt_copied, 3 * u + 3)
                if u >= 1:
                    pe.wait_ge(o_norm, u)
                if u >= 5 and u % 4 == 1:
                    pe.wait_ge(oa_ready, u // 4)
                groups = dil_groups(n)
                total = sum(g[1] for g in groups)
                done = 0
                for g, (k0, nb, col) in enumerate(groups):
                    head = 4 * g + j
                    for i in range(nb):
                        mm = pe.matmul(ps[:, 7, j * DH:(j + 1) * DH], PT[:, col // P + i, :],
                                       Vna[:, k0 // P + i, head * DH:(head + 1) * DH],
                                       start=(done == 0), stop=(done == total - 1))
                        done += 1
                mm.then_inc(pv_done, 1)

            def oa_turn(n):
                pe.wait_ge(o_norm, min(4 * n + 5, 16))
                for i in range(2):
                    mm = pe.transpose(ps[:, 7, 256 + i * P:256 + (i + 1) * P], onat[n % 2][:, i * P:(i + 1) * P], ident[:, :])
                mm.then_inc(oT_psum, 1)

            pe.wait_ge(vnat_copied, 6)
            for u in range(16 + 3):
                if u >= 7 and u % 4 == 3:
                    oa_turn(u // 4 - 1)
                if u < 16:
                    t = T_GATE_A + u // 2
                    if u % 2 == 0:
                        slab_start(t)
                    mm = products(t, t % 2, KT, Ah, Al, 0, 1, 4 * (u % 2), 4 * (u % 2) + 4)
                    if u % 2:
                        mm.then_inc(slab_done, 1)
                if 0 <= u - 2 < 16:
                    dil_pv(u - 2)
                if 0 <= u - 1 < 16:
                    dil_turn(u - 1)
                if u < 16:
                    dil_scores(u)
            oa_turn(3)

            for t in range(T_QKV_B, T_GATE_B):
                full_slab(t, Ah, Al, 0, 1)
                i = t - T_QKV_B - 9
                if i >= 0:
                    pe.wait_ge(evac_done, t)
                    v_turn(6 + i, vtb[:, i % 2, :])
            pe.wait_ge(evac_done, T_GATE_B)
            v_turn(9, vtb[:, 1, :])

            def sb_scores_mm(w):
                n, h = w // 8, w % 8
                b = DH * (h % 2)
                if w >= 2:
                    pe.wait_ge(z_done, w - 1)
                pe.matmul(ps[:, 2 + w % 2, 0:(n + 1) * P], qb[b:b + DH, h // 2, n * P:(n + 1) * P],
                          kb[b:b + DH, h // 2, 0:(n + 1) * P], start=True, stop=True).then_inc(sb_scores, 1)

            def sb_turn(w):
                pe.wait_ge(sb_probs, w + 1)
                if w >= 2:
                    pe.wait_ge(sb_pt_copied, w - 1)
                for i in range(w // 8 + 1):
                    mm = pe.transpose(ps[:, 4 + w % 2, i * P:(i + 1) * P], Cs[:, w % 2, i * P:(i + 1) * P], ident[:, :])
                mm.then_inc(sb_pt_psum, 1)

            def sb_pv_mm(w):
                n, h = w // 8, w % 8
                pe.wait_ge(sb_pt_copied, w + 1)
                if h == 0 and n >= 1:
                    pe.wait_ge(ob_nat, n)
                for i in range(n + 1):
                    mm = pe.matmul(ps[:, 6, h * DH:(h + 1) * DH], PTb[:, w % 2, i * P:(i + 1) * P],
                                   Vnb[:, i, h * DH:(h + 1) * DH], start=(i == 0), stop=(i == n))
                mm.then_inc(sb_pv, 1)

            def ob_turn(n):
                pe.wait_ge(ob_nat, n + 1)
                if n >= 1:
                    pe.wait_ge(ob_ready, n)
                for i in range(4):
                    mm = pe.transpose(ps[:, 7, i * P:(i + 1) * P], onatb[:, i * P:(i + 1) * P], ident[:, :])
                mm.then_inc(obT_psum, 1)

            pe.wait_ge(vnat_copied, 10)
            for i in range(32 + 6):
                if i < 32:
                    t = T_GATE_B + i // 4
                    if i % 4 == 0:
                        slab_start(t)
                    mm = products(t, t % 2, KT, Ah, Al, 0, 1, 2 * (i % 4), 2 * (i % 4) + 2)
                    if i % 4 == 3:
                        mm.then_inc(slab_done, 1)
                if 0 <= i - 4 < 32:
                    sb_pv_mm(i - 4)
                if 0 <= i - 3 < 32:
                    sb_turn(i - 3)
                if i < 32:
                    sb_scores_mm(i)
                if i >= 12 and (i - 12) % 8 == 0:
                    ob_turn((i - 12) // 8)

            pe.wait_ge(oa_ready, 4)
            for t in range(T_UP_A, T_UP_B):
                full_slab(t, Bh, Bl, 0, 1)
            pe.wait_ge(ob_ready, 4)
            for t in range(T_UP_B, T_OUT):
                full_slab(t, Bh, Bl, 2, 1)
            for t in range(T_OUT, T_MLP):
                full_slab(t, Ah, Al, 0, 1, split_ready(N_MERGE) if t == T_OUT else None)
            pe.wait_ge(ob_ready, 4)
            stats(1, ONE)
            mlp(ONE)

            stats(2, ONE)

            full_slab(T2, Ah, Al, 0, ALL, split_ready(N2_MIX))
            stats(3, ALL)

            def job(what):
                kind = what[0]
                if kind == "gate_up":
                    pe.wait_ge(evac_done, T2_LR + 1)
                    pe.wait_ge(ms_ready, 4)
                    for j in range(2):
                        for half in range(2):
                            mm = pe.matmul(ps[:, 4 + 2 * j + half, 0:HALF2], wgu[:, j * P:(j + 1) * P],
                                           lr[0:16, half * HALF2:(half + 1) * HALF2], start=True, stop=True)
                        mm.then_inc(gu_psum, 1)
                elif kind == "v_rows":
                    h = what[1]
                    beta = 64 * (h % 2)
                    pe.wait_ge(evac_done, T2_V + h + 1)
                    for g, (c0, nc_) in enumerate(((0, 4), (4, 4), (8, 1))):
                        x = 3 * h + g
                        if x >= 2:
                            pe.wait_ge(vr_copied, x - 1)
                        else:
                            pe.wait_ge(u_ready, 2)
                        for i in range(nc_):
                            c = c0 + i
                            mm = pe.matmul(ps[beta:beta + 64, 5 + 2 * (x % 2), i * P:(i + 1) * P],
                                           v2[:, h, c * CH:(c + 1) * CH], ident[:, :], start=True, stop=True)
                        mm.then_inc(vr_psum, 1)
                elif kind == "unit_mm":
                    y = what[1]
                    l, j = y // 2, y % 2
                    if y >= U_START:
                        return
                    pe.wait_ge(qk_ready, y + 1)
                    if y >= 2:
                        pe.wait_ge(sc_done, min(y - 1, U_END))
                    if y < U_END:
                        Q, K = (Qp, Kp) if l < U_DIAG // 2 else (q2, k2)
                        k0 = 0 if l < U_DIAG // 2 else CH
                        for c in range(8):
                            for hh in range(2):
                                b = 64 * hh
                                mm = pe.matmul(ps[b:b + 64, 4 + 2 * j, c * CH:(c + 1) * CH],
                                               K[b:b + 64, j, k0 + c * CH:k0 + (c + 1) * CH],
                                               Q[b:b + 64, j, c * CH:(c + 1) * CH], start=True, stop=True)
                        mm.then_inc(mm_done, 1)
                    else:
                        pe.wait_ge(sc_done, U_END)
                        for c in range(8):
                            for hh in range(2):
                                b = 64 * hh
                                mm = pe.matmul(ps[b:b + 64, 4 + 2 * j, c * CH:(c + 1) * CH],
                                               Kp[b:b + 64, j, c * CH:(c + 1) * CH], ident[b:b + 64, b:b + 64],
                                               start=True, stop=True)
                        mm.then_inc(kn_psum, 1)
                elif kind == "kv":
                    j = what[1]
                    pe.wait_ge(kn_copied, 2)
                    pe.wait_ge(vr_copied, 12)
                    for c in range(8):
                        for hh in range(2):
                            b = 64 * hh
                            mm = pe.matmul(ps[b:b + 64, 4 + 2 * j + c // 4, (c % 4) * P:(c % 4 + 1) * P],
                                           Kn[b:b + 64, j, c * CH:(c + 1) * CH],
                                           Vn[b:b + 64, j, c * P:(c + 1) * P], start=True, stop=True)
                    mm.then_inc(kv_psum, 1)
                elif kind == "o_mm":
                    h = what[1]
                    j, b = h // 2, 64 * (h % 2)
                    if h == 0:
                        pe.wait_ge(st_done, 16)
                        pe.wait_ge(qk_ready, U_START + 2)
                    if h >= 2:
                        pe.wait_ge(o_copied, h - 1)
                    for c in range(1, NCH):
                        at = slice((c - 1) * CH, c * CH)
                        pe.matmul(ps[:, 4 + h % 2, at], Vn[b:b + 64, j, c * P:(c + 1) * P], sc[b:b + 64, j, at],
                                  start=True, stop=False)
                        mm = pe.matmul(ps[:, 4 + h % 2, at], st[b:b + 64, j, (c - 1) * P:c * P],
                                       Qs[b:b + 64, j, at], start=False, stop=True)
                    mm.then_inc(o_psum, 1)
                elif kind == "o_stat":
                    h = what[1]
                    pe.wait_ge(o_sq, h + 1)
                    if h >= 2:
                        pe.wait_ge(o_ms, h - 1)
                    pe.matmul(ps[:, 6 + h % 2, :], ones[:, :], osb2, start=True, stop=True).then_inc(o_stat, 1)

            for t in range(T2, T2_OUT):
                if T2_PM <= t < T2_R:
                    g = t - T2_PM
                    full_slab(t, Bh, Bl, g, REAL, lambda k: pe.wait_ge(act_ready, N2_POOL + g + 1))
                elif T2_GY <= t < T2_GB and (t - T2_GY) % 4 >= 2:
                    full_slab(t, Bh, Bl, 4, REAL, split_ready(N2_PM))
                elif T2_GO <= t:
                    full_slab(t, Bh, Bl, 0, REAL, split_ready(N2_O))
                elif t < T2_Q or T2_A <= t < T2_PM:
                    if t > T2:
                        full_slab(t, Ah, Al, 0, ALL)
                else:
                    full_slab(t, Ah, Al, 0, REAL, None, META)
                for what in between[t]:
                    job(what)
            for t in range(T2_OUT, T2_MLP):
                full_slab(t, Ah, Al, 0, REAL, split_ready(N2_M) if t == T2_OUT else None)
            stats(4, REAL)
            mlp(REAL)
            stats(5, REAL)
            pe.wait_ge(y_ready, KT)
            for a in range(4):
                for half in range(2):
                    if a >= 1:
                        pe.wait_ge(y_copied, 2 * a - 1 + half)
                    for i in range(4):
                        mm = pe.transpose(ps[:, 4 + half, i * P:(i + 1) * P],
                                          Y[:, 4 * half + i, a * P:(a + 1) * P], ident[:, :])
                    mm.then_inc(y_psum, 1)


_INS = ["x", "norm_mix_g", "w_in", "b_gate", "w_up_dil", "w_up_sb", "w_out", "norm_mlp_g", "w_mlp_in",
        "w_mlp_out", "norm_final_g", "meta_tokens_2", "norm_mix_2", "w_in_2", "w_pool_mix_2", "pool_scale_2",
        "w_pool_out_2", "w_gate_up_2", "b_gate_2", "gla_norm_2", "w_gla_out_2", "w_out_2", "norm_ffn_2",
        "w_ff1_2", "w_ff2_2", "norm_final_2"]


def kernel(**inputs):
    import numpy as _np
    import concourse.bacc as _bacc
    from concourse.bass_utils import run_bass_kernel_spmd as _run

    nc = _bacc.Bacc("TRN2", target_bir_lowering=False, num_devices=1)
    arrays, aps = {}, {}
    for name in _INS:
        a = _np.ascontiguousarray(inputs[name])
        arrays[f"in_{name}"] = a
        aps[name] = nc.dram_tensor(f"in_{name}", a.shape, mybir.dt.from_np(a.dtype), kind="ExternalInput").ap()
    aps["out"] = nc.dram_tensor("out_0", (1, S1, DM), F32, kind="ExternalOutput").ap()
    build(nc, aps)
    r = _run(nc, [arrays], core_ids=[0])
    return r.results[0]["out_0"]
```

```python
from contextlib import ExitStack

import concourse.bass as bass
from concourse import mybir

F32 = mybir.dt.float32
F32R = mybir.dt.float32r
I32 = mybir.dt.int32
U32 = mybir.dt.uint32
ALU = mybir.AluOpType
ACT = mybir.ActivationFunctionType
AX_X = mybir.AxisListType.X

P = 128
DM = 1024
KT = DM // P
S1 = 512
META = 16
S2 = META + S1
ONE, ALL, REAL = 1, 2, 3
HALF2 = S2 // 2
DH = 64
DIL_W, SB_W = 768, 512
D_FF = 4 * DM
CHUNKS = D_FF // DM
NEG = -1.0e30
EPS = 1.0e-6
DILATIONS = (1, 4, 16)
SLOPES = [2.0 ** (-8.0 * (i + 1) / 12) for i in range(12)]
DIL_STEPS = 21
SB_STEPS = 38
CH, NCH = 64, 9
PADL = NCH * CH
PAD = PADL - S2
TAU = 16.0
EXP_LN_SET = "natural_log_exp_and_others"
LEVELS = (64, 32, 16, 8, 4, 2)
WINDOWS = (2, 4, 8, 16)

G_MLP, G_FIN, G_MIX2, G_FFN2, G_FIN2, B_GATE, B_GATE2, POOL_SC, GLA_G, G_MIX, NVEC = (
    0, 8, 16, 24, 32, 40, 56, 58, 62, 66, 74)

T_QKV_A, T_GATE_A, T_QKV_B, T_GATE_B, T_UP_A, T_UP_B, T_OUT, T_MLP = 0, 18, 26, 38, 46, 54, 62, 70
T2 = T_MLP + 16 * CHUNKS
T2_K, T2_LR, T2_Q, T2_A, T2_V, T2_R, T2_PM, T2_GY = (
    T2, T2 + 2, T2 + 3, T2 + 5, T2 + 9, T2 + 13, T2 + 17, T2 + 18)
T2_GB = T2_GY + 16
T2_GO = T2_GB + 8
T2_OUT = T2_GO + 8
T2_MLP = T2_OUT + 8
T_END = T2_MLP + 16 * CHUNKS
N_MIX, N_MERGE, N_MLP, N_HID = 0, 8, 16, 24
N2_MIX = N_HID + 8 * CHUNKS
N2_POOL, N2_PM, N2_O, N2_M, N2_FFN = N2_MIX + 8, N2_MIX + 12, N2_MIX + 16, N2_MIX + 20, N2_MIX + 28
N2_HID = N2_FFN + 8


def staged(n):
    return n + 1 - sum(KT for n0 in (N_MIX, N_MLP, N2_MIX, N2_FFN) if n0 < n)


def make_loads():
    loads, t = [], 0

    def add(name, at, kt, slabs):
        nonlocal t
        loads.append((name, at, kt, slabs, t))
        t += slabs

    def wide(name, base, tiles, kt=KT):
        for i in range(0, tiles, 2):
            add(name, base + i * P, kt, 2)

    wide("w_in", 0, 18)
    wide("w_in", 3 * DIL_W + 3 * SB_W, 8)
    wide("w_in", 3 * DIL_W, 12)
    wide("w_in", 3 * DIL_W + 3 * SB_W + DM, 8)
    wide("w_up_dil", 0, 8, 2)
    wide("w_up_sb", 0, 8, 4)
    wide("w_out", 0, 8)
    assert t == T_MLP
    first_mlp = len(loads)
    for c in range(CHUNKS):
        wide("mlp_in", c * DM, 8)
        for i in range(4):
            add("mlp_out", (c, i), KT, 2)
    assert t == T2
    wide("w_in_2", 768, 2)
    add("w_in_2", 2048, KT, 1)
    wide("w_in_2", 512, 2)
    wide("w_in_2", 0, 4)
    wide("w_in_2", 1024, 4)
    wide("w_in_2", 1536, 4)
    add("pool_mix", 0, 4, 1)
    for i in range(0, 8, 2):
        add("w_in_2", 2064 + i * P, KT, 2)
        add("pool_out", i * P, 4, 2)
    wide("w_in_2", 2064 + DM, 8)
    wide("gla_out", 0, 8, 4)
    wide("w_out_2", 0, 8)
    assert t == T2_MLP
    second_mlp = len(loads)
    for c in range(CHUNKS):
        wide("mlp_in_2", c * DM, 8)
        for i in range(4):
            add("mlp_out_2", (c, i), KT, 2)
    return loads, first_mlp, second_mlp


def make_between():
    between = {t: [] for t in range(T2, T2_MLP)}
    between[T2_LR + 1] += [("gate_up",)]
    between[T2_LR + 2] += [("decay",)]
    for g in range(4):
        between[T2_A + g + 2] += [("pool_split", g)]
        between[T2_V + g + 1] += [("v_rows", g)]
    units = 2 * (len(LEVELS) + 3)
    t = T2_A
    for y in range(units + 2):
        if y < units:
            between[t] += [("unit_d", y)]
        if 0 <= y - 1 < units:
            between[t] += [("unit_qk", y - 1)]
        if 0 <= y - 2 < units:
            between[t] += [("unit_mm", y - 2)]
        t += 1
        if t == T2_PM:
            t += 1
    assert t <= T2_GY + 8
    between[T2_GY + 8] += [("kv", 0)]
    between[T2_GY + 12] += [("kv", 1)]
    t = T2_GY + 14
    for h in range(4):
        between[t + 2 * h] += [("o_mm", h)]
        between[t + 2 * h + 1] += [("o_stat", h)]
        between[t + 2 * h + 2] += [("o_norm", h)]
    assert t + 8 < T2_GO
    return between


def build(nc, d):
    loads, first_mlp, second_mlp = make_loads()
    between = make_between()
    slab = {}
    for p, (_, _, kt, n, t) in enumerate(loads):
        for i in range(n):
            slab[t + i] = (p, i, kt, n)

    def weight_view(name, at, kt, cols):
        if name == "pool_mix":
            return d["w_pool_mix_2"][0].rearrange("g c e -> c g e")
        if name in ("mlp_out", "mlp_out_2"):
            c, i = at
            w = d["w_mlp_out" if name == "mlp_out" else "w_ff2_2"][0]
            return w[c * DM:(c + 1) * DM, i * 256:(i + 1) * 256].rearrange("(k p) n -> p k n", p=P)
        w = d[{"w_in": "w_in", "w_up_dil": "w_up_dil", "w_up_sb": "w_up_sb", "w_out": "w_out",
               "mlp_in": "w_mlp_in", "w_in_2": "w_in_2", "pool_out": "w_pool_out_2",
               "gla_out": "w_gla_out_2", "w_out_2": "w_out_2", "mlp_in_2": "w_ff1_2"}[name]][0]
        return w[:, at:at + cols].rearrange("(k p) n -> p k n", p=P)

    ctx = ExitStack()
    with ctx:
        def sb(name, shape, dt=F32):
            return ctx.enter_context(nc.sbuf_tensor(name, shape, dt))

        def sem(name):
            return ctx.enter_context(nc.semaphore(name))

        X = sb("X", [P, KT, S2])
        Ah, Al = sb("Ah", [P, KT, S2], F32R), sb("Al", [P, KT, S2], F32R)
        Bh, Bl = sb("Bh", [P, KT, S2], F32R), sb("Bl", [P, KT, S2], F32R)
        raw = sb("raw", [P, 2, 2 * DM])
        wh, wl = sb("wh", [P, 2, DM], F32R), sb("wl", [P, 2, DM], F32R)
        F = sb("F", [P, 2, S2])
        SQ = sb("SQ", [P, 2, META + S2])
        SS, RS = sb("SS", [P, S2]), sb("RS", [P, S2])
        ident, ones = sb("ident", [P, P]), sb("ones", [P, P])
        vecT = sb("vecT", [P, NVEC])
        halfb = sb("halfb", [P, 16])
        wgu = sb("wgu", [16, 256])
        stat = sb("stat", [P, 5, 16])
        ebe = sb("ebe", [P, 2, NCH])
        masks = sb("masks", [P, 6, CH])
        AR = 19456
        arena = sb("arena", [P, AR])
        ps = ctx.enter_context(nc.psum_tensor("ps", [P, 8, 512], F32))

        def region(at, *shape):
            n = 1
            for s in shape:
                n *= s
            assert at + n <= AR, (at, shape)
            v = arena[:, at:at + n]
            if len(shape) == 2:
                v = v.rearrange("p (a b) -> p a b", a=shape[0])
            return v

        SBM = region(0, 512)
        D0, D1, D2 = region(512, 256), region(768, 512), region(1280, 512)
        qa, ka = region(1792, 6, 512), region(4864, 6, 512)
        Vna = region(7936, 4, 768)
        Lg = region(11008, 2, 1280)
        PT = region(13568, 10, 128)
        onat = [region(14848, 256), region(19200, 256)]
        vt = region(13568, 2, 512)
        GA = region(15104, 8, 512)
        qb, kb = region(1792, 4, 512), region(3840, 4, 512)
        Vnb = region(5888, 4, 512)
        GB = region(7936, 8, 512)
        Zs, Es, Cs = region(12032, 2, 512), region(13056, 2, 512), region(14080, 2, 512)
        PTb = region(512, 2, 512)
        onatb = SQ[:, 0, 0:512]
        vtb = region(512, 2, 512)
        xnat = region(1792, 4, 1024)
        mnat = region(5888, 1024)
        vrow, grow = region(6912, 128), region(7040, 128)
        DI = arena[:, 11008:11520].bitcast(I32)
        DM4 = arena[:, 11520:12032].bitcast(I32)
        PEN = region(12032, 512)
        k2, q2 = region(0, 2, PADL), region(1152, 2, S1)
        bS = region(2176, 2, PADL)
        la = region(3328, 2, PADL)
        Kn = region(3328, 2, CH * 8)
        GB2 = region(0, 8, S1)
        Ed = region(4480, 2, S1)
        Qp, Kp = region(5504, 2, S1), region(6528, 2, S1)
        st = region(4480, 2, 8 * P)
        osb = region(6528, 2, S1)
        osb2 = region(3584, S1)
        sc = region(7552, 2, S1)
        Vn = region(8576, 2, NCH * P)
        Qs = region(10880, 2, S1)
        sr = region(11904, 4, S1)
        apad = region(11904, 2, S2)
        G2 = region(13952, 2, S1)
        reset = region(13952, PADL)
        UU = region(14976, 2, S2)
        E2 = region(16032, S2)
        lr = region(16560, S2)
        v2 = region(17088, 4, PADL)
        ma = region(14976, 8, S1)
        SQ2, SS2 = region(8576, 2, S1), region(9600, S2)
        gain2 = region(10128, KT)
        meta2 = region(10136, KT, META)
        msq = region(10264, KT, META)
        RS1 = region(4480, S1)
        wsum = SQ
        Y = region(0, 8, S1)
        ON = region(4096, 4, DM)
        Y_BANKS = (1, 3, 4, 5)
        r_tok = stat[:, 4, 0:4]

        params_in, gain_in = sem("params_in"), sem("gain_in")
        x_in = [sem(f"x_in{i}") for i in range(4)]
        w_landed = [sem("w_landed0"), sem("w_landed1")]
        hi_ready, lo_ready = sem("hi_ready"), sem("lo_ready")
        slab_done, evac_done = sem("slab_done"), sem("evac_done")
        f_ready, hi_split, act_ready = sem("f_ready"), sem("hi_split"), sem("act_ready")
        sq_ready, ss_done = sem("sq_ready"), sem("ss_done")
        stat_done, ms_ready, sqrt_ready, rstd_ready = (
            sem("stat_done"), sem("ms_ready"), sem("sqrt_ready"), sem("rstd_ready"))
        consts_ready, pool_step = sem("consts_ready"), sem("pool_step")
        di_ready, dist_step, dist_raw = sem("di_ready"), sem("dist_step"), sem("dist_raw")
        bias_ready = sem("bias_ready")
        gain_psum, gain_ready, late_scaled = sem("gain_psum"), sem("gain_ready"), sem("late_scaled")
        vec_psum, vec_ready, halfb_ready = sem("vec_psum"), sem("vec_ready"), sem("halfb_ready")
        xt_psum, xt_copied, meta_psum, meta_copied = (
            sem("xt_psum"), sem("xt_copied"), sem("meta_psum"), sem("meta_copied"))
        vtrans_done, vnat_copied = sem("vtrans_done"), sem("vnat_copied")
        gate_done = sem("gate_done")
        scores_done, logits_done, max_done, negmax_ready, probs_ready = (
            sem("scores_done"), sem("logits_done"), sem("max_done"), sem("negmax_ready"), sem("probs_ready"))
        pt_psum, pt_copied, pv_done, rden_done, o_norm = (
            sem("pt_psum"), sem("pt_copied"), sem("pv_done"), sem("rden_done"), sem("o_norm"))
        oT_psum, oa_hi, oa_ready = sem("oT_psum"), sem("oa_hi"), sem("oa_ready")
        sb_scores, z_done, sb_abs, sb_exp, sb_ln = (
            sem("sb_scores"), sem("z_done"), sem("sb_abs"), sem("sb_exp"), sem("sb_ln"))
        sb_sp, sb_scan, sb_la, sb_probs = sem("sb_sp"), sem("sb_scan"), sem("sb_la"), sem("sb_probs")
        sb_pt_psum, sb_pt_copied, sb_pv = sem("sb_pt_psum"), sem("sb_pt_copied"), sem("sb_pv")
        ob_nat, obT_psum, ob_hi, ob_ready = sem("ob_nat"), sem("obT_psum"), sem("ob_hi"), sem("ob_ready")
        gain2_ready, meta_sum, meta_hi, meta_split = (
            sem("gain2_ready"), sem("meta_sum"), sem("meta_hi"), sem("meta_split"))
        sq2_ready, ss2_done, sqrt1_ready, ms1_step = (
            sem("sq2_ready"), sem("ss2_done"), sem("sqrt1_ready"), sem("ms1_step"))
        x_normed = sem("x_normed")
        zeros2_ready = sem("zeros2_ready")
        gu_psum, u_ready, u_abs, u_exp, u_ln, la_ready, bs_ready, ebe_ready = (
            sem("gu_psum"), sem("u_ready"), sem("u_abs"), sem("u_exp"), sem("u_ln"), sem("la_ready"),
            sem("bs_ready"), sem("ebe_ready"))
        vr_psum, vr_copied = sem("vr_psum"), sem("vr_copied")
        d_ready, d_abs, d_exp, qk_ready, mm_done, sc_done = (
            sem("d_ready"), sem("d_abs"), sem("d_exp"), sem("qk_ready"), sem("mm_done"), sem("sc_done"))
        kn_psum, kn_copied, kv_psum, st_done = sem("kn_psum"), sem("kn_copied"), sem("kv_psum"), sem("st_done")
        o_psum, o_copied, o_sq, o_stat, o_ms, o_sqrt, o_rstd, o_scaled = (
            sem("o_psum"), sem("o_copied"), sem("o_sq"), sem("o_stat"), sem("o_ms"), sem("o_sqrt"),
            sem("o_rstd"), sem("o_scaled"))
        win_done = sem("win_done")
        silu_tanh, silu_done = sem("silu_tanh"), sem("silu_done")
        y_ready, y_psum, y_copied, y_low, y_high, out_done = (
            sem("y_ready"), sem("y_psum"), sem("y_copied"), sem("y_low"), sem("y_high"), sem("out_done"))

        def dense_psum(t, kind):
            if kind == ONE:
                return ps[:, t % 2, :]
            bank = 2 * ((t + 1) % 2)
            if kind == REAL:
                return ps[:, bank, :]
            return ps[:, bank:bank + 2, 0:HALF2]

        def pool_bank(g):
            slot = 2 * ((T2_PM + 1) % 2)
            return ps[:, (slot, slot + 1, 5, 7)[g], :]

        def tokens(ap, kind):
            return ap.rearrange("p (a b) -> p a b", a=2) if kind == ALL else ap

        def flat(bank):
            return ps[:, bank:bank + 2, :].rearrange("p a b -> p (a b)")

        def width(kind):
            return S2 if kind == ALL else S1

        def raw_half(p_slot, half, kt, n):
            return raw[:, p_slot, 0:kt * n * P].rearrange("p (k n) -> p k n", k=kt)[
                :, :, half * P:(half + 1) * P]

        def raw_slab(t):
            p, half, kt, n = slab[t]
            return raw_half(p % 2, half, kt, n)

        def w_slab(w, slot, kt):
            return w[:, slot, 0:kt * P].rearrange("p (k n) -> p k n", k=kt)

        def dil_groups(n):
            nb0 = 1 if n == 0 else 2
            return [(P * (n + 1 - nb0), nb0, 0), (0, n + 1, nb0 * P), (0, n + 1, (nb0 + n + 1) * P)]

        def pt_blocks(u, g):
            if u % 2 == 0:
                return PT[:, (0, 2, 6)[g]:(2, 6, 10)[g], :]
            v = (SQ[:, 0, 0:2 * P], F[:, 0, 0:4 * P], F[:, 1, 0:4 * P])[g]
            return v.rearrange("p (a b) -> p a b", b=P)

        def level_ref(y):
            l, j = y // 2, y % 2
            c0 = 1 if l < len(LEVELS) else 0
            b = LEVELS[l] if l < len(LEVELS) else CH
            at = b // 2 - 1 if l < len(LEVELS) else CH - 1
            v = bS[:, j, c0 * CH:(c0 + 8) * CH].rearrange("p (a b) -> p a b", b=b)
            return v, v[:, :, at:at + 1].to_broadcast([P, S1 // b, b]), b

        U_DIAG, U_END, U_START = 2 * len(LEVELS), 2 * len(LEVELS) + 2, 2 * len(LEVELS) + 4
        def exp_no(y):
            return y if y < U_DIAG else y - 2
        NORMED, HIDDEN = {ONE: (Bh, Bl), REAL: (Ah, Al)}, {ONE: (Ah, Al), REAL: (Bh, Bl)}
        MLPS = {ONE: (T_MLP, N_HID, first_mlp), REAL: (T2_MLP, N2_HID, second_mlp)}

        block = ctx.enter_context(nc.Block())

        @block.sync
        def _(sp):
            def load_x(i):
                at = slice(i * 256, (i + 1) * 256)
                sp.dma_start(xnat[:, :, at], d["x"][0].rearrange("(a p) d -> p a d", p=P)[:, :, at])\
                  .then_inc(x_in[i], 16)

            def params():
                row = 0
                for name, n in (("norm_mlp_g", 8), ("norm_final_g", 8), ("norm_mix_2", 8),
                                ("norm_ffn_2", 8), ("norm_final_2", 8), ("b_gate", 16), ("b_gate_2", 2),
                                ("pool_scale_2", 4), ("gla_norm_2", 4)):
                    v = d[name] if len(d[name].shape) == 1 else d[name][0]
                    sp.dma_start(vrow[row:row + n, :], v.rearrange("(a b) -> a b", b=P)).then_inc(params_in, 16)
                    row += n
                sp.dma_start(mnat[0:META, :], d["meta_tokens_2"]).then_inc(params_in, 16)
                sp.dma_start(wgu[:, :], d["w_gate_up_2"][0]).then_inc(params_in, 16)

            def load(p):
                name, at, kt, n, t = loads[p]
                if p >= 2:
                    sp.wait_ge(lo_ready, loads[p - 2][4] + loads[p - 2][3])
                view = weight_view(name, at, kt, n * P)
                sp.dma_start(raw[:, p % 2, 0:kt * n * P].rearrange("p (k n) -> p k n", k=kt), view)\
                  .then_inc(w_landed[p % 2], 16)

            def mlp_loads(which, w1, w2):
                t0, _, p0 = MLPS[which]
                with sp.Fori(0, CHUNKS - 1) as c:
                    for i in range(8):
                        sp.wait_ge(lo_ready, t0 + 16 * c + 2 * i - 2)
                        if i < 4:
                            src = w1[:, bass.ds(c * DM + i * 256, 256)]
                        else:
                            src = w2[bass.ds(c * DM, DM), (i - 4) * 256:(i - 3) * 256]
                        sp.dma_start(raw[:, (p0 + i) % 2, :].rearrange("p (k n) -> p k n", k=KT),
                                     src.rearrange("(k p) n -> p k n", p=P))\
                          .then_inc(w_landed[(p0 + i) % 2], 16)

            sp.dma_start(grow[0:KT, :], d["norm_mix_g"][0].rearrange("(a b) -> a b", b=P)).then_inc(gain_in, 16)
            load_x(0)
            load_x(1)
            load(0)
            load_x(2)
            load_x(3)
            load(1)
            params()
            for p in range(2, first_mlp):
                load(p)
            mlp_loads(ONE, d["w_mlp_in"][0], d["w_mlp_out"][0])
            for p in range(first_mlp + 8 * (CHUNKS - 1), second_mlp):
                load(p)
            mlp_loads(REAL, d["w_ff1_2"][0], d["w_ff2_2"][0])
            for p in range(second_mlp + 8 * (CHUNKS - 1), len(loads)):
                load(p)
            for a in range(4):
                sp.wait_ge(y_low, a + 1)
                sp.wait_ge(y_high, a + 1)
                sp.dma_start(d["out"][0, a * P:(a + 1) * P, :], ON[:, a, :]).then_inc(out_done, 16)
            sp.wait_ge(out_done, 64)

        @block.gpsimd
        def _(pool):
            step = 0

            def after(ins):
                nonlocal step
                step += 1
                ins.then_inc(pool_step, 1)
                pool.wait_ge(pool_step, step)

            after(pool.memset(ident[:, :], 0.0))
            pool.memset(ones[:, :], 1.0).then_inc(consts_ready, 1)
            pool.affine_select(out=ident[:, :], in_=ident[:, :], compare_op=ALU.not_equal, fill=1.0, base=0,
                               pattern=[[-1, P]], channel_multiplier=1).then_inc(consts_ready, 1)
            pool.iota(DI, pattern=[[-1, 512]], base=384, channel_multiplier=1).then_inc(di_ready, 1)
            after(pool.memset(SBM, 0.0))
            pool.affine_select(out=SBM, in_=SBM, compare_op=ALU.is_gt, fill=NEG, base=384,
                               pattern=[[-1, 512]], channel_multiplier=1).then_inc(bias_ready, 1)
            def add_squares(norm, kind):
                w = width(kind)
                if norm >= 1:
                    pool.wait_ge(stat_done, norm)
                for m in range(KT - 1):
                    f = 8 * norm + m
                    pool.wait_ge(sq_ready, f + 1)
                    if m == 0:
                        pool.tensor_copy(SS[:, 0:w], SQ[:, f % 2, 0:w]).then_inc(ss_done, 1)
                    else:
                        pool.wait_ge(ss_done, f)
                        pool.tensor_tensor(SS[:, 0:w], SS[:, 0:w], SQ[:, f % 2, 0:w], ALU.add).then_inc(ss_done, 1)

            add_squares(0, ONE)
            pool.wait_ge(dist_raw, 3)
            for dist, base, n in ((D1, 384, 512), (D2, 384, 512)):
                pool.affine_select(out=dist, in_=dist, compare_op=ALU.is_ge, fill=NEG, base=base,
                                   pattern=[[-1, n]], channel_multiplier=1).then_inc(bias_ready, 1)
            after(pool.affine_select(out=D0, in_=D0, compare_op=ALU.is_ge, fill=NEG, base=128,
                                     pattern=[[-1, 256]], channel_multiplier=1))
            pool.affine_select(out=D0, in_=D0, compare_op=ALU.is_ge, fill=NEG, base=0,
                               pattern=[[1, 256]], channel_multiplier=-1).then_inc(bias_ready, 1)
            after(pool.memset(masks[:, :, :], 1.0))
            for i, b in enumerate((32, 16, 8, 4, 2, 1)):
                for h in range(2):
                    v = masks[64 * h:64 * h + 64, i, :].rearrange("p (a b) -> p a b", b=b)
                    after(pool.affine_select(out=v, in_=v, compare_op=ALU.is_ge, fill=0.0, base=0,
                                             pattern=[[-b, CH // b], [0, b]], channel_multiplier=1))
                    after(pool.affine_select(out=v, in_=v, compare_op=ALU.is_ge, fill=0.0, base=b - 1,
                                             pattern=[[b, CH // b], [0, b]], channel_multiplier=-1))
            add_squares(1, ONE)
            pool.wait_ge(act_ready, N_MERGE + 8)
            pool.memset(k2[:, :, 0:PAD], 0.0)
            pool.memset(la[:, :, 0:PAD], 0.0)
            pool.memset(v2[:, :, 0:PAD], 0.0)
            after(pool.memset(reset, 1.0))
            pool.memset(reset.rearrange("p (a b) -> p a b", b=CH)[:, :, 0:1], 0.0).then_inc(zeros2_ready, 1)
            pool.wait_ge(meta_copied, 1)
            g2 = vecT[:, G_MIX2:G_MIX2 + KT]
            pool.tensor_tensor(gain2, vecT[:, G_FIN:G_FIN + KT], g2, ALU.mult)
            pool.tensor_tensor(meta2, X[:, :, 0:META], g2.unsqueeze(2).to_broadcast([P, KT, META]), ALU.mult)\
                .then_inc(gain2_ready, 1)
            after(pool.tensor_tensor(msq, X[:, :, 0:META], X[:, :, 0:META], ALU.mult))
            after(pool.tensor_tensor(msq[:, 0:4, :], msq[:, 0:4, :], msq[:, 4:8, :], ALU.add))
            after(pool.tensor_tensor(msq[:, 0:2, :], msq[:, 0:2, :], msq[:, 2:4, :], ALU.add))
            pool.tensor_tensor(SS2[:, 0:META], msq[:, 0, :], msq[:, 1, :], ALU.add).then_inc(meta_sum, 1)
            pool.wait_ge(stat_done, 2)
            for m in range(KT - 1):
                f = 16 + m
                pool.wait_ge(sq_ready, f + 1)
                if m == 0:
                    pool.tensor_copy(SS[:, 0:S1], SQ[:, f % 2, 0:S1]).then_inc(ss_done, 1)
                else:
                    pool.wait_ge(ss_done, f)
                    pool.tensor_tensor(SS[:, 0:S1], SS[:, 0:S1], SQ[:, f % 2, 0:S1], ALU.add).then_inc(ss_done, 1)
                pool.wait_ge(sq2_ready, m + 1)
                if m == 0:
                    pool.tensor_copy(SS2[:, META:S2], SQ2[:, 0, :]).then_inc(ss2_done, 1)
                else:
                    pool.wait_ge(ss2_done, m)
                    pool.tensor_tensor(SS2[:, META:S2], SS2[:, META:S2], SQ2[:, m % 2, :], ALU.add)\
                        .then_inc(ss2_done, 1)
            done = 0
            for g in range(4):
                pool.wait_ge(evac_done, T2_A + g + 1)
                if g >= 1:
                    pool.wait_ge(f_ready, staged(N2_POOL + g - 1))
                else:
                    pool.wait_ge(ss2_done, 8)
                cur = apad[:, g % 2, :]
                for k in range(g + 1):
                    s = 2 ** k
                    nxt = wsum[:, k % 2, 0:S2]
                    lo = 2 * s - 1 if k < g else META
                    pool.tensor_tensor(nxt[:, lo:], cur[:, lo:], cur[:, lo - s:S2 - s], ALU.add)\
                        .then_inc(win_done, 1)
                    done += 1
                    pool.wait_ge(win_done, done)
                    cur = nxt
            add_squares(3, REAL)
            add_squares(4, REAL)

        @block.scalar
        def _(act):
            def convert(t):
                if t >= T_END:
                    return
                p, half, kt, n = slab[t]
                if half == 0:
                    act.wait_ge(w_landed[p % 2], 16 * (p // 2 + 1))
                if t >= 2:
                    act.wait_ge(slab_done, t - 1)
                act.activation(w_slab(wh, t % 2, kt), raw_slab(t), ACT.Copy).then_inc(hi_ready, 1)

            def split(n, dst, src):
                act.wait_ge(f_ready, staged(n))
                act.activation(dst, src, ACT.Copy).then_inc(hi_split, 1)

            def square(norm, m, kind):
                f = 8 * norm + m
                if f >= 2:
                    act.wait_ge(ss_done, f - 1)
                src = X[:, m, S2 - width(kind):S2]
                act.activation(SQ[:, f % 2, 0:width(kind)], src, ACT.Square).then_inc(sq_ready, 1)

            def feed(norm, n, m, col, kind, dst=None, ready=None):
                if ready is not None:
                    ready()
                if m == KT - 1:
                    square(norm, m, kind)
                act.activation((Ah if dst is None else dst)[:, m, 0:width(kind)], X[:, m, S2 - width(kind):S2],
                               ACT.Copy, scale=vecT[:, col + m:col + m + 1]).then_inc(hi_split, 1)
                if m < KT - 1:
                    square(norm, m, kind)

            def stats(norm):
                act.wait_ge(ms_ready, norm + 1)
                act.activation(RS[:, 0:S1], RS[:, 0:S1], ACT.Sqrt).then_inc(sqrt_ready, 1)

            def gate(t, g, col=None):
                act.wait_ge(evac_done, t + 1)
                act.activation(g, g, ACT.Tanh, bias=halfb[:, col:col + 1] if col is not None else 0.0,
                               scale=0.5).then_inc(gate_done, 1)

            def mlp_chunk(which, c, last):
                t0, n0, p0 = MLPS[which]
                w = width(which)
                for j in range(16):
                    t = t0 + j

                    def weights():
                        if last and j >= 14:
                            convert(t + 16 * c + 2)
                        else:
                            i = (j + 2) // 2
                            if j % 2 == 0:
                                act.wait_ge(w_landed[(p0 + i) % 2], (p0 + i) // 2 * 16 + 16 + 64 * c)
                            act.wait_ge(slab_done, t + 16 * c + 1)
                            act.activation(w_slab(wh, t % 2, KT), raw_half((p0 + i) % 2, j % 2, KT, 2), ACT.Copy)\
                               .then_inc(hi_ready, 1)

                    if j < 7:
                        weights()
                    if j < 8:
                        act.wait_ge(f_ready, staged(n0) + 8 * c + j)
                        act.activation(HIDDEN[which][0][:, j, 0:w], F[:, (n0 + j) % 2, 0:w], ACT.Copy)\
                           .then_inc(hi_split, 1)
                    elif last:
                        m = j - 8
                        act.wait_ge(evac_done, t + 16 * c + 1)
                        square(2 if which == ONE else 4, m, which)
                        if which == ONE:
                            x = X[:, m, META:S2]
                            if m >= 2:
                                act.wait_ge(ss2_done, m - 1)
                            else:
                                act.wait_ge(gain2_ready, 1)
                            act.activation(SQ2[:, m % 2, :], x, ACT.Square, scale=vecT[:, G_FIN + m:G_FIN + m + 1])\
                               .then_inc(sq2_ready, 1)
                            act.activation(Bh[:, m, META:S2], x, ACT.Copy, scale=gain2[:, m:m + 1])\
                               .then_inc(hi_split, 1)
                            if m == 0:
                                act.activation(Bh[:, :, 0:META], meta2, ACT.Copy).then_inc(meta_hi, 1)
                        else:
                            act.activation(Y[:, m, :], X[:, m, META:S2], ACT.Copy,
                                           scale=vecT[:, G_FIN2 + m:G_FIN2 + m + 1]).then_inc(y_ready, 1)
                            if m == 4:
                                act.wait_ge(y_psum, 4)
                                for a in range(4):
                                    act.activation(ON[:, a, 0:512], ps[:, Y_BANKS[a], :], ACT.Copy)\
                                       .then_inc(y_copied, 1)
                    if j >= 7:
                        weights()

            def mlp(which):
                with act.Fori(0, CHUNKS - 1) as c:
                    mlp_chunk(which, c, False)
                mlp_chunk(which, CHUNKS - 1, True)

            act.preload_act_table(ACT.Sqrt)
            act.wait_ge(gain_ready, 1)
            for m in range(KT):
                feed(0, N_MIX + m, m, G_MIX, ONE, ready=lambda: act.wait_ge(xt_copied, m + 1))
                if m in (2, 4):
                    convert(m // 2 - 1)
            convert(2)
            convert(3)
            stats(0)

            def v_copy(i, dst):
                act.wait_ge(vtrans_done, i + 1)
                act.activation(dst, ps[:, 6 + i % 2, :].rearrange("p (a b) -> p a b", a=4), ACT.Copy)\
                   .then_inc(vnat_copied, 1)

            for t in range(T_QKV_A + 3, T_GATE_A):
                convert(t + 1)
                if t == T_QKV_A + 9:
                    act.wait_ge(vec_ready, 1)
                    act.activation(halfb[:, :], vecT[:, B_GATE:B_GATE + 16], ACT.Copy, scale=0.5)\
                       .then_inc(halfb_ready, 1)
                if t >= T_QKV_A + 14:
                    v_copy(t - 14, Vna[:, :, (t - 14) * P:(t - 13) * P])
            for i in (4, 5):
                v_copy(i, Vna[:, :, i * P:(i + 1) * P])

            act.wait_ge(halfb_ready, 1)

            def dil_exp(u):
                ncol = sum(g[1] for g in dil_groups(u // 4)) * P
                act.wait_ge(negmax_ready, u + 1)
                act.activation(Lg[:, u % 2, 0:ncol], Lg[:, u % 2, 0:ncol], ACT.Exp, bias=stat[:, 1, u:u + 1],
                               scale=0.125, accum_out=stat[:, 2, u:u + 1]).then_inc(probs_ready, 1)

            def dil_copy(u):
                if u >= 2:
                    act.wait_ge(pv_done, u - 1)
                for g, (_, nb, col) in enumerate(dil_groups(u // 4)):
                    act.wait_ge(pt_psum, 3 * u + g + 1)
                    act.activation(pt_blocks(u, g)[:, 0:nb, :],
                                   ps[:, 5 + (3 * u + g) % 2, 0:nb * P].rearrange("p (a b) -> p a b", a=nb), ACT.Copy)\
                       .then_inc(pt_copied, 1)

            def oa_hi_copy(n):
                act.wait_ge(oT_psum, n + 1)
                act.activation(Bh[:, 0:2, n * P:(n + 1) * P],
                               ps[:, 7, 256:512].rearrange("p (a b) -> p a b", a=2), ACT.Copy).then_inc(oa_hi, 1)

            for u in range(DIL_STEPS):
                if u >= 16:
                    convert(T_QKV_B + u - 16 + 1)
                elif u % 2 == 0:
                    convert(T_GATE_A + u // 2 + 1)
                if u >= 8 and u % 4 == 0:
                    oa_hi_copy(u // 4 - 2)
                if 0 <= u - 2 < 16:
                    dil_copy(u - 2)
                if 0 <= u - 1 < 16:
                    dil_exp(u - 1)
                if u % 2 == 0 and 2 <= u <= 16:
                    s = u // 2
                    gate(T_GATE_A + s - 1, GA[:, s - 1, :], s - 1)

            for t in range(T_QKV_B + DIL_STEPS - 16, T_GATE_B):
                convert(t + 1)
                i = t - T_QKV_B - 8 - 2
                if i >= 0:
                    v_copy(6 + i, Vnb[:, :, i * P:(i + 1) * P])
            for i in (2, 3):
                v_copy(6 + i, Vnb[:, :, i * P:(i + 1) * P])

            def sb_ln_chain(w):
                e = Es[:, w % 2, 0:P * (w // 8 + 1)]
                act.wait_ge(z_done, w + 1)
                if w >= 2:
                    act.wait_ge(sb_scan, w - 1)
                act.activation(e, Zs[:, w % 2, 0:P * (w // 8 + 1)], ACT.Abs).then_inc(sb_abs, 1)
                act.wait_ge(sb_abs, w + 1)
                act.activation(e, e, ACT.Exp, scale=-1.0).then_inc(sb_exp, 1)
                act.wait_ge(sb_exp, w + 1)
                act.activation(e, e, ACT.Ln, bias=1.0).then_inc(sb_ln, 1)

            def sb_prob(w):
                act.wait_ge(sb_la, w + 1)
                c = Cs[:, w % 2, 0:P * (w // 8 + 1)]
                act.activation(c, c, ACT.Exp).then_inc(sb_probs, 1)

            def sb_copy(w):
                act.wait_ge(sb_pt_psum, w + 1)
                if w >= 2:
                    act.wait_ge(sb_pv, w - 1)
                nk = P * (w // 8 + 1)
                act.activation(PTb[:, w % 2, 0:nk], ps[:, 4 + w % 2, 0:nk], ACT.Copy).then_inc(sb_pt_copied, 1)

            def sb_out(n):
                act.wait_ge(sb_pv, 8 * n + 8)
                if n >= 1:
                    act.wait_ge(obT_psum, n)
                act.activation(onatb, ps[:, 6, :], ACT.Copy).then_inc(ob_nat, 1)

            def ob_hi_copy(n):
                act.wait_ge(obT_psum, n + 1)
                act.activation(Bh[:, 2:6, n * P:(n + 1) * P],
                               ps[:, 7, :].rearrange("p (a b) -> p a b", a=4), ACT.Copy).then_inc(ob_hi, 1)

            act.preload_act_table_set(EXP_LN_SET)
            for i in range(SB_STEPS):
                if i % 4 == 0 and i < 32:
                    convert(T_GATE_B + i // 4 + 1)
                elif i >= 32:
                    convert(T_UP_A + i - 32 + 1)
                if i >= 12 and (i - 12) % 8 == 0:
                    sb_out((i - 12) // 8)
                if 0 <= i - 4 < 32:
                    sb_copy(i - 4)
                if 0 <= i - 1 < 32:
                    sb_ln_chain(i - 1)
                if 0 <= i - 2 < 32:
                    sb_prob(i - 2)
                if i >= 13 and (i - 13) % 8 == 0:
                    ob_hi_copy((i - 13) // 8)

            for t in range(T_UP_A + SB_STEPS - 32, T_UP_B + 1):
                convert(t + 1)
            for m in range(2):
                gate(T_GATE_B + m, GB[:, m, :], 8 + m)
            for m in range(KT):
                convert(T_UP_B + m + 2)
                if m + 2 < KT:
                    gate(T_GATE_B + m + 2, GB[:, m + 2, :], 8 + m + 2)
                split(N_MERGE + m, Ah[:, m, 0:S1], F[:, (N_MERGE + m) % 2, 0:S1])
            act.preload_act_table(ACT.Sqrt)
            for m in range(KT):
                if m >= 1:
                    convert(T_OUT + m + 1)
                feed(1, N_MLP + m, m, G_MLP, ONE, Bh, lambda: act.wait_ge(evac_done, T_OUT + m + 1))
            convert(T_MLP + 1)
            stats(1)
            mlp(ONE)

            def decay_exp():
                act.preload_act_table_set(EXP_LN_SET)
                for j in range(2):
                    u, e = UU[:, j, :], E2
                    act.wait_ge(u_ready, j + 1)
                    if j == 1:
                        act.wait_ge(la_ready, 1)
                    act.activation(e, u, ACT.Abs).then_inc(u_abs, 1)
                    act.wait_ge(u_abs, j + 1)
                    act.activation(e, e, ACT.Exp, scale=-1.0).then_inc(u_exp, 1)
                    act.wait_ge(u_exp, j + 1)
                    act.activation(e, e, ACT.Ln, bias=1.0).then_inc(u_ln, 1)
                for j in range(2):
                    act.wait_ge(bs_ready, j + 1)
                    act.activation(ebe[:, j, :], bS[:, j, CH - 1:PADL:CH], ACT.Exp, scale=1.0 / TAU)\
                       .then_inc(ebe_ready, 1)

            def job(what):
                kind = what[0]
                if kind == "decay":
                    decay_exp()
                elif kind == "v_rows":
                    h = what[1]
                    for g, (c0, nc_) in enumerate(((0, 4), (4, 4), (8, 1))):
                        act.wait_ge(vr_psum, 3 * h + g + 1)
                        beta = 64 * (h % 2)
                        act.activation(Vn[beta:beta + 64, h // 2, c0 * P:(c0 + nc_) * P],
                                       ps[beta:beta + 64, 5 + 2 * ((3 * h + g) % 2), 0:nc_ * P], ACT.Copy)\
                           .then_inc(vr_copied, 1)
                elif kind == "unit_d":
                    y = what[1]
                    l, j = y // 2, y % 2
                    if l == U_DIAG // 2:
                        return
                    x = exp_no(y)
                    e = Ed[:, x % 2, :]
                    if y < U_START:
                        act.wait_ge(d_ready, x + 1)
                        act.activation(e, e, ACT.Abs).then_inc(d_abs, 1)
                        act.wait_ge(d_abs, x + 1)
                        act.activation(e, e, ACT.Exp, scale=-1.0 / TAU).then_inc(d_exp, 1)
                    else:
                        act.wait_ge(qk_ready, y - 2 + 1)
                        act.activation(e, bS[:, j, CH:], ACT.Exp, scale=1.0 / TAU).then_inc(d_exp, 1)
                elif kind == "unit_mm":
                    y = what[1]
                    if U_END <= y < U_START:
                        j = y - U_END
                        act.wait_ge(kn_psum, j + 1)
                        act.activation(Kn[:, j, :], ps[:, 4 + 2 * j, :], ACT.Copy).then_inc(kn_copied, 1)
                elif kind == "o_mm":
                    h = what[1]
                    act.wait_ge(o_copied, h + 1)
                    if h >= 1:
                        act.wait_ge(o_stat, h)
                    act.activation(osb2, osb[:, h % 2, :], ACT.Square).then_inc(o_sq, 1)
                elif kind == "o_stat":
                    h = what[1]
                    act.wait_ge(o_ms, h + 1)
                    act.activation(SQ[:, h % 2, 0:S1], SQ[:, h % 2, 0:S1], ACT.Sqrt).then_inc(o_sqrt, 1)
                elif kind == "o_norm":
                    h = what[1]
                    n = N2_O + h
                    split(n, Ah[:, h, 0:S1], F[:, n % 2, 0:S1])
                elif kind == "pool_split":
                    g = what[1]
                    n = N2_POOL + g
                    split(n, Ah[:, g, 0:S1], F[:, n % 2, 0:S1])

            def evac(t):
                if t == T2_PM:
                    for g in range(4):
                        n = N2_PM + g
                        split(n, Ah[:, 4 + g, 0:S1], F[:, n % 2, 0:S1])
                elif T2_R <= t < T2_PM:
                    i = t - T2_R
                    act.wait_ge(evac_done, t + 1)
                    if i >= 2:
                        act.wait_ge(silu_done, i - 1)
                    act.activation(G2[:, i % 2, :], sr[:, i, :], ACT.Tanh, scale=0.5).then_inc(silu_tanh, 1)
                elif T2_GY <= t < T2_GB and (t - T2_GY) % 4 < 2:
                    gate(t, G2[:, (t - T2_GY) % 2, :])
                elif T2_GB <= t < T2_GO:
                    gate(t, GB2[:, t - T2_GB, :])
                elif T2_GO <= t < T2_OUT:
                    n = N2_M + t - T2_GO
                    if t == T2_GO:
                        act.wait_ge(slab_done, T2_GO)
                    split(n, Bh[:, t - T2_GO, 0:S1], F[:, n % 2, 0:S1])

            for t in range(T2, T2_OUT):
                if t > T2:
                    convert(t + 1)
                if t == T2:
                    act.wait_ge(ms_ready, 3)
                    act.activation(RS[:, :], RS[:, :], ACT.Sqrt).then_inc(sqrt_ready, 1)
                    act.activation(RS1, RS1, ACT.Sqrt).then_inc(sqrt1_ready, 1)
                if t > T2:
                    evac(t - 1)
                for what in between[t]:
                    job(what)
            evac(T2_OUT - 1)
            for m in range(KT):
                convert(T2_OUT + m + 1)
                feed(3, N2_FFN + m, m, G_FFN2, REAL, Ah, lambda: act.wait_ge(evac_done, T2_OUT + m + 1))
            convert(T2_MLP + 1)
            stats(3)
            mlp(REAL)
            act.wait_ge(ms_ready, 5)
            act.activation(r_tok, r_tok, ACT.Sqrt).then_inc(sqrt_ready, 1)
            act.wait_ge(rstd_ready, 5)
            act.wait_ge(y_psum, KT)
            for a in range(4):
                act.activation(ON[:, a, 512:1024], ps[:, Y_BANKS[a], :], ACT.Copy, scale=r_tok[:, a:a + 1])\
                   .then_inc(y_high, 1)

        @block.vector
        def _(dve):
            def convert(t):
                if t >= T_END:
                    return
                kt = slab[t][2]
                dve.wait_ge(hi_ready, t + 1)
                dve.tensor_tensor(w_slab(wl, t % 2, kt), raw_slab(t), w_slab(wh, t % 2, kt), ALU.subtract)\
                   .then_inc(lo_ready, 1)

            def split(n, lo, src, hi):
                dve.wait_ge(hi_split, n + 1)
                dve.tensor_tensor(lo, src, hi, ALU.subtract).then_inc(act_ready, 1)

            def add_square(norm, m, kind):
                w = width(kind)
                f = 8 * norm + m
                dve.wait_ge(sq_ready, f + 1)
                dve.wait_ge(ss_done, f)
                dve.tensor_tensor(SS[:, 0:w], SS[:, 0:w], SQ[:, f % 2, 0:w], ALU.add).then_inc(ss_done, 1)

            def feed(norm, n, m, col, kind, hi=None, lo=None):
                w = width(kind)
                hi, lo = (Ah, Al) if hi is None else (hi, lo)
                if m == KT - 1:
                    add_square(norm, m, kind)
                dve.wait_ge(hi_split, n + 1)
                dve.scalar_tensor_tensor(out=lo[:, m, 0:w], in0=X[:, m, S2 - w:S2], scalar=vecT[:, col + m:col + m + 1],
                                         in1=hi[:, m, 0:w], op0=ALU.mult, op1=ALU.subtract).then_inc(act_ready, 1)

            def stats(norm):
                dve.wait_ge(stat_done, norm + 1)
                dve.tensor_scalar(RS[:, 0:S1], ps[:, 7, :], 1.0 / DM, EPS, ALU.mult, ALU.add).then_inc(ms_ready, 1)
                dve.wait_ge(sqrt_ready, norm + 1)
                dve.reciprocal(RS[:, 0:S1], RS[:, 0:S1]).then_inc(rstd_ready, 1)
                dve.wait_ge(rstd_ready, norm + 1)

            def scaled(t, dst, kind, rows=P):
                scale = RS[0:rows, META:S2] if kind == REAL else RS[0:rows, 0:width(kind)]
                dve.wait_ge(slab_done, t + 1)
                dve.tensor_tensor(tokens(dst, kind), dense_psum(t, kind)[0:rows], tokens(scale, kind), ALU.mult)\
                   .then_inc(evac_done, 1)

            def gated(t, no, g, dst, kind):
                dve.wait_ge(slab_done, t + 1)
                dve.wait_ge(gate_done, no + 1)
                dve.scalar_tensor_tensor(out=dst, in0=g, scalar=1.0, in1=dense_psum(t, kind),
                                         op0=ALU.add, op1=ALU.mult).then_inc(evac_done, 1)

            def add_half(t, m, kind):
                dve.wait_ge(slab_done, t + 1)
                x = X[:, m, META:S2]
                dve.scalar_tensor_tensor(out=x, in0=dense_psum(t, kind), scalar=0.5, in1=x,
                                         op0=ALU.mult, op1=ALU.add).then_inc(evac_done, 1)

            def add_residual(t, ps_t, m, kind):
                dve.wait_ge(slab_done, t + 1)
                dve.tensor_tensor(X[:, m, META:S2], X[:, m, META:S2], dense_psum(ps_t, kind), ALU.add)\
                   .then_inc(evac_done, 1)

            def mlp_chunk(which, c, last):
                t0, n0, p0 = MLPS[which]
                w = width(which)
                for j in range(16):
                    t = t0 + j

                    def weights():
                        if last and j >= 14:
                            convert(t + 16 * c + 2)
                        else:
                            dve.wait_ge(hi_ready, t + 16 * c + 3)
                            dve.tensor_tensor(w_slab(wl, t % 2, KT), raw_half((p0 + (j + 2) // 2) % 2, j % 2, KT, 2),
                                              w_slab(wh, t % 2, KT), ALU.subtract).then_inc(lo_ready, 1)

                    if j < 7:
                        weights()
                    if j < 8:
                        f = F[:, (n0 + j) % 2, 0:w]
                        dve.wait_ge(slab_done, t + 16 * c + 1)
                        dve.tensor_tensor(f, dense_psum(t, which), RS[:, 0:w], ALU.mult).then_inc(evac_done, 1)
                        dve.wait_ge(evac_done, t + 16 * c + 1)
                        dve.scalar_tensor_tensor(out=f, in0=f, scalar=0.0, in1=f, op0=ALU.max, op1=ALU.mult)\
                           .then_inc(f_ready, 1)
                        dve.wait_ge(hi_split, n0 + 8 * c + (j + 1))
                        dve.tensor_tensor(HIDDEN[which][1][:, j, 0:w], f, HIDDEN[which][0][:, j, 0:w], ALU.subtract)\
                           .then_inc(act_ready, 1)
                    else:
                        add_residual(t + 16 * c, t, j - 8, which)
                        if last:
                            m = j - 8
                            if m == KT - 1:
                                add_square(2 if which == ONE else 4, m, which)
                            if which == ONE:
                                if m == KT - 1:
                                    dve.wait_ge(sq2_ready, KT)
                                    dve.wait_ge(ss2_done, m)
                                    dve.wait_ge(meta_sum, 1)
                                    dve.tensor_tensor(SS2[:, META:S2], SS2[:, META:S2], SQ2[:, m % 2, :], ALU.add)\
                                       .then_inc(ss2_done, 1)
                                dve.wait_ge(hi_split, N2_MIX + m + 1)
                                dve.scalar_tensor_tensor(out=Bl[:, m, META:S2], in0=X[:, m, META:S2],
                                                         scalar=gain2[:, m:m + 1], in1=Bh[:, m, META:S2],
                                                         op0=ALU.mult, op1=ALU.subtract).then_inc(act_ready, 1)
                                if m == 0:
                                    dve.wait_ge(meta_hi, 1)
                                    dve.tensor_tensor(Bl[:, :, 0:META], meta2, Bh[:, :, 0:META], ALU.subtract)\
                                       .then_inc(meta_split, 1)
                    if j >= 7:
                        weights()

            def mlp(which):
                with dve.Fori(0, CHUNKS - 1) as c:
                    mlp_chunk(which, c, False)
                mlp_chunk(which, CHUNKS - 1, True)

            def vectors_and_distances():
                dve.wait_ge(di_ready, 1)
                for i, (dist, dil) in enumerate(((D1, 4), (D2, 16))):
                    dve.tensor_scalar(DM4, DI, dil - 1, None, ALU.bitwise_and).then_inc(dist_step, 1)
                    dve.wait_ge(dist_step, 2 * i + 1)
                    dve.tensor_scalar(PEN, DM4, 0.0, NEG, ALU.is_gt, ALU.mult).then_inc(dist_step, 1)
                    dve.wait_ge(dist_step, 2 * i + 2)
                    dve.scalar_tensor_tensor(out=dist, in0=DI, scalar=-1.0, in1=PEN, op0=ALU.mult, op1=ALU.add)\
                       .then_inc(dist_raw, 1)
                    dve.wait_ge(dist_raw, i + 1)
                dve.tensor_scalar(D0, DI[:, 256:512], -1.0, None, ALU.mult).then_inc(dist_raw, 1)
                dve.wait_ge(vec_psum, 1)
                dve.tensor_copy(vecT[:, 0:G_MIX], ps[:, 5, 0:G_MIX]).then_inc(vec_ready, 1)
                dve.wait_ge(meta_psum, 1)
                dve.tensor_copy(X[:, :, 0:META], ps[:, 4, 0:KT * META].rearrange("p (a b) -> p a b", a=KT))\
                   .then_inc(meta_copied, 1)
                dve.wait_ge(vec_ready, 1)

            dve.wait_ge(gain_psum, 1)
            dve.tensor_copy(vecT[:, G_MIX:G_MIX + KT], ps[:, 5, 0:KT]).then_inc(gain_ready, 1)
            dve.wait_ge(gain_ready, 1)
            for m in range(KT):
                dve.wait_ge(xt_psum, m + 1)
                dve.tensor_copy(X[:, m, META:S2], ps[:, (2, 3, 6, 7)[m % 4], :]).then_inc(xt_copied, 1)
                if m >= 1:
                    feed(0, N_MIX + m - 1, m - 1, G_MIX, ONE)
                if m in (3, 5):
                    convert(m // 2 - 1)
            feed(0, N_MIX + KT - 1, KT - 1, G_MIX, ONE)

            def qkv_a(t):
                i = t - T_QKV_A
                if i >= 14:
                    dve.wait_ge(vtrans_done, i - 13)
                return qa[:, i, :] if i < 6 else ka[:, i - 6, :] if i < 12 else vt[:, i % 2, :]

            for t in (0, 1):
                dve.wait_ge(slab_done, t + 1)
                dve.tensor_copy(qkv_a(t), dense_psum(t, ONE)).then_inc(evac_done, 1)
                convert(t + 2)
            stats(0)
            for t in (0, 1):
                dve.tensor_tensor(qkv_a(t), qkv_a(t), RS[:, 0:S1], ALU.mult).then_inc(late_scaled, 1)
            for t in range(T_QKV_A + 3, T_GATE_A + 1):
                scaled(t - 1, qkv_a(t - 1), ONE)
                if t < T_GATE_A:
                    convert(t + 1)
                if t == T_QKV_A + 7:
                    vectors_and_distances()

            def dil_softmax(u):
                n, j = u // 4, u % 4
                groups = dil_groups(n)
                dve.wait_ge(scores_done, u + 1)
                if u >= 2:
                    dve.wait_ge(pt_psum, 3 * (u - 1))
                for g, (k0, nb, col) in enumerate(groups):
                    dist = (D0, D1, D2)[g]
                    w = nb * P
                    dve.scalar_tensor_tensor(out=Lg[:, u % 2, col:col + w], in0=dist[:, dist.shape[1] - w:],
                                             scalar=8.0 * SLOPES[4 * g + j], in1=ps[:, 2 + g, 0:w],
                                             op0=ALU.mult, op1=ALU.add).then_inc(logits_done, 1)
                dve.wait_ge(logits_done, 3 * u + 3)
                ncol = sum(g[1] for g in groups) * P
                dve.tensor_reduce(stat[:, 0, u:u + 1], Lg[:, u % 2, 0:ncol], AX_X, ALU.max).then_inc(max_done, 1)
                dve.wait_ge(max_done, u + 1)
                dve.tensor_scalar(stat[:, 1, u:u + 1], stat[:, 0, u:u + 1], -0.125, None, ALU.mult)\
                   .then_inc(negmax_ready, 1)

            def dil_norm(u):
                n, j = u // 4, u % 4
                dve.wait_ge(probs_ready, u + 1)
                dve.reciprocal(stat[:, 3, u:u + 1], stat[:, 2, u:u + 1]).then_inc(rden_done, 1)
                dve.wait_ge(rden_done, u + 1)
                dve.wait_ge(pv_done, u + 1)
                if j == 0 and n >= 2:
                    dve.wait_ge(oT_psum, n - 1)
                dve.tensor_scalar(onat[n % 2][:, j * DH:(j + 1) * DH], ps[:, 7, j * DH:(j + 1) * DH],
                                  stat[:, 3, u:u + 1], None, ALU.mult).then_inc(o_norm, 1)

            def oa_lo(n):
                dve.wait_ge(oa_hi, n + 1)
                dve.tensor_tensor(Bl[:, 0:2, n * P:(n + 1) * P],
                                  ps[:, 7, 256:512].rearrange("p (a b) -> p a b", a=2),
                                  Bh[:, 0:2, n * P:(n + 1) * P], ALU.subtract).then_inc(oa_ready, 1)

            dve.wait_ge(bias_ready, 4)
            def qkv_b(t):
                i = t - T_QKV_B
                if i == 0:
                    dve.wait_ge(scores_done, 16)
                if i >= 10:
                    dve.wait_ge(vtrans_done, 6 + i - 9)
                scaled(t, qb[:, i, :] if i < 4 else kb[:, i - 4, :] if i < 8 else vtb[:, i % 2, :], ONE)

            for u in range(DIL_STEPS):
                if 0 <= u - 4 < 16:
                    dil_norm(u - 4)
                if u > 16:
                    qkv_b(T_QKV_B + u - 17)
                elif u % 2 == 0 and u >= 2:
                    scaled(T_GATE_A + u // 2 - 1, GA[:, u // 2 - 1, :], ONE)
                if u >= 16:
                    convert(T_QKV_B + u - 16 + 1)
                elif u % 2 == 0:
                    convert(T_GATE_A + u // 2 + 1)
                if u >= 8 and u % 4 == 0:
                    oa_lo(u // 4 - 2)
                if 0 <= u - 1 < 16:
                    dil_softmax(u - 1)

            for t in range(T_QKV_B + DIL_STEPS - 16, T_GATE_B + 1):
                qkv_b(t - 1)
                if t < T_GATE_B:
                    convert(t + 1)

            def sb_z(w):
                n = w // 8
                nk = P * (n + 1)
                dve.wait_ge(sb_scores, w + 1)
                if w >= 2:
                    dve.wait_ge(sb_la, w - 1)
                dve.scalar_tensor_tensor(out=Zs[:, w % 2, 0:nk], in0=ps[:, 2 + w % 2, 0:nk], scalar=0.125,
                                         in1=SBM[:, 512 - nk:512], op0=ALU.mult, op1=ALU.add).then_inc(z_done, 1)

            def sb_log_a(w):
                nk = P * (w // 8 + 1)
                z, e, c = Zs[:, w % 2, 0:nk], Es[:, w % 2, 0:nk], Cs[:, w % 2, 0:nk]
                dve.wait_ge(sb_ln, w + 1)
                dve.scalar_tensor_tensor(out=e, in0=z, scalar=0.0, in1=e, op0=ALU.max, op1=ALU.add)\
                   .then_inc(sb_sp, 1)
                dve.wait_ge(sb_sp, w + 1)
                if w >= 2:
                    dve.wait_ge(sb_pt_psum, w - 1)
                dve.tensor_tensor_scan(c[:, ::-1], ones[:, 0:1].to_broadcast([P, nk]), e[:, ::-1], 0.0,
                                       ALU.mult, ALU.add).then_inc(sb_scan, 1)
                dve.wait_ge(sb_scan, w + 1)
                dve.tensor_tensor(c, z, c, ALU.subtract).then_inc(sb_la, 1)

            def merge_a(m):
                gated(T_UP_A + m, m, GA[:, m, :], GA[:, m, :], ONE)

            def ob_lo(n):
                dve.wait_ge(ob_hi, n + 1)
                dve.tensor_tensor(Bl[:, 2:6, n * P:(n + 1) * P], ps[:, 7, :].rearrange("p (a b) -> p a b", a=4),
                                  Bh[:, 2:6, n * P:(n + 1) * P], ALU.subtract).then_inc(ob_ready, 1)

            for i in range(SB_STEPS):
                if i % 4 == 0 and 4 <= i <= 32:
                    scaled(T_GATE_B + i // 4 - 1, GB[:, i // 4 - 1, :], ONE)
                elif i > 32:
                    merge_a(i - 33)
                if i >= 32:
                    convert(T_UP_A + i - 32 + 1)
                elif i % 4 == 0:
                    convert(T_GATE_B + i // 4 + 1)
                if 0 <= i - 1 < 32:
                    sb_z(i - 1)
                if 0 <= i - 2 < 32:
                    sb_log_a(i - 2)
                if i >= 13 and (i - 13) % 8 == 0:
                    ob_lo((i - 13) // 8)

            for m in range(SB_STEPS - 33, KT):
                merge_a(m)
                convert(T_UP_A + m + 2)
            for m in range(KT):
                t = T_UP_B + m
                n = N_MERGE + m
                f = F[:, n % 2, 0:S1]
                if m >= 2:
                    dve.wait_ge(act_ready, n - 1)
                gated(t, 8 + m, GB[:, m, :], f, ONE)
                dve.wait_ge(evac_done, t + 1)
                dve.tensor_tensor(f, f, GA[:, m, :], ALU.add).then_inc(f_ready, 1)
                convert(t + 2)
                if m >= 1:
                    split(n - 1, Al[:, m - 1, 0:S1], F[:, (n - 1) % 2, 0:S1], Ah[:, m - 1, 0:S1])
            split(N_MERGE + 7, Al[:, 7, 0:S1], F[:, (N_MERGE + 7) % 2, 0:S1], Ah[:, 7, 0:S1])
            for m in range(KT):
                if m >= 1:
                    convert(T_OUT + m + 1)
                add_half(T_OUT + m, m, ONE)
                feed(1, N_MLP + m, m, G_MLP, ONE, Bh, Bl)
            convert(T_MLP + 1)
            stats(1)
            mlp(ONE)

            def first_stats():
                dve.wait_ge(stat_done, 3)
                dve.tensor_scalar(RS1, ps[:, 7, :], 1.0 / DM, EPS, ALU.mult, ALU.add).then_inc(ms1_step, 1)
                dve.wait_ge(ms1_step, 1)
                dve.tensor_scalar(RS[:, META:S2], RS1, EPS, None, ALU.mult).then_inc(ms1_step, 1)
                dve.wait_ge(ms1_step, 2)
                dve.scalar_tensor_tensor(out=RS[:, META:S2], in0=ps[:, 6, :], scalar=1.0 / DM, in1=RS[:, META:S2],
                                         op0=ALU.mult, op1=ALU.add)
                dve.tensor_scalar(RS[:, 0:META], ps[:, 5, 0:META], 1.0 / DM, EPS, ALU.mult, ALU.add)\
                   .then_inc(ms_ready, 1)
                dve.wait_ge(sqrt_ready, 3)
                dve.reciprocal(RS[:, :], RS[:, :]).then_inc(rstd_ready, 1)
                dve.wait_ge(rstd_ready, 3)

            def residual(m):
                if m == 0:
                    dve.wait_ge(sqrt1_ready, 1)
                    dve.reciprocal(RS1, RS1).then_inc(ms1_step, 1)
                    dve.wait_ge(ms1_step, 3)
                x = X[:, m, META:S2]
                dve.scalar_tensor_tensor(out=x, in0=x, scalar=vecT[:, G_FIN + m:G_FIN + m + 1], in1=RS1,
                                         op0=ALU.mult, op1=ALU.mult).then_inc(x_normed, 1)

            def mixed_lo(g):
                n = N2_PM + g
                split(n, Al[:, 4 + g, 0:S1], F[:, n % 2, 0:S1], Ah[:, 4 + g, 0:S1])

            def silu(i):
                dve.wait_ge(silu_tanh, i + 1)
                dve.scalar_tensor_tensor(out=sr[:, i, :], in0=G2[:, i % 2, :], scalar=1.0, in1=sr[:, i, :],
                                         op0=ALU.add, op1=ALU.mult).then_inc(silu_done, 1)

            def evac(t):
                if t < T2_LR:
                    scaled(t, k2[:, t - T2_K, PAD:PADL], ALL)
                elif t == T2_LR:
                    scaled(t, lr[0:16, :], ALL, 16)
                elif t < T2_A:
                    dve.wait_ge(slab_done, t + 1)
                    dve.scalar_tensor_tensor(out=q2[:, t - T2_Q, :], in0=dense_psum(t, REAL), scalar=0.125,
                                             in1=RS[:, META:S2], op0=ALU.mult, op1=ALU.mult).then_inc(evac_done, 1)
                elif t < T2_V:
                    scaled(t, apad[:, (t - T2_A) % 2, :], ALL)
                elif t < T2_R:
                    scaled(t, v2[:, t - T2_V, PAD:PADL], ALL)
                elif t < T2_PM:
                    i = t - T2_R
                    scaled(t, sr[:, i, :], REAL)
                    if i >= 1:
                        silu(i - 1)
                elif t == T2_PM:
                    dve.wait_ge(slab_done, t + 1)
                    for g in range(4):
                        n = N2_PM + g
                        dve.wait_ge(act_ready, n - 1)
                        dve.tensor_scalar(F[:, n % 2, 0:S1], pool_bank(g), vecT[:, POOL_SC + g:POOL_SC + g + 1], None,
                                          ALU.mult).then_inc(f_ready, 1)
                        if g >= 1:
                            mixed_lo(g - 1)
                    dve.wait_ge(f_ready, staged(N2_PM + 3))
                    dve.sem_inc(evac_done, 1)
                    mixed_lo(3)
                    silu(3)
                elif t < T2_GB:
                    i = t - T2_GY
                    if i == 0:
                        dve.wait_ge(silu_done, 4)
                    if i % 4 < 2:
                        scaled(t, G2[:, i % 2, :], REAL)
                    else:
                        m = i // 4 * 2 + i % 2
                        if m == 0:
                            dve.wait_ge(vr_psum, 12)
                        gated(t, 16 + m, G2[:, i % 2, :], ma[:, m, :], REAL)
                elif t < T2_GO:
                    scaled(t, GB2[:, t - T2_GB, :], REAL)
                elif t < T2_OUT:
                    m = t - T2_GO
                    n = N2_M + m
                    f, g = F[:, n % 2, 0:S1], G2[:, m % 2, :]
                    gated(t, 24 + m, GB2[:, m, :], g, REAL)
                    dve.wait_ge(evac_done, t + 1)
                    if m >= 2:
                        dve.wait_ge(act_ready, n - 1)
                    dve.tensor_tensor(f, ma[:, m, :], g, ALU.add).then_inc(f_ready, 1)

            def job(what):
                kind = what[0]
                if kind == "gate_up":
                    for j in range(2):
                        dve.wait_ge(gu_psum, j + 1)
                        dve.tensor_scalar(tokens(UU[:, j, :], 2), ps[:, 4 + 2 * j:6 + 2 * j, 0:HALF2],
                                          vecT[:, B_GATE2 + j:B_GATE2 + j + 1], None, ALU.add).then_inc(u_ready, 1)
                elif kind == "decay":
                    for j in range(2):
                        dve.wait_ge(u_ln, j + 1)
                        dve.scalar_tensor_tensor(out=la[:, j, PAD:PADL], in0=UU[:, j, :], scalar=0.0, in1=E2,
                                                 op0=ALU.min, op1=ALU.subtract).then_inc(la_ready, 1)
                        dve.wait_ge(la_ready, j + 1)
                        dve.tensor_tensor_scan(bS[:, j, :], reset, la[:, j, :], 0.0, ALU.mult, ALU.add)\
                           .then_inc(bs_ready, 1)
                    dve.wait_ge(bs_ready, 2)
                elif kind == "unit_d":
                    y = what[1]
                    if y // 2 == U_DIAG // 2 or y >= U_START:
                        return
                    x = exp_no(y)
                    v, ref, b = level_ref(y)
                    if x >= 2:
                        dve.wait_ge(qk_ready, (y - 2 if y < U_DIAG else y - 4) + 1)
                    dve.tensor_tensor(Ed[:, x % 2, :].rearrange("p (a b) -> p a b", b=b), v, ref, ALU.subtract)\
                       .then_inc(d_ready, 1)
                elif kind == "unit_qk":
                    y = what[1]
                    l, j = y // 2, y % 2
                    if l == U_DIAG // 2:
                        dve.sem_inc(qk_ready, 1)
                        return
                    x = exp_no(y)
                    e = Ed[:, x % 2, :]
                    dve.wait_ge(d_exp, x + 1)
                    if y < U_DIAG:
                        if y >= 2:
                            dve.wait_ge(mm_done, y - 1)
                        dve.tensor_tensor(Qp[:, j, :], q2[:, j, :], e, ALU.mult)
                        dve.tensor_tensor(Kp[:, j, :], k2[:, j, CH:], e, ALU.mult).then_inc(qk_ready, 1)
                    elif y < U_START:
                        dve.wait_ge(mm_done, U_DIAG - 2 + j + 1)
                        dve.tensor_tensor(Kp[:, j, :], k2[:, j, 0:8 * CH], e, ALU.mult).then_inc(qk_ready, 1)
                    else:
                        dve.tensor_tensor(Qs[:, j, :], q2[:, j, :], e, ALU.mult).then_inc(qk_ready, 1)
                    dve.wait_ge(qk_ready, y + 1)
                elif kind == "unit_mm":
                    y = what[1]
                    l, j = y // 2, y % 2
                    if y >= U_END:
                        return
                    dve.wait_ge(mm_done, y + 1)
                    src = ps[:, 4 + 2 * j, :]
                    if l == 0:
                        dve.tensor_copy(sc[:, j, :], src).then_inc(sc_done, 1)
                    else:
                        dve.wait_ge(sc_done, y - 1)
                        dve.copy_predicated(
                            sc[:, j, :].rearrange("p (a b) -> p a b", b=CH),
                            masks[:, l - 1, :].bitcast(U32).unsqueeze(1).to_broadcast([P, NCH - 1, CH]),
                            src.rearrange("p (a b) -> p a b", b=CH)).then_inc(sc_done, 1)
                elif kind == "kv":
                    j = what[1]
                    dve.wait_ge(kv_psum, j + 1)
                    dve.wait_ge(ebe_ready, 2)
                    if j == 0:
                        dve.wait_ge(kn_psum, 2)
                    for c in range(8):
                        kv = flat(4 + 2 * j)[:, c * P:(c + 1) * P]
                        dst = st[:, j, c * P:(c + 1) * P]
                        if c == 0:
                            ins = dve.tensor_copy(dst, kv)
                        else:
                            ins = dve.scalar_tensor_tensor(out=dst, in0=st[:, j, (c - 1) * P:c * P],
                                                           scalar=ebe[:, j, c:c + 1], in1=kv,
                                                           op0=ALU.mult, op1=ALU.add)
                        ins.then_inc(st_done, 1)
                        dve.wait_ge(st_done, 8 * j + c + 1)
                elif kind == "o_mm":
                    h = what[1]
                    dve.wait_ge(o_psum, h + 1)
                    if h >= 2:
                        dve.wait_ge(f_ready, staged(N2_O + h - 2))
                    dve.tensor_copy(osb[:, h % 2, :], ps[:, 4 + h % 2, :]).then_inc(o_copied, 1)
                elif kind == "o_stat":
                    h = what[1]
                    dve.wait_ge(o_stat, h + 1)
                    dve.tensor_scalar(SQ[:, h % 2, 0:S1], ps[:, 6 + h % 2, :], 4.0 / P, 4.0 * EPS, ALU.mult, ALU.add)\
                       .then_inc(o_ms, 1)
                elif kind == "o_norm":
                    h = what[1]
                    o, r = osb[:, h % 2, :], SQ[:, h % 2, 0:S1]
                    dve.wait_ge(o_sqrt, h + 1)
                    dve.reciprocal(r, r).then_inc(o_rstd, 1)
                    dve.wait_ge(o_rstd, h + 1)
                    dve.tensor_tensor(o, o, r, ALU.mult).then_inc(o_scaled, 1)
                    dve.wait_ge(o_scaled, h + 1)
                    n = N2_O + h
                    f = F[:, n % 2, 0:S1]
                    dve.scalar_tensor_tensor(out=f, in0=o, scalar=vecT[:, GLA_G + h:GLA_G + h + 1],
                                             in1=sr[:, h, :], op0=ALU.mult, op1=ALU.mult).then_inc(f_ready, 1)
                    split(n, Al[:, h, 0:S1], f, Ah[:, h, 0:S1])
                elif kind == "pool_split":
                    g = what[1]
                    w = WINDOWS[g]
                    n = N2_POOL + g
                    f = F[:, n % 2, 0:S1]
                    dve.wait_ge(win_done, (g + 1) * (g + 2) // 2)
                    dve.scalar_tensor_tensor(out=f, in0=wsum[:, g % 2, META:S2], scalar=1.0 / w,
                                             in1=apad[:, g % 2, META:], op0=ALU.mult, op1=ALU.subtract)\
                       .then_inc(f_ready, 1)
                    split(n, Al[:, g, 0:S1], f, Ah[:, g, 0:S1])

            def merged_lo(m):
                n = N2_M + m
                split(n, Bl[:, m, 0:S1], F[:, n % 2, 0:S1], Bh[:, m, 0:S1])

            dve.wait_ge(zeros2_ready, 1)
            for t in range(T2, T2_OUT + 1):
                if t == T2 + 1:
                    first_stats()
                if t > T2:
                    evac(t - 1)
                    if t == T2_OUT:
                        merged_lo(6)
                        merged_lo(7)
                    convert(t + 1)
                if T2 < t < T2_A:
                    residual(2 * (t - T2 - 1))
                    residual(2 * (t - T2 - 1) + 1)
                if t == T2_A:
                    dve.wait_ge(x_normed, KT)
                if T2_GO + 2 <= t < T2_OUT:
                    merged_lo(t - T2_GO - 2)
                if t < T2_OUT:
                    for what in between[t]:
                        job(what)
            for m in range(KT):
                if m >= 1:
                    convert(T2_OUT + m + 1)
                add_half(T2_OUT + m, m, REAL)
                feed(3, N2_FFN + m, m, G_FFN2, REAL, Ah, Al)
            convert(T2_MLP + 1)
            stats(3)
            mlp(REAL)
            dve.wait_ge(stat_done, 5)
            dve.tensor_scalar(r_tok, ps[:, 7, 0:4], 1.0 / DM, EPS, ALU.mult, ALU.add).then_inc(ms_ready, 1)
            dve.wait_ge(sqrt_ready, 5)
            dve.reciprocal(r_tok, r_tok).then_inc(rstd_ready, 1)
            dve.wait_ge(rstd_ready, 5)
            dve.wait_ge(y_copied, 4)
            for a in range(4):
                dve.tensor_scalar(ON[:, a, 0:512], ON[:, a, 0:512], r_tok[:, a:a + 1], None, ALU.mult)\
                   .then_inc(y_low, 1)

        @block.tensor
        def _(pe):
            def products(t_ps, slot, kt, Oh, Ol, o0, kind, k_from, k_to, ready=None, col0=0):
                h, l = w_slab(wh, slot, kt), w_slab(wl, slot, kt)
                last = None
                for k in range(k_from, k_to):
                    if ready is not None:
                        ready(k)
                    for i, (a, b) in enumerate(((h, Oh), (h, Ol), (l, Oh))):
                        start, stop = k == 0 and i == 0, k == kt - 1 and i == 2
                        if kind == ALL:
                            for half in range(2):
                                last = pe.matmul(dense_psum(t_ps, ALL)[:, half, :], a[:, k, :],
                                                 b[:, o0 + k, half * HALF2:(half + 1) * HALF2],
                                                 start=start, stop=stop)
                        else:
                            last = pe.matmul(dense_psum(t_ps, kind), a[:, k, :], b[:, o0 + k, col0:col0 + S1],
                                             start=start, stop=stop)
                return last

            def slab_start(t):
                pe.wait_ge(lo_ready, t + 1)
                if t >= 2:
                    pe.wait_ge(evac_done, t - 1)

            def full_slab(t, Oh, Ol, o0, kind, ready=None, col0=0):
                kt = slab[t][2]
                slab_start(t)
                products(t, t % 2, kt, Oh, Ol, o0, kind, 0, kt, ready, col0).then_inc(slab_done, 1)

            def split_ready(n0):
                return lambda k: pe.wait_ge(act_ready, n0 + k + 1)

            def stats(norm):
                pe.wait_ge(ss_done, 8 * norm + 8)
                pe.matmul(ps[:, 7, :], ones[:, :], SS[:, 0:S1], start=True, stop=True).then_inc(stat_done, 1)

            def slab_with_stats(t, ops, kind, ready, sums):
                slab_start(t)
                products(t, t % 2, KT, *ops, 0, kind, 0, KT // 2, ready)
                sums()
                products(t, t % 2, KT, *ops, 0, kind, KT // 2, KT, ready).then_inc(slab_done, 1)

            def mlp_chunk(which, c, last):
                t0, n0, _ = MLPS[which]
                for j in range(1, 16 if last else 17):
                    t = t0 + j
                    pe.wait_ge(lo_ready, t + 16 * c + 1)
                    pe.wait_ge(evac_done, t + 16 * c - 1)
                    ready = None
                    if j == 8:
                        def ready(k):
                            pe.wait_ge(act_ready, n0 + 8 * c + (k + 1))
                    ops = HIDDEN[which] if 8 <= j < 16 else NORMED[which]
                    products(t, t % 2, KT, *ops, 0, which, 0, KT, ready).then_inc(slab_done, 1)
                    if last and which == REAL and j >= 9:
                        turn_y(j - 9)

            def turn_y(m):
                pe.wait_ge(y_ready, m + 1)
                if m == 4:
                    pe.wait_ge(y_copied, 4)
                for a in range(4):
                    mm = pe.transpose(ps[:, Y_BANKS[a], (m % 4) * P:(m % 4 + 1) * P], Y[:, m, a * P:(a + 1) * P],
                                      ident[:, :])
                mm.then_inc(y_psum, 1)

            def mlp(which):
                norm, feed_n = (1, N_MLP) if which == ONE else (3, N2_FFN)
                slab_with_stats(MLPS[which][0], NORMED[which], which, split_ready(feed_n),
                                lambda: stats(norm))
                with pe.Fori(0, CHUNKS - 1) as c:
                    mlp_chunk(which, c, False)
                mlp_chunk(which, CHUNKS - 1, True)

            def turn_x(m):
                pe.wait_ge(x_in[m // 2], 16)
                if m >= 4:
                    pe.wait_ge(xt_copied, m - 3)
                for a in range(4):
                    mm = pe.transpose(ps[:, (2, 3, 6, 7)[m % 4], a * P:(a + 1) * P],
                                      xnat[:, a, m * P:(m + 1) * P], ident[:, :])
                mm.then_inc(xt_psum, 1)

            def turn_vectors():
                pe.wait_ge(params_in, 16 * 11)
                pe.wait_ge(gain_ready, 1)
                pe.transpose(ps[:, 5, 0:G_MIX], vrow[0:G_MIX, :], ident[0:G_MIX, 0:G_MIX]).then_inc(vec_psum, 1)
                for m in range(KT):
                    mm = pe.transpose(ps[:, 4, m * META:(m + 1) * META], mnat[0:META, m * P:(m + 1) * P],
                                      ident[0:META, 0:META])
                mm.then_inc(meta_psum, 1)

            pe.wait_ge(consts_ready, 2)
            pe.wait_ge(gain_in, 16)
            pe.transpose(ps[:, 5, 0:KT], grow[0:KT, :], ident[0:KT, 0:KT]).then_inc(gain_psum, 1)
            for m in range(KT):
                turn_x(m)
            for k in range(KT + 2):
                for t, kk in ((0, k), (1, k - 2)):
                    if kk == 0:
                        slab_start(t)
                    if 0 <= kk < KT:
                        mm = products(t, t, KT, Ah, Al, 0, ONE, kk, kk + 1, split_ready(N_MIX))
                        if kk == KT - 1:
                            mm.then_inc(slab_done, 1)

            def v_turn(i, src):
                if i >= 2:
                    pe.wait_ge(vnat_copied, i - 1)
                for a in range(4):
                    mm = pe.transpose(ps[:, 6 + i % 2, a * P:(a + 1) * P], src[:, a * P:(a + 1) * P], ident[:, :])
                mm.then_inc(vtrans_done, 1)

            stats(0)
            for t in range(2, T_GATE_A):
                full_slab(t, Ah, Al, 0, ONE)
                if t == 3:
                    turn_vectors()
                if t >= 13:
                    pe.wait_ge(evac_done, t)
                    if t == 13:
                        pe.wait_ge(ms_ready, 1)
                    v_turn(t - 13, vt[:, (t - 1) % 2, :])

            def dil_scores(u):
                n, j = u // 4, u % 4
                if u >= 1:
                    pe.wait_ge(logits_done, 3 * u)
                for g, (k0, nb, _) in enumerate(dil_groups(n)):
                    head = 4 * g + j
                    b = DH * (head % 2)
                    mm = pe.matmul(ps[:, 2 + g, 0:nb * P], qa[b:b + DH, head // 2, n * P:(n + 1) * P],
                                   ka[b:b + DH, head // 2, k0:k0 + nb * P], start=True, stop=True)
                mm.then_inc(scores_done, 1)

            def dil_turn(u, which):
                pe.wait_ge(probs_ready, u + 1)
                for g in which:
                    _, nb, col = dil_groups(u // 4)[g]
                    if 3 * u + g >= 2:
                        pe.wait_ge(pt_copied, 3 * u + g - 1)
                    for i in range(nb):
                        mm = pe.transpose(ps[:, 5 + (3 * u + g) % 2, i * P:(i + 1) * P],
                                          Lg[:, u % 2, col + i * P:col + (i + 1) * P], ident[:, :])
                    mm.then_inc(pt_psum, 1)

            def dil_pv(u):
                n, j = u // 4, u % 4
                pe.wait_ge(pt_copied, 3 * u + 3)
                if u == 0:
                    pe.wait_ge(vnat_copied, 6)
                if u >= 1:
                    pe.wait_ge(o_norm, u)
                if u >= 5 and u % 4 == 1:
                    pe.wait_ge(oa_ready, u // 4)
                groups = dil_groups(n)
                total = sum(g[1] for g in groups)
                done = 0
                for g, (k0, nb, col) in enumerate(groups):
                    head = 4 * g + j
                    for i in range(nb):
                        mm = pe.matmul(ps[:, 7, j * DH:(j + 1) * DH], pt_blocks(u, g)[:, i, :],
                                       Vna[:, k0 // P + i, head * DH:(head + 1) * DH],
                                       start=(done == 0), stop=(done == total - 1))
                        done += 1
                mm.then_inc(pv_done, 1)

            def oa_turn(n):
                pe.wait_ge(o_norm, min(4 * n + 5, 16))
                for i in range(2):
                    mm = pe.transpose(ps[:, 7, 256 + i * P:256 + (i + 1) * P], onat[n % 2][:, i * P:(i + 1) * P],
                                      ident[:, :])
                mm.then_inc(oT_psum, 1)

            pe.wait_ge(late_scaled, 2)
            for u in range(DIL_STEPS):
                if u < 16:
                    t = T_GATE_A + u // 2
                    if u % 2 == 0:
                        slab_start(t)
                    mm = products(t, t % 2, KT, Ah, Al, 0, ONE, 4 * (u % 2), 4 * (u % 2) + 4)
                    if u % 2:
                        mm.then_inc(slab_done, 1)
                    if u == 0:
                        pe.wait_ge(evac_done, T_GATE_A)
                        v_turn(5, vt[:, 1, :])
                else:
                    full_slab(T_QKV_B + u - 16, Ah, Al, 0, ONE)
                if u >= 8 and u % 4 == 0:
                    oa_turn(u // 4 - 2)
                if 0 <= u - 2 < 16:
                    dil_turn(u - 2, (0, 1))
                if 0 <= u - 3 < 16:
                    dil_pv(u - 3)
                if 0 <= u - 2 < 16:
                    dil_turn(u - 2, (2,))
                if u < 16:
                    dil_scores(u)

            for t in range(T_QKV_B + DIL_STEPS - 16, T_GATE_B):
                full_slab(t, Ah, Al, 0, ONE)
                i = t - T_QKV_B - 9
                if i >= 0:
                    pe.wait_ge(evac_done, t)
                    v_turn(6 + i, vtb[:, i % 2, :])

            def sb_scores_mm(w):
                n, h = w // 8, w % 8
                b = DH * (h % 2)
                if w >= 2:
                    pe.wait_ge(z_done, w - 1)
                pe.matmul(ps[:, 2 + w % 2, 0:(n + 1) * P], qb[b:b + DH, h // 2, n * P:(n + 1) * P],
                          kb[b:b + DH, h // 2, 0:(n + 1) * P], start=True, stop=True).then_inc(sb_scores, 1)

            def sb_turn(w):
                pe.wait_ge(sb_probs, w + 1)
                if w >= 2:
                    pe.wait_ge(sb_pt_copied, w - 1)
                for i in range(w // 8 + 1):
                    mm = pe.transpose(ps[:, 4 + w % 2, i * P:(i + 1) * P], Cs[:, w % 2, i * P:(i + 1) * P], ident[:, :])
                mm.then_inc(sb_pt_psum, 1)

            def sb_pv_mm(w):
                n, h = w // 8, w % 8
                pe.wait_ge(sb_pt_copied, w + 1)
                if w == 0:
                    pe.wait_ge(vnat_copied, 10)
                if h == 0 and n >= 1:
                    pe.wait_ge(ob_nat, n)
                for i in range(n + 1):
                    mm = pe.matmul(ps[:, 6, h * DH:(h + 1) * DH], PTb[:, w % 2, i * P:(i + 1) * P],
                                   Vnb[:, i, h * DH:(h + 1) * DH], start=(i == 0), stop=(i == n))
                mm.then_inc(sb_pv, 1)

            def ob_turn(n):
                pe.wait_ge(ob_nat, n + 1)
                if n >= 1:
                    pe.wait_ge(ob_ready, n)
                for i in range(4):
                    mm = pe.transpose(ps[:, 7, i * P:(i + 1) * P], onatb[:, i * P:(i + 1) * P], ident[:, :])
                mm.then_inc(obT_psum, 1)

            for i in range(SB_STEPS):
                if i < 32:
                    t = T_GATE_B + i // 4
                    if i % 4 == 0:
                        slab_start(t)
                    mm = products(t, t % 2, KT, Ah, Al, 0, ONE, 2 * (i % 4), 2 * (i % 4) + 2)
                    if i % 4 == 3:
                        mm.then_inc(slab_done, 1)
                    if i == 0:
                        pe.wait_ge(evac_done, T_GATE_B)
                        v_turn(9, vtb[:, 1, :])
                else:
                    if i == 32:
                        pe.wait_ge(oa_ready, 4)
                    full_slab(T_UP_A + i - 32, Bh, Bl, 0, ONE)
                if 0 <= i - 4 < 32:
                    sb_pv_mm(i - 4)
                if 0 <= i - 3 < 32:
                    sb_turn(i - 3)
                if i < 32:
                    sb_scores_mm(i)
                if i >= 12 and (i - 12) % 8 == 0:
                    ob_turn((i - 12) // 8)

            for t in range(T_UP_A + SB_STEPS - 32, T_UP_B):
                full_slab(t, Bh, Bl, 0, ONE)
            pe.wait_ge(ob_ready, 4)
            for t in range(T_UP_B, T_OUT):
                full_slab(t, Bh, Bl, 2, ONE)
            for t in range(T_OUT, T_MLP):
                full_slab(t, Ah, Al, 0, ONE, split_ready(N_MERGE) if t == T_OUT else None)
            mlp(ONE)

            def first_stats():
                pe.wait_ge(ss_done, 24)
                pe.matmul(ps[:, 7, :], ones[:, :], SS[:, 0:S1], start=True, stop=True)
                pe.wait_ge(ss2_done, 8)
                pe.matmul(ps[:, 6, :], ones[:, :], SS2[:, META:S2], start=True, stop=True)
                pe.matmul(ps[:, 5, 0:META], ones[:, :], SS2[:, 0:META], start=True, stop=True).then_inc(stat_done, 1)

            pe.wait_ge(meta_split, 1)
            slab_with_stats(T2, (Bh, Bl), ALL, split_ready(N2_MIX), first_stats)

            def job(what):
                kind = what[0]
                if kind == "gate_up":
                    pe.wait_ge(evac_done, T2_LR + 1)
                    pe.wait_ge(ms_ready, 3)
                    for j in range(2):
                        for half in range(2):
                            mm = pe.matmul(ps[:, 4 + 2 * j + half, 0:HALF2], wgu[:, j * P:(j + 1) * P],
                                           lr[0:16, half * HALF2:(half + 1) * HALF2], start=True, stop=True)
                        mm.then_inc(gu_psum, 1)
                elif kind == "v_rows":
                    h = what[1]
                    beta = 64 * (h % 2)
                    pe.wait_ge(evac_done, T2_V + h + 1)
                    for g, (c0, nc_) in enumerate(((0, 4), (4, 4), (8, 1))):
                        x = 3 * h + g
                        if x >= 2:
                            pe.wait_ge(vr_copied, x - 1)
                        else:
                            pe.wait_ge(u_ready, 2)
                        for i in range(nc_):
                            c = c0 + i
                            dst = ps[beta:beta + 64, 5 + 2 * (x % 2), i * P:(i + 1) * P]
                            v = v2[:, h, c * CH:(c + 1) * CH]
                            if beta == 0:
                                mm = pe.transpose(dst, v, ident[:, :])
                            else:
                                mm = pe.matmul(dst, v, ident[:, :], start=True, stop=True)
                        mm.then_inc(vr_psum, 1)
                elif kind == "unit_mm":
                    y = what[1]
                    l, j = y // 2, y % 2
                    if y >= U_START:
                        return
                    pe.wait_ge(qk_ready, y + 1)
                    if y >= 2:
                        pe.wait_ge(sc_done, min(y - 1, U_END))
                    if y < U_END:
                        Q, K = (Qp, Kp) if l < U_DIAG // 2 else (q2, k2)
                        k0 = 0 if l < U_DIAG // 2 else CH
                        for c in range(8):
                            for hh in range(2):
                                b = 64 * hh
                                mm = pe.matmul(ps[b:b + 64, 4 + 2 * j, c * CH:(c + 1) * CH],
                                               K[b:b + 64, j, k0 + c * CH:k0 + (c + 1) * CH],
                                               Q[b:b + 64, j, c * CH:(c + 1) * CH], start=True, stop=True)
                        mm.then_inc(mm_done, 1)
                    else:
                        pe.wait_ge(sc_done, U_END)
                        for c in range(8):
                            for hh in range(2):
                                b = 64 * hh
                                mm = pe.matmul(ps[b:b + 64, 4 + 2 * j, c * CH:(c + 1) * CH],
                                               Kp[b:b + 64, j, c * CH:(c + 1) * CH], ident[b:b + 64, b:b + 64],
                                               start=True, stop=True)
                        mm.then_inc(kn_psum, 1)
                elif kind == "kv":
                    j = what[1]
                    pe.wait_ge(kn_copied, 2)
                    pe.wait_ge(vr_copied, 12)
                    for c in range(8):
                        for hh in range(2):
                            b = 64 * hh
                            mm = pe.matmul(ps[b:b + 64, 4 + 2 * j + c // 4, (c % 4) * P:(c % 4 + 1) * P],
                                           Kn[b:b + 64, j, c * CH:(c + 1) * CH],
                                           Vn[b:b + 64, j, c * P:(c + 1) * P], start=True, stop=True)
                    mm.then_inc(kv_psum, 1)
                elif kind == "o_mm":
                    h = what[1]
                    j, b = h // 2, 64 * (h % 2)
                    if h == 0:
                        pe.wait_ge(st_done, 16)
                        pe.wait_ge(qk_ready, U_START + 2)
                    if h >= 2:
                        pe.wait_ge(o_copied, h - 1)
                    for c in range(1, NCH):
                        at = slice((c - 1) * CH, c * CH)
                        pe.matmul(ps[:, 4 + h % 2, at], Vn[b:b + 64, j, c * P:(c + 1) * P], sc[b:b + 64, j, at],
                                  start=True, stop=False)
                        mm = pe.matmul(ps[:, 4 + h % 2, at], st[b:b + 64, j, (c - 1) * P:c * P],
                                       Qs[b:b + 64, j, at], start=False, stop=True)
                    mm.then_inc(o_psum, 1)
                elif kind == "o_stat":
                    h = what[1]
                    pe.wait_ge(o_sq, h + 1)
                    if h >= 2:
                        pe.wait_ge(o_ms, h - 1)
                    pe.matmul(ps[:, 6 + h % 2, :], ones[:, :], osb2, start=True, stop=True).then_inc(o_stat, 1)

            for t in range(T2, T2_OUT):
                if t == T2_PM:
                    slab_start(t)
                    pe.wait_ge(vr_copied, 12)
                    h, l = w_slab(wh, t % 2, 4), w_slab(wl, t % 2, 4)
                    for g in range(4):
                        pe.wait_ge(act_ready, N2_POOL + g + 1)
                        for i, (a, b) in enumerate(((h, Ah), (h, Al), (l, Ah))):
                            mm = pe.matmul(pool_bank(g), a[:, g, :], b[:, g, 0:S1], start=(i == 0), stop=(i == 2))
                    mm.then_inc(slab_done, 1)
                elif T2_GY <= t < T2_GB and (t - T2_GY) % 4 >= 2:
                    full_slab(t, Ah, Al, 4, REAL, split_ready(N2_PM))
                elif T2_GO <= t:
                    full_slab(t, Ah, Al, 0, REAL, split_ready(N2_O))
                elif t < T2_Q or T2_A <= t < T2_R:
                    if t > T2:
                        full_slab(t, Bh, Bl, 0, ALL)
                else:
                    full_slab(t, Bh, Bl, 0, REAL, None, META)
                for what in between[t]:
                    job(what)
            for t in range(T2_OUT, T2_MLP):
                full_slab(t, Bh, Bl, 0, REAL, split_ready(N2_M) if t == T2_OUT else None)
            mlp(REAL)
            pe.wait_ge(ss_done, 8 * 4 + 8)
            for a in range(4):
                mm = pe.matmul(ps[:, 7, a:a + 1], SS[:, a * P:(a + 1) * P], ones[:, 0:1], start=True, stop=True)
            mm.then_inc(stat_done, 1)
            turn_y(KT - 1)


_INS = ["x", "norm_mix_g", "w_in", "b_gate", "w_up_dil", "w_up_sb", "w_out", "norm_mlp_g", "w_mlp_in",
        "w_mlp_out", "norm_final_g", "meta_tokens_2", "norm_mix_2", "w_in_2", "w_pool_mix_2", "pool_scale_2",
        "w_pool_out_2", "w_gate_up_2", "b_gate_2", "gla_norm_2", "w_gla_out_2", "w_out_2", "norm_ffn_2",
        "w_ff1_2", "w_ff2_2", "norm_final_2"]


def kernel(**inputs):
    import numpy as _np
    import concourse.bacc as _bacc
    from concourse.bass_utils import run_bass_kernel_spmd as _run

    nc = _bacc.Bacc("TRN2", target_bir_lowering=False, num_devices=1)
    arrays, aps = {}, {}
    for name in _INS:
        a = _np.ascontiguousarray(inputs[name])
        arrays[f"in_{name}"] = a
        aps[name] = nc.dram_tensor(f"in_{name}", a.shape, mybir.dt.from_np(a.dtype), kind="ExternalInput").ap()
    aps["out"] = nc.dram_tensor("out_0", (1, S1, DM), F32, kind="ExternalOutput").ap()
    build(nc, aps)
    r = _run(nc, [arrays], core_ids=[0])
    return r.results[0]["out_0"]
```
